# Optimizing a Trainium2 kernel written in Bass

```python
import jax, jax.numpy as jnp
from jax import lax
import numpy as np
import math

D_MODEL = 1024
BATCH = 1
SEQ = 256
DEPTH = 2

PLE_DIM = 256
N_MIXERS = 2
D_FF = 2816
FFN_HALF = 0.5
MLA_HEADS = 16
MLA_Q_RANK = 512
MLA_KV_RANK = 256
MLA_NOPE = 64
MLA_ROPE = 32
MLA_V = 64
ROPE_THETA = 10000.0
FOX_HEADS = 16
FOX_HEAD_DIM = 64
Q_BLOCK = 128
EPS = 1e-6
N_MLA_LAYERS = (DEPTH + N_MIXERS - 1) // N_MIXERS
N_FOX_LAYERS = DEPTH // N_MIXERS


def rms_norm(x, g):
    xf = x.astype(jnp.float32)
    y = xf * lax.rsqrt(jnp.mean(xf * xf, axis=-1, keepdims=True) + EPS)
    return (y * g.astype(jnp.float32)).astype(x.dtype)

def swiglu(x, w_in, w_out):
    gate, up = jnp.split(x @ w_in, 2, axis=-1)
    return (jax.nn.silu(gate) * up) @ w_out

def rope(x, pos):
    r = x.shape[-1]
    inv_freq = ROPE_THETA ** (-jnp.arange(0, r, 2, dtype=jnp.float32) / r)
    ang = pos.astype(jnp.float32)[:, :, None, None] * inv_freq
    cos = jnp.cos(ang).astype(x.dtype)
    sin = jnp.sin(ang).astype(x.dtype)
    x1, x2 = jnp.split(x, 2, axis=-1)
    return jnp.concatenate([x1 * cos - x2 * sin, x1 * sin + x2 * cos], axis=-1)

def block_causal_attention(q, k, v, decay=None):
    b, s, h, dk = q.shape
    dv = v.shape[-1]
    nb = s // Q_BLOCK
    scale = dk ** -0.5
    qb = q.reshape(b, nb, Q_BLOCK, h, dk).transpose(1, 0, 2, 3, 4)
    blk = jnp.arange(nb)
    k_pos = jnp.arange(s)
    c_k = None if decay is None else decay.transpose(0, 2, 1)

    def attend(qi, i, c_qi):
        logits = jnp.einsum('bqhd,bkhd->bhqk', qi, k).astype(jnp.float32) * scale
        if c_qi is not None:
            logits = logits + c_qi[:, :, :, None] - c_k[:, :, None, :]
        q_pos = i * Q_BLOCK + jnp.arange(Q_BLOCK)
        mask = k_pos[None, :] <= q_pos[:, None]
        logits = jnp.where(mask[None, None], logits, -jnp.inf)
        probs = jax.nn.softmax(logits, axis=-1)
        return jnp.einsum('bhqk,bkhd->bqhd', probs.astype(v.dtype), v)

    if decay is None:
        out = lax.map(lambda a: attend(a[0], a[1], None), (qb, blk))
    else:
        c_qb = decay.reshape(b, nb, Q_BLOCK, h).transpose(1, 0, 3, 2)
        out = lax.map(lambda a: attend(a[0], a[1], a[2]), (qb, blk, c_qb))
    return out.transpose(1, 0, 2, 3, 4).reshape(b, s, h, dv)

def mla_mixer(hn, pos, w_in, g_q_lat, w_uq, g_kv_lat, w_ukv, g_qn, g_kn, w_o):
    b, s, _ = hn.shape
    z = hn @ w_in
    c_q = z[..., :MLA_Q_RANK]
    c_kv = z[..., MLA_Q_RANK:MLA_Q_RANK + MLA_KV_RANK]
    k_pe = z[..., MLA_Q_RANK + MLA_KV_RANK:]
    q = (rms_norm(c_q, g_q_lat) @ w_uq).reshape(b, s, MLA_HEADS, MLA_NOPE + MLA_ROPE)
    kv = (rms_norm(c_kv, g_kv_lat) @ w_ukv).reshape(b, s, MLA_HEADS, MLA_NOPE + MLA_V)
    k_nope, v = kv[..., :MLA_NOPE], kv[..., MLA_NOPE:]
    k_pe_h = jnp.broadcast_to(k_pe[:, :, None, :], (b, s, MLA_HEADS, MLA_ROPE))
    k = jnp.concatenate([k_nope, k_pe_h], axis=-1)
    q = rms_norm(q, g_qn)
    k = rms_norm(k, g_kn)
    q = jnp.concatenate([q[..., :MLA_NOPE], rope(q[..., MLA_NOPE:], pos)], axis=-1)
    k = jnp.concatenate([k[..., :MLA_NOPE], rope(k[..., MLA_NOPE:], pos)], axis=-1)
    o = block_causal_attention(q, k, v)
    return o.reshape(b, s, MLA_HEADS * MLA_V) @ w_o

def fox_mixer(hn, w_in, b_f, g_qn, g_kn, w_o):
    b, s, _ = hn.shape
    hd = FOX_HEADS * FOX_HEAD_DIM
    z = hn @ w_in
    q = z[..., :hd].reshape(b, s, FOX_HEADS, FOX_HEAD_DIM)
    k = z[..., hd:2 * hd].reshape(b, s, FOX_HEADS, FOX_HEAD_DIM)
    v = z[..., 2 * hd:3 * hd].reshape(b, s, FOX_HEADS, FOX_HEAD_DIM)
    f_logit = z[..., 3 * hd:].astype(jnp.float32) + b_f.astype(jnp.float32)
    log_f = jax.nn.log_sigmoid(f_logit)
    decay = jnp.cumsum(log_f, axis=1)
    q = rms_norm(q, g_qn)
    k = rms_norm(k, g_kn)
    o = block_causal_attention(q, k, v, decay)
    return o.reshape(b, s, hd) @ w_o

def first_inputs(seed: int = 0) -> dict:
    key = jax.random.key(seed)
    ks = iter(jax.random.split(key, 40))

    def dense(shape, fan_in):
        return jax.random.normal(next(ks), shape, jnp.float32) * (fan_in ** -0.5)

    def gain(shape):
        return 1.0 + 0.1 * jax.random.normal(next(ks), shape, jnp.float32)

    x = jax.random.normal(next(ks), (BATCH, SEQ, D_MODEL), jnp.float32)
    p = jax.random.normal(next(ks), (DEPTH, BATCH, SEQ, PLE_DIM), jnp.float32)
    positions = jnp.broadcast_to(jnp.arange(SEQ, dtype=jnp.int32), (BATCH, SEQ))
    na, nf = N_MLA_LAYERS, N_FOX_LAYERS
    fox_in = 3 * FOX_HEADS * FOX_HEAD_DIM + FOX_HEADS
    return {
        "x": x,
        "p": p,
        "positions": positions,
        "g_ffn1": gain((DEPTH, D_MODEL)),
        "g_mix": gain((DEPTH, D_MODEL)),
        "g_ffn2": gain((DEPTH, D_MODEL)),
        "g_ple": gain((DEPTH, D_MODEL)),
        "ffn1_w_in": dense((DEPTH, D_MODEL, 2 * D_FF), D_MODEL),
        "ffn1_w_out": dense((DEPTH, D_FF, D_MODEL), D_FF),
        "ffn2_w_in": dense((DEPTH, D_MODEL, 2 * D_FF), D_MODEL),
        "ffn2_w_out": dense((DEPTH, D_FF, D_MODEL), D_FF),
        "ple_w_proj": dense((DEPTH, PLE_DIM, D_MODEL), PLE_DIM),
        "ple_w_gate": dense((DEPTH, D_MODEL, D_MODEL), D_MODEL),
        "mla_w_in": dense((na, D_MODEL, MLA_Q_RANK + MLA_KV_RANK + MLA_ROPE), D_MODEL),
        "mla_g_q_lat": gain((na, MLA_Q_RANK)),
        "mla_w_uq": dense((na, MLA_Q_RANK, MLA_HEADS * (MLA_NOPE + MLA_ROPE)), MLA_Q_RANK),
        "mla_g_kv_lat": gain((na, MLA_KV_RANK)),
        "mla_w_ukv": dense((na, MLA_KV_RANK, MLA_HEADS * (MLA_NOPE + MLA_V)), MLA_KV_RANK),
        "mla_g_qn": gain((na, MLA_NOPE + MLA_ROPE)),
        "mla_g_kn": gain((na, MLA_NOPE + MLA_ROPE)),
        "mla_w_o": dense((na, MLA_HEADS * MLA_V, D_MODEL), MLA_HEADS * MLA_V),
        "fox_w_in": dense((nf, D_MODEL, fox_in), D_MODEL),
        "fox_b_f": jax.random.uniform(next(ks), (nf, FOX_HEADS), jnp.float32, 1.0, 4.0),
        "fox_g_qn": gain((nf, FOX_HEAD_DIM)),
        "fox_g_kn": gain((nf, FOX_HEAD_DIM)),
        "fox_w_o": dense((nf, FOX_HEADS * FOX_HEAD_DIM, D_MODEL), FOX_HEADS * FOX_HEAD_DIM),
    }

def first_block(x, p, positions, g_ffn1, g_mix, g_ffn2, g_ple,
              ffn1_w_in, ffn1_w_out, ffn2_w_in, ffn2_w_out, ple_w_proj, ple_w_gate,
              mla_w_in, mla_g_q_lat, mla_w_uq, mla_g_kv_lat, mla_w_ukv,
              mla_g_qn, mla_g_kn, mla_w_o,
              fox_w_in, fox_b_f, fox_g_qn, fox_g_kn, fox_w_o):
    h = x
    for i in range(DEPTH):
        h = h + FFN_HALF * swiglu(rms_norm(h, g_ffn1[i]), ffn1_w_in[i], ffn1_w_out[i])
        hn = rms_norm(h, g_mix[i])
        j = i // N_MIXERS
        if i % N_MIXERS == 0:
            h = h + mla_mixer(hn, positions, mla_w_in[j], mla_g_q_lat[j], mla_w_uq[j],
                              mla_g_kv_lat[j], mla_w_ukv[j], mla_g_qn[j], mla_g_kn[j],
                              mla_w_o[j])
        else:
            h = h + fox_mixer(hn, fox_w_in[j], fox_b_f[j], fox_g_qn[j], fox_g_kn[j],
                              fox_w_o[j])
        h = h + FFN_HALF * swiglu(rms_norm(h, g_ffn2[i]), ffn2_w_in[i], ffn2_w_out[i])
        gate = jax.nn.sigmoid(rms_norm(h, g_ple[i]) @ ple_w_gate[i])
        h = h + gate * (p[i] @ ple_w_proj[i])
    return h


DEPTH_2 = 1

CHUNK = 64
CONV_A_GROUPS = 8
CONV_A_GROUP_DIM = D_MODEL // 16
CONV_A_DIM = CONV_A_GROUPS * CONV_A_GROUP_DIM
CONV_A_WIDTH = 3
DN_HEADS = 4
DN_HEAD_DIM = D_MODEL // 8
DN_DIM = DN_HEADS * DN_HEAD_DIM
DN_CONV_WIDTH = 4
MIX_DIM = CONV_A_DIM + DN_DIM
IN_PROJ_DIM = 3 * CONV_A_DIM + 4 * DN_DIM + 2 * DN_HEADS
N_GROUPS = 4
EXPERTS_PER_GROUP = 8
N_EXPERTS = N_GROUPS * EXPERTS_PER_GROUP
TOP_K = 2
EXPERT_FF = D_MODEL // 2
MOE_BLOCK = 128


def rms_norm_2(x, g):
    xf = x.astype(jnp.float32)
    y = xf * lax.rsqrt(jnp.mean(xf * xf, axis=-1, keepdims=True) + EPS)
    return (y * g.astype(jnp.float32)).astype(x.dtype)

def causal_dwconv(x, w):
    K = w.shape[0]
    S = x.shape[1]
    xp = jnp.pad(x, ((0, 0), (K - 1, 0), (0, 0)))
    y = xp[:, 0:S] * w[0]
    for j in range(1, K):
        y = y + xp[:, j:j + S] * w[j]
    return y

def short_conv_mixer(hx, b, c, conv_w, norm_g):
    Bsz, S, _ = hx.shape
    y = b * causal_dwconv(c * hx, conv_w)
    y = y.reshape(Bsz, S, CONV_A_GROUPS, CONV_A_GROUP_DIM)
    y = rms_norm_2(y, norm_g.reshape(CONV_A_GROUPS, CONV_A_GROUP_DIM))
    return y.reshape(Bsz, S, CONV_A_DIM)

def chunk_gated_delta(q, k, v, beta, g):
    Bsz, H, S, dk = q.shape
    dv = v.shape[-1]
    n = S // CHUNK

    def chunks(t):
        return t.reshape((Bsz, H, n, CHUNK) + t.shape[3:])

    q, k, v, beta, g = chunks(q), chunks(k), chunks(v), chunks(beta), chunks(g)
    g = jnp.cumsum(g, axis=-1)
    causal = jnp.tril(jnp.ones((CHUNK, CHUNK), bool))
    strict = jnp.tril(jnp.ones((CHUNK, CHUNK), bool), -1)
    decay = jnp.exp(jnp.where(causal, g[..., :, None] - g[..., None, :], -jnp.inf))
    k_beta = k * beta[..., None]
    L = jnp.where(strict, jnp.einsum('bhncd,bhnjd->bhncj', k_beta, k) * decay, 0.0)
    eye = jnp.eye(CHUNK, dtype=jnp.float32)
    rhs = jnp.concatenate([v * beta[..., None], k_beta * jnp.exp(g)[..., None]], axis=-1)
    uw = lax.linalg.triangular_solve(eye + L, rhs, left_side=True, lower=True, unit_diagonal=True)
    u, w = uw[..., :dv], uw[..., dv:]
    intra = jnp.einsum('bhncd,bhnjd->bhncj', q, k) * decay
    q_dec = q * jnp.exp(g)[..., None]
    g_last = g[..., -1]
    k_dec = k * jnp.exp(g_last[..., None] - g)[..., None]

    def to_scan(t):
        return jnp.moveaxis(t, 2, 0)

    xs = (to_scan(u), to_scan(w), to_scan(q_dec), to_scan(intra), to_scan(k_dec), to_scan(g_last))

    def step(state, inp):
        u_i, w_i, qd_i, a_i, kd_i, gl_i = inp
        v_new = u_i - jnp.einsum('bhck,bhkv->bhcv', w_i, state)
        o_i = jnp.einsum('bhck,bhkv->bhcv', qd_i, state) + jnp.einsum('bhcj,bhjv->bhcv', a_i, v_new)
        state = state * jnp.exp(gl_i)[..., None, None] + jnp.einsum('bhck,bhcv->bhkv', kd_i, v_new)
        return state, o_i

    s0 = jnp.zeros((Bsz, H, dk, dv), jnp.float32)
    _, o = lax.scan(step, s0, xs)
    return jnp.moveaxis(o, 0, 2).reshape(Bsz, H, S, dv)

def gated_deltanet(q, k, v, z, beta_logit, a_logit, conv_w, a_log, dt_bias, norm_g):
    Bsz, S, _ = q.shape
    dtype = q.dtype
    qkv = jax.nn.silu(causal_dwconv(jnp.concatenate([q, k, v], axis=-1), conv_w)).astype(jnp.float32)
    q, k, v = jnp.split(qkv, 3, axis=-1)

    def heads(t):
        return t.reshape(Bsz, S, DN_HEADS, DN_HEAD_DIM).transpose(0, 2, 1, 3)

    q, k, v = heads(q), heads(k), heads(v)
    q = q * lax.rsqrt(jnp.sum(q * q, axis=-1, keepdims=True) + EPS) * (DN_HEAD_DIM ** -0.5)
    k = k * lax.rsqrt(jnp.sum(k * k, axis=-1, keepdims=True) + EPS)
    beta = jax.nn.sigmoid(beta_logit.astype(jnp.float32)).transpose(0, 2, 1)
    g = (-jnp.exp(a_log.astype(jnp.float32))
         * jax.nn.softplus(a_logit.astype(jnp.float32) + dt_bias.astype(jnp.float32))).transpose(0, 2, 1)
    o = chunk_gated_delta(q, k, v, beta, g).transpose(0, 2, 1, 3)
    zf = z.astype(jnp.float32).reshape(Bsz, S, DN_HEADS, DN_HEAD_DIM)
    o = rms_norm_2(o, norm_g) * jax.nn.silu(zf)
    return o.reshape(Bsz, S, DN_DIM).astype(dtype)

def hier_moe(h, router_group_w, router_expert_w, w_gate, w_up, w_down):
    N, D = h.shape
    group_logits = (h @ router_group_w).astype(jnp.float32)
    group_idx = jnp.argmax(group_logits, axis=-1)
    group_prob = jnp.take_along_axis(jax.nn.softmax(group_logits, axis=-1), group_idx[:, None], axis=1)
    exp_logits = (h @ router_expert_w).astype(jnp.float32).reshape(N, N_GROUPS, EXPERTS_PER_GROUP)
    exp_logits = jnp.take_along_axis(exp_logits, group_idx[:, None, None], axis=1)[:, 0]
    top_p, top_local = lax.top_k(jax.nn.softmax(exp_logits, axis=-1), TOP_K)
    gate = group_prob * top_p / jnp.sum(top_p, axis=-1, keepdims=True)
    expert_id = (group_idx[:, None] * EXPERTS_PER_GROUP + top_local).astype(jnp.int32)

    flat_e = expert_id.reshape(-1)
    flat_tok = jnp.repeat(jnp.arange(N, dtype=jnp.int32), TOP_K)
    flat_gate = gate.reshape(-1)
    order = jnp.argsort(flat_e)
    sorted_e = flat_e[order]
    counts = jnp.bincount(flat_e, length=N_EXPERTS)
    padded = (counts + MOE_BLOCK - 1) // MOE_BLOCK * MOE_BLOCK
    pad_end = jnp.cumsum(padded)
    pad_start = pad_end - padded
    start = jnp.cumsum(counts) - counts
    dest = pad_start[sorted_e] + jnp.arange(N * TOP_K, dtype=jnp.int32) - start[sorted_e]
    P = N * TOP_K + N_EXPERTS * MOE_BLOCK
    slot_tok = jnp.full((P,), N, jnp.int32).at[dest].set(flat_tok[order])
    slot_gate = jnp.zeros((P,), jnp.float32).at[dest].set(flat_gate[order])
    n_blocks = P // MOE_BLOCK
    block_expert = jnp.minimum(
        jnp.searchsorted(pad_end, jnp.arange(n_blocks, dtype=jnp.int32) * MOE_BLOCK, side='right'),
        N_EXPERTS - 1)
    h_pad = jnp.concatenate([h, jnp.zeros((1, D), h.dtype)], axis=0)
    xb = h_pad[slot_tok].reshape(n_blocks, MOE_BLOCK, D)

    def expert_block(args):
        xblk, e = args
        a = xblk @ w_gate[e]
        b = xblk @ w_up[e]
        return (jax.nn.silu(a) * b) @ w_down[e]

    yb = lax.map(expert_block, (xb, block_expert)).reshape(P, D)
    out = jnp.zeros((N + 1, D), jnp.float32).at[slot_tok].add(yb.astype(jnp.float32) * slot_gate[:, None])
    return out[:N].astype(h.dtype)

def second_inputs(seed: int = 0) -> dict:
    key = jax.random.key(seed)
    ks = jax.random.split(key, 18)
    f32 = jnp.float32

    def normal(k, shape, scale):
        return jax.random.normal(k, shape, f32) * scale

    def gain(k, shape):
        return 1.0 + 0.05 * jax.random.normal(k, shape, f32)

    dt = jnp.exp(jax.random.uniform(ks[7], (DEPTH_2, DN_HEADS), f32, math.log(1e-3), math.log(1e-1)))
    return {
        "x": normal(ks[0], (BATCH, SEQ, D_MODEL), 1.0),
        "mix_norm_g": gain(ks[1], (DEPTH_2, D_MODEL)),
        "w_in": normal(ks[2], (DEPTH_2, D_MODEL, IN_PROJ_DIM), D_MODEL ** -0.5),
        "conv_a_w": normal(ks[3], (DEPTH_2, CONV_A_WIDTH, CONV_A_DIM), CONV_A_WIDTH ** -0.5),
        "conv_a_norm_g": gain(ks[4], (DEPTH_2, CONV_A_DIM)),
        "dn_conv_w": normal(ks[5], (DEPTH_2, DN_CONV_WIDTH, 3 * DN_DIM), DN_CONV_WIDTH ** -0.5),
        "dn_a_log": jnp.log(jax.random.uniform(ks[6], (DEPTH_2, DN_HEADS), f32, 1.0, 16.0)),
        "dn_dt_bias": dt + jnp.log(-jnp.expm1(-dt)),
        "dn_norm_g": gain(ks[8], (DEPTH_2, DN_HEAD_DIM)),
        "w_out": normal(ks[9], (DEPTH_2, MIX_DIM, D_MODEL), MIX_DIM ** -0.5),
        "ffn_norm_g": gain(ks[10], (DEPTH_2, D_MODEL)),
        "router_group_w": normal(ks[11], (DEPTH_2, D_MODEL, N_GROUPS), D_MODEL ** -0.5),
        "router_expert_w": normal(ks[12], (DEPTH_2, D_MODEL, N_EXPERTS), D_MODEL ** -0.5),
        "w_gate": normal(ks[13], (DEPTH_2, N_EXPERTS, D_MODEL, EXPERT_FF), D_MODEL ** -0.5),
        "w_up": normal(ks[14], (DEPTH_2, N_EXPERTS, D_MODEL, EXPERT_FF), D_MODEL ** -0.5),
        "w_down": normal(ks[15], (DEPTH_2, N_EXPERTS, EXPERT_FF, D_MODEL), EXPERT_FF ** -0.5),
        "final_norm_g": gain(ks[16], (D_MODEL,)),
    }

def second_block(x, mix_norm_g, w_in, conv_a_w, conv_a_norm_g, dn_conv_w, dn_a_log, dn_dt_bias,
              dn_norm_g, w_out, ffn_norm_g, router_group_w, router_expert_w, w_gate, w_up, w_down,
              final_norm_g):
    Bsz, S, D = x.shape
    sizes = (CONV_A_DIM,) * 3 + (DN_DIM,) * 4 + (DN_HEADS,) * 2
    split_idx = []
    acc = 0
    for s in sizes[:-1]:
        acc += s
        split_idx.append(acc)
    for l in range(DEPTH_2):
        h = rms_norm_2(x, mix_norm_g[l])
        proj = h @ w_in[l]
        a_h, a_b, a_c, d_q, d_k, d_v, d_z, d_beta, d_alpha = jnp.split(proj, split_idx, axis=-1)
        y_a = short_conv_mixer(a_h, a_b, a_c, conv_a_w[l], conv_a_norm_g[l])
        y_b = gated_deltanet(d_q, d_k, d_v, d_z, d_beta, d_alpha, dn_conv_w[l], dn_a_log[l],
                             dn_dt_bias[l], dn_norm_g[l])
        x = x + jnp.concatenate([y_a, y_b], axis=-1) @ w_out[l]
        h = rms_norm_2(x, ffn_norm_g[l]).reshape(Bsz * S, D)
        x = x + hier_moe(h, router_group_w[l], router_expert_w[l], w_gate[l], w_up[l], w_down[l]).reshape(Bsz, S, D)
    return rms_norm_2(x, final_norm_g)


def setup_inputs(seed=0):
    out = dict(first_inputs(seed))
    for name, value in second_inputs(seed + 1).items():
        if name != "x":
            out[name + "_2"] = value
    return out


def reference(
    x, p, positions, g_ffn1, g_mix, g_ffn2, g_ple, ffn1_w_in, ffn1_w_out, ffn2_w_in, ffn2_w_out,
    ple_w_proj, ple_w_gate, mla_w_in, mla_g_q_lat, mla_w_uq, mla_g_kv_lat, mla_w_ukv, mla_g_qn,
    mla_g_kn, mla_w_o, fox_w_in, fox_b_f, fox_g_qn, fox_g_kn, fox_w_o, mix_norm_g_2, w_in_2,
    conv_a_w_2, conv_a_norm_g_2, dn_conv_w_2, dn_a_log_2, dn_dt_bias_2, dn_norm_g_2, w_out_2,
    ffn_norm_g_2, router_group_w_2, router_expert_w_2, w_gate_2, w_up_2, w_down_2,
    final_norm_g_2,
):
    x = first_block(
        x, p, positions, g_ffn1, g_mix, g_ffn2, g_ple, ffn1_w_in, ffn1_w_out, ffn2_w_in,
        ffn2_w_out, ple_w_proj, ple_w_gate, mla_w_in, mla_g_q_lat, mla_w_uq, mla_g_kv_lat,
        mla_w_ukv, mla_g_qn, mla_g_kn, mla_w_o, fox_w_in, fox_b_f, fox_g_qn, fox_g_kn, fox_w_o,
    )
    return second_block(
        x, mix_norm_g_2, w_in_2, conv_a_w_2, conv_a_norm_g_2, dn_conv_w_2, dn_a_log_2,
        dn_dt_bias_2, dn_norm_g_2, w_out_2, ffn_norm_g_2, router_group_w_2, router_expert_w_2,
        w_gate_2, w_up_2, w_down_2, final_norm_g_2,
    )


_drawn_inputs = setup_inputs


def setup_inputs(seed=0):
    import zlib

    import numpy as np

    out = dict(_drawn_inputs(seed))
    spreads = {}
    factors = {'dn_norm_g_2': 3.085, 'conv_a_norm_g_2': 2.703, 'ffn_norm_g_2': 2.696}
    for name, (base, spread) in spreads.items():
        noise = np.random.default_rng([zlib.crc32(name.encode()), seed]).standard_normal(out[name].shape)
        drawn = base * np.exp(spread * noise) if base else spread * noise
        out[name] = __import__('jax').numpy.asarray(drawn.astype(out[name].dtype))
    for name, factor in factors.items():
        out[name] = (out[name] * factor).astype(out[name].dtype)
    return out
```

```python
from contextlib import ExitStack

import numpy as np
import concourse.bass as bass
from concourse import mybir

P = 128
T = 256
D = 1024
KD = D // P
DEPTH = 2
FF = 2816
FFC = FF // P
PLE = 256
EPS = 1e-6
H = 16
QR, KVR, NOPE, ROPE, DV = 512, 256, 64, 32, 64
QK = NOPE + ROPE
DNH = 4
CG = 512
NE, NG, EPG, EFF = 32, 4, 8, 512
EC = EFF // P
CT = 24
RING = 4
NEG = -1.0e30

F32 = mybir.dt.float32
I32 = mybir.dt.int32
ALU = mybir.AluOpType
ACT = mybir.ActivationFunctionType
AXX = mybir.AxisListType.X


def chunks_of(tiles):
    return -(-tiles // CT)


def stream_plan():
    sizes = []
    for layer in range(DEPTH):
        sizes.append((f"ffn1_{layer}", FFC))
        if layer == 0:
            sizes += [("mla_in", chunks_of(7 * KD)), ("mla_q", chunks_of(H * 4)), ("mla_kv", chunks_of(32)),
                      ("mla_o", chunks_of(64))]
        else:
            sizes += [("fox_qk", chunks_of(128)), ("fox_v", chunks_of(64)), ("fox_o", chunks_of(64))]
        sizes += [(f"ffn2_{layer}", FFC), (f"ple_{layer}", chunks_of(80))]
    sizes += [("mix_in", chunks_of(28 * KD)), ("mix_out", chunks_of(64)), ("moe", NE * EC)]
    plan, at = {}, 0
    for name, n in sizes:
        plan[name] = at
        at += n
    return plan, at


PLAN, N_CHUNKS = stream_plan()

PARAMS = [("g_ffn1_0", 8), ("g_mix_0", 8), ("g_ffn2_0", 8), ("g_ple_0", 8), ("g_ffn1_1", 8), ("g_mix_1", 8),
          ("g_ffn2_1", 8), ("g_ple_1", 8), ("g_q_lat", 4), ("g_kv_lat", 2), ("mla_qn", 1), ("mla_kn", 1),
          ("fox_qn", 1), ("fox_kn", 1), ("g_mix2", 8), ("conv_a_w", 12), ("conv_a_g", 4), ("dn_conv_w", 48),
          ("dn_g", 1), ("g_ffn_2", 8), ("g_final", 8), ("inv_freq", 1), ("rope_sign", 1), ("b_f", 16),
          ("a_log", 4), ("dt_bias", 4), ("w_f", 128), ("w_ba", 64), ("w_router", 8 * 36), ("first_wins", 32)]
COL, NPAR = {}, 0
for _name, _n in PARAMS:
    COL[_name] = NPAR
    NPAR += _n

LIN, _at = {}, 0
for _name, _n in [("mla_in", 4), ("mla_q", 8), ("mla_k", 8), ("mla_v", 4), ("mla_o", 4), ("ple_0", 8),
                  ("fox_qk", 8), ("fox_v", 4), ("fox_o", 4), ("ple_1", 8), ("mix_in", 14), ("mix_out", 4)]:
    LIN[_name] = _at
    _at += _n

HN = {"mla_q": 0, "mla_k": 8, "fox_qk": 16, "conv_a": 24, "dn_q": 26, "dn_k": 28, "dn_o": 30}
NORM = {n: i for i, n in enumerate(["ffn1_0", "mix_0", "q_lat", "kv_lat", "ffn2_0", "ple_0", "ffn1_1", "mix_1",
                                    "ffn2_1", "ple_1", "mix2", "ffn_2", "final"])}
GU = {"ffn1_0": 0, "ffn2_0": FFC, "ffn1_1": 2 * FFC, "ffn2_1": 3 * FFC, "moe": 4 * FFC}
HREADY = {"ffn1_0": 1, "mix_0": 2, "ffn2_0": 3, "ple_0": 4, "ffn1_1": 5, "mix_1": 6, "ffn2_1": 7, "ple_1": 8,
          "mix2": 9, "ffn_2": 10, "final": 11}
TWO_PI = 6.283185307179586
PI2_A = 6.28125
PI2_B = 0.0019350051879882812
PI2_C = TWO_PI - PI2_A - PI2_B
ROUND = 1.5 * 2 ** 23


class Steps:

    def __init__(self, eng, sem):
        self.eng, self.sem, self.n = eng, sem, 0

    def done(self, ins):
        self.n += 1
        ins.then_inc(self.sem, 1)

    def settled(self):
        self.eng.wait_ge(self.sem, self.n)

    def link(self, ins):
        self.done(ins)
        self.settled()


def two_block_kernel(nc, xT, pT, pos, par, weights, out):
    with ExitStack() as ctx:
        def sb(name, shape, dt=F32):
            return ctx.enter_context(nc.sbuf_tensor("sb_" + name, shape, dt))

        def sem(name):
            return ctx.enter_context(nc.semaphore(name))

        ring = sb("ring", [P, RING, CT * P])
        h = sb("h", [P, KD, T])
        hn = sb("hn", [P, KD, T])
        sq = sb("sq", [P, KD, T])
        lnv = sb("lnv", [P, 2, 2 * T])
        rstd = sb("rstd", [P, 2, T])
        params = sb("params", [P, NPAR])
        pin = sb("pin", [P, 2 * DEPTH, T])
        ones = sb("ones", [P, P])
        ones64 = sb("ones64", [P, P])
        ident = sb("ident", [P, P])
        upper = sb("upper", [P, P])
        mask = sb("mask", [P, 3 * P])
        head_row = sb("head_row", [H, H, P])
        eps_col = sb("eps_col", [P, 1])
        level = sb("level", [P, 7, P])
        expg = sb("expg", [P, 2, T])
        gate_r = sb("gate_r", [P, 2, T])
        act = sb("act", [P, 2, T])
        qk = sb("qk", [P, 2 * H, T])
        qT, kT = qk[:, 0:H, :], qk[:, H:2 * H, :]
        v_tok = sb("v_tok", [P, 2, D])
        oT = sb("oT", [P, KD, T])
        sqh = sb("sqh", [P, 2, 2, T])
        rsh = sb("rsh", [P, 2, 2 * T])
        cosr = sb("cosr", [P, T])
        sinr = sb("sinr", [P, T])
        rope_t = sb("rope_t", [P, 3, 2 * T])
        kpe = sb("kpe", [P, T])
        kr = sb("kr", [P, T])
        gq = sb("gq", [P, 4])
        logits = sb("logits", [P, 2, 3 * P])
        probs = sb("probs", [P, 2, 3 * P])
        pT_sb = sb("pT_sb", [P, 2, 3 * P])
        nmax = sb("nmax", [P, 2 * H, 2])
        psums = sb("psums", [P, 2 * H, 2])
        small = sb("small", [P, 512])
        ndec = sb("ndec", [H, T])
        dtok = sb("dtok", [P, 2, H])
        scratch = sb("scratch", [P, 5224])
        route = sb("route", [P, 2, 320])

        posi = v_tok[:, 0, 0:T].bitcast(I32)
        cq = oT[:, 0:4, :]
        ckv = oT[:, 4:6, :]
        PADQ = T + 3
        PADU = T + 2
        gate_rows = qk[:, :, :].rearrange("p e t -> p (e t)")
        qkv_pad = scratch[:, 0:12 * PADQ].rearrange("p (n t) -> p n t", t=PADQ)
        u_pad = scratch[:, 12 * PADQ:12 * PADQ + 4 * PADU].rearrange("p (n t) -> p n t", t=PADU)
        a_h = qT[:, 0:4, :]
        a_b = qT[:, 4:8, :]
        z_gate = qT[:, 8:12, :]
        y_a = qT[:, 12:16, :]
        qkv = kT[:, 0:12, :]
        convt = kT[:, 12:16, :]
        mixT = oT

        B = [ctx.enter_context(nc.psum_tensor(f"bank{i}", [P, 512], F32)) for i in range(8)]
        OUTB = B[4:8]

        par_in, x_in, p_in, pos_in = sem("par_in"), sem("x_in"), sem("p_in"), sem("pos_in")
        slot_in = [sem(f"slot_in{j}") for j in range(RING)]
        ring_free = sem("ring_free")
        consts = sem("consts")
        pool_step = sem("pool_step")
        act_step = sem("act_step")
        dve_step = sem("dve_step")
        h_ready = sem("h_ready")
        norm_sq, norm_sum, norm_rstd, norm_out = sem("norm_sq"), sem("norm_sum"), sem("norm_rstd"), sem("norm_out")
        gu_ready, sig_ready, glu_step, act_ready, acc_ready = (
            sem("gu_ready"), sem("sig_ready"), sem("glu_step"), sem("act_ready"), sem("acc_ready"))
        lin_ready, lin_free = sem("lin_ready"), sem("lin_free")
        hn_src, hn_sq, hn_sum, hn_rs, hn_done = sem("hn_src"), sem("hn_sq"), sem("hn_sum"), sem("hn_rs"), sem("hn_done")
        rope_arg, rope_sin = sem("rope_arg"), sem("rope_sin")
        scores, masked, expd, rcpd, prob_ready = sem("scores"), sem("masked"), sem("expd"), sem("rcpd"), sem("prob_ready")
        turned, pt_ready, pv_done, o_ready = sem("turned"), sem("pt_ready"), sem("pv_done"), sem("o_ready")
        f_ready, f_abs, f_ln, logf_ready, dec_sum, dec_ready = (
            sem("f_ready"), sem("f_abs"), sem("f_ln"), sem("logf_ready"), sem("dec_sum"), sem("dec_ready"))
        ple_e = sem("ple_e")
        silu_in, silu_e, z_exp = sem("silu_in"), sem("silu_e"), sem("z_exp")
        ba_ready, ba_abs, ba_ln, bg_ready = sem("ba_ready"), sem("ba_abs"), sem("ba_ln"), sem("bg_ready")
        rows_ready, gdiff, gdecay, dn_qk, dn_ready = (
            sem("rows_ready"), sem("gdiff"), sem("gdecay"), sem("dn_qk"), sem("dn_ready"))
        tok_ready, tok_scaled = sem("tok_ready"), sem("tok_scaled")
        inv_p, inv_p_sb, inv_x, inv_done = sem("inv_p"), sem("inv_p_sb"), sem("inv_x"), sem("inv_done")
        dn_pe, dn_sb = sem("dn_pe"), sem("dn_sb")
        mix_ready = sem("mix_ready")
        rt_ready, rt_max, rt_exp, rt_gate, rt_rows, rt_free = (
            sem("rt_ready"), sem("rt_max"), sem("rt_exp"), sem("rt_gate"), sem("rt_rows"), sem("rt_free"))
        out_done = sem("out_done")

        def col(name, i=0, n=1):
            return params[:, COL[name] + i:COL[name] + i + n]

        def rep(ap, n):
            return ap.rearrange("p (a t) -> p a t", a=1).to_broadcast([ap.shape[0], n, ap.shape[1]])

        silu_tmp = [v_tok[:, 0, :].rearrange("p (n t) -> p n t", t=T), v_tok[:, 1, :].rearrange("p (n t) -> p n t", t=T),
                    mixT[:, 4:8, :]]
        vflat = v_tok[:, :, :].rearrange("p a n -> p (a n)")
        DELTA = {
            "decay": sq[:, 0:4, :].rearrange("p a t -> p (a t)").rearrange("p (c t) -> p c t", t=P),
            "brow": sq[:, 4:8, :].rearrange("p a t -> p (a t)").rearrange("p (c t) -> p c t", t=P),
            "lt": hn[:, 0:4, :].rearrange("p a t -> p (a t)").rearrange("p (c t) -> p c t", t=P),
            "intra": hn[:, 4:8, :].rearrange("p a t -> p (a t)").rearrange("p (c t) -> p c t", t=P),
            "x": vflat[:, 0:1024].rearrange("p (c t) -> p c t", t=P),
            "xt": vflat[:, 1024:2048].rearrange("p (c t) -> p c t", t=P),
            "lw": pin[:, :, :].rearrange("p a t -> p (a t)").rearrange("p (c t) -> p c t", t=P),
            "pm": mixT[:, 4:8, :].rearrange("p a t -> p (a t)").rearrange("p (c t) -> p c t", t=P),
            "vb": scratch[:, 4200:5224].rearrange("p (c t) -> p c t", t=P),
            "vn": scratch[:, 0:1024].rearrange("p (c t) -> p c t", t=P),
            "kd": scratch[:, 1024:1536].rearrange("p (c t) -> p c t", t=P),
            "state": scratch[:, 1536:2048].rearrange("p (c t) -> p c t", t=P),
            "qd": scratch[:, 2048:2560].rearrange("p (c t) -> p c t", t=P),
            "egrow": scratch[:, 2560:3072].rearrange("p (c t) -> p c t", t=P),
        }

        block = ctx.enter_context(nc.Block())

        @block.sync
        def _(sp):
            sp.dma_start(params[:], par).then_inc(par_in, 16)
            sp.dma_start(h[:], xT).then_inc(x_in, 16)
            for j in range(RING):
                sp.dma_start(ring[:, j, :], weights[j]).then_inc(slot_in[j], 16)
            sp.dma_start(pin[:], pT).then_inc(p_in, 16)
            sp.dma_start(posi, pos).then_inc(pos_in, 16)
            whole = N_CHUNKS // RING
            with sp.Fori(1, whole) as r:
                for j in range(RING):
                    sp.wait_ge(ring_free, r * RING + (j - RING + 1))
                    sp.dma_start(ring[:, j, :], weights[r * RING + j]).then_inc(slot_in[j], 16)
            for n in range(whole * RING, N_CHUNKS):
                sp.wait_ge(ring_free, n - RING + 1)
                sp.dma_start(ring[:, n % RING, :], weights[n]).then_inc(slot_in[n % RING], 16)
            sp.wait_ge(norm_out, NORM["final"] + 1)
            sp.dma_start(out, hn[:]).then_inc(out_done, 16)
            sp.wait_ge(out_done, 16)

        @block.gpsimd
        def _(pool):
            st = Steps(pool, pool_step)
            for t, v in ((ones, 1.0), (ones64, 0.0), (ident, 0.0), (upper, 1.0), (mask, 0.0), (head_row, 0.0),
                         (eps_col, EPS), (level, 1.0)):
                st.link(nc.gpsimd.memset(t[:], v))
            st.link(nc.gpsimd.memset(scratch[:, 0:12 * PADQ + 4 * PADU], 0.0))
            st.settled()
            for g in range(2):
                st.link(nc.gpsimd.memset(ones64[64 * g:64 * g + 64, 64 * g:64 * g + 64], 1.0))
            st.link(nc.gpsimd.affine_select(out=ident[:], in_=ident[:], compare_op=ALU.not_equal, fill=1.0, base=0,
                                            pattern=[[-1, P]], channel_multiplier=1))
            st.link(nc.gpsimd.affine_select(out=upper[:], in_=upper[:], compare_op=ALU.is_ge, fill=0.0, base=0,
                                            pattern=[[1, P]], channel_multiplier=-1))
            for c in (0, 2):
                m = mask[:, c * P:(c + 1) * P]
                st.link(nc.gpsimd.affine_select(out=m, in_=m, compare_op=ALU.is_ge, fill=NEG, base=0,
                                                pattern=[[-1, P]], channel_multiplier=1))
            st.link(nc.gpsimd.affine_select(out=head_row[:], in_=head_row[:], compare_op=ALU.not_equal, fill=1.0,
                                            base=0, pattern=[[-1, H], [0, P]], channel_multiplier=1))
            for i in range(7):
                w = 1 << i
                v = level[:, i, :].rearrange("p (b a r) -> p b a r", a=2, r=w)
                st.link(nc.gpsimd.memset(v[:, :, 0, :], 0.0))
                up = v[:, :, 1, :]
                st.link(nc.gpsimd.affine_select(out=up, in_=up, compare_op=ALU.is_ge, fill=0.0, base=0,
                                                pattern=[[-2 * w, P // (2 * w)], [0, w]], channel_multiplier=1))
                st.link(nc.gpsimd.affine_select(out=up, in_=up, compare_op=ALU.is_ge, fill=0.0, base=w - 1,
                                                pattern=[[2 * w, P // (2 * w)], [0, w]], channel_multiplier=-1))
            st.settled()
            nc.gpsimd.memset(small[:, 511:512], 0.0).then_inc(consts, 1)

        @block.tensor
        def _(pe):
            owed = [0]

            def mm(o, l, r, start, stop, inc=None):
                ins = nc.tensor.matmul(o, l, r, start=start, stop=stop, skip_group_check=True)
                if inc is not None:
                    ins.then_inc(inc, 1)
                elif owed[0]:
                    ins.then_inc(ring_free, owed[0])
                    owed[0] = 0
                return ins

            def chunk_in(n):
                pe.wait_ge(slot_in[n % RING], 16 * (n // RING + 1))

            def tile(n, i, c0=0, c1=P):
                return ring[:, n % RING, i * P + c0:i * P + c1]

            class Tiles:

                def __init__(self, name):
                    self.at, self.i = PLAN[name], 0

                def next(self, c0=0, c1=P, width=1, hold=False):
                    n, i = self.at + self.i // CT, self.i % CT
                    if i == 0:
                        chunk_in(n)
                    self.i += width
                    return ring[:, n % RING, i * P + c0:(i + width - 1) * P + c1]

                def used(self):
                    if self.i % CT == 0:
                        owed[0] += 1

                def end(self):
                    if self.i % CT:
                        owed[0] += 1

            def norm_sums(name, nk):
                n = NORM[name]
                pe.wait_ge(norm_sq, n + 1)
                for k in range(nk):
                    mm(B[2][:, 0:T], ones[:], sq[:, k, :], k == 0, k == nk - 1, norm_sum if k == nk - 1 else None)

            def normed(name):
                pe.wait_ge(norm_out, NORM[name] + 1)

            def bank_free(g):
                if g >= 4:
                    pe.wait_ge(lin_free, g - 3)
                return OUTB[g % 4]

            def project(name, lin, groups, rhs, nk, per=2, cols=P):
                tl = Tiles(name)
                for g in range(groups[0], groups[1]):
                    bank = bank_free(LIN[lin] + g)
                    n_tiles = per(g) if callable(per) else per
                    for j in range(n_tiles):
                        for k in range(nk):
                            mm(bank[0:cols, j * T:(j + 1) * T], tl.next(0, cols), rhs[:, k, :], k == 0, k == nk - 1,
                               lin_ready if k == nk - 1 and j == n_tiles - 1 else None)
                            tl.used()
                tl.end()

            def head_sums(g, lhsT, parts):
                pe.wait_ge(hn_sq, g + 1)
                mm(B[2 + g % 2][0:parts, :], lhsT, sqh[0:parts, g % 2, :, :].rearrange("p a t -> p (a t)"), True, True,
                   hn_sum)

            def gated(name, n_chunks, peel):
                base, gu0 = PLAN[name], GU[name]

                def gate_up(slot, par):
                    for part in range(2):
                        for k in range(KD):
                            last = part == 1 and k == KD - 1
                            mm(B[par][:, part * T:(part + 1) * T], tile(slot, part * KD + k), hn[:, k, :], k == 0,
                               k == KD - 1, gu_ready if last else None)

                def down(slot, par, start, stop, free):
                    for m in range(KD):
                        inc = None
                        if m == KD - 1:
                            inc = acc_ready if stop else ring_free
                        mm(OUTB[m // 2][:, (m % 2) * T:(m % 2 + 1) * T], tile(slot, 2 * KD + m), act[:, par, :],
                           start and m % 2 == 0, stop, inc)

                chunk_in(base)
                gate_up(base, 0)
                for c in range(1, peel):
                    chunk_in(base + c)
                    gate_up(base + c, c % 2)
                    pe.wait_ge(act_ready, gu0 + c)
                    down(base + c - 1, (c - 1) % 2, c == 1, False, True)
                with pe.Fori(0, (n_chunks - peel) // RING) as r:
                    for j in range(RING):
                        c = peel + j
                        pe.wait_ge(slot_in[(base + c) % RING], r * 16 + 16 * ((base + c) // RING + 1))
                        gate_up(base + c, c % 2)
                        pe.wait_ge(act_ready, r * RING + (gu0 + c))
                        down(base + c - 1, (c - 1) % 2, False, False, True)
                pe.wait_ge(act_ready, gu0 + n_chunks)
                down(base + n_chunks - 1, (n_chunks - 1) % 2, False, True, False)
                owed[0] += 1

            def attention(first, kq, fox):
                for i in range(H + 2):
                    if i < H:
                        a = first + i
                        if i >= 2:
                            pe.wait_ge(masked, a - 1)
                        s = B[a % 2]
                        for cols, q0, k1 in ((0, 0, P), (P, P, T)):
                            ql, kl = kq(i, q0, q0 + P, 0, k1)
                            mm(s[:, cols:cols + k1], ql, kl, True, not fox,
                               None if fox or cols == 0 else scores)
                            if fox:
                                mm(s[:, cols:cols + k1], head_row[:, i, :], ndec[:, 0:k1], False, True,
                                   None if cols == 0 else scores)
                    if 1 <= i <= H:
                        a = first + i - 1
                        pe.wait_ge(prob_ready, a + 1)
                        for j in range(3):
                            ins = nc.tensor.transpose(B[2 + a % 2][:, j * P:(j + 1) * P],
                                                      probs[:, a % 2, j * P:(j + 1) * P], ident[:])
                        ins.then_inc(turned, 1)
                    if i >= 2:
                        hd = i - 2
                        a = first + hd
                        pair = a // 2
                        pe.wait_ge(pt_ready, a + 1)
                        if hd % 2 == 0 and hd >= 4:
                            pe.wait_ge(o_ready, pair - 1)
                        ob = B[4 + pair % 2]
                        lo = 64 * (hd % 2)
                        v0, v1 = (v_tok[:, c, hd * DV:(hd + 1) * DV] for c in range(2))
                        mm(ob[lo:lo + DV, 0:P], v0, pT_sb[:, a % 2, 0:P], True, True)
                        mm(ob[lo:lo + DV, P:T], v0, pT_sb[:, a % 2, P:2 * P], True, False)
                        mm(ob[lo:lo + DV, P:T], v1, pT_sb[:, a % 2, 2 * P:3 * P], False, True, pv_done)

            def ple(layer):
                name = f"ple_{layer}"
                norm_sums(name, KD)
                normed(name)
                if layer == 0:
                    pe.wait_ge(p_in, 16)
                tl = Tiles(name)
                for m in range(KD):
                    bank = bank_free(LIN[name] + m)
                    for k in range(KD):
                        mm(bank[:, 0:T], tl.next(), hn[:, k, :], k == 0, k == KD - 1)
                        tl.used()
                    for k in range(2):
                        mm(bank[:, T:2 * T], tl.next(), pin[:, 2 * layer + k, :], k == 0, k == 1,
                           lin_ready if k == 1 else None)
                        tl.used()
                tl.end()

            def values(name, lin, src, nk):
                tl = Tiles(name)
                tl.i = 0 if name != "mla_kv" else 16
                for half in range(2):
                    t0 = tl.i
                    w = []
                    for k in range(nk):
                        n, i = tl.at + tl.i // CT, tl.i % CT
                        if i == 0:
                            chunk_in(n)
                        w.append(ring[:, n % RING, i * P:(i + 4) * P])
                        tl.i += 4
                    for c in range(2):
                        bank = bank_free(LIN[lin] + 2 * half + c)
                        for k in range(nk):
                            mm(bank[:, :], src[:, k, c * P:(c + 1) * P], w[k], k == 0, k == nk - 1,
                               lin_ready if k == nk - 1 else None)
                    owed[0] += tl.i // CT - t0 // CT
                tl.end()

            pe.wait_ge(consts, 1)
            norm_sums("ffn1_0", KD)
            normed("ffn1_0")
            gated("ffn1_0", FFC, 2)

            norm_sums("mix_0", KD)
            normed("mix_0")
            project("mla_in", "mla_in", (0, 4), hn, KD, per=lambda g: 2 if g < 3 else 1)
            norm_sums("q_lat", 4)
            norm_sums("kv_lat", 2)
            normed("q_lat")
            tl = Tiles("mla_q")
            for g in range(9):
                if g < 8:
                    bank = bank_free(LIN["mla_q"] + g)
                    for j in range(2):
                        for k in range(4):
                            mm(bank[0:QK, j * T:(j + 1) * T], tl.next(0, QK), hn[:, k, :], k == 0, k == 3,
                               lin_ready if k == 3 and j == 1 else None)
                            tl.used()
                if g >= 1:
                    head_sums(HN["mla_q"] + g - 1, ones[0:QK, 0:QK], QK)
            tl.end()
            normed("kv_lat")
            n = PLAN["mla_kv"]
            chunk_in(n)
            for g in range(9):
                if g < 8:
                    bank = bank_free(LIN["mla_k"] + g)
                    for j in range(2):
                        for k in range(2):
                            mm(bank[0:NOPE, j * T:(j + 1) * T], tile(n, 2 * g + k, 64 * j, 64 * j + NOPE),
                               hn[:, 4 + k, :], k == 0, k == 1, lin_ready if k == 1 and j == 1 else None)
                if g >= 1:
                    head_sums(HN["mla_k"] + g - 1, ones[0:QK, 0:QK], QK)
            values("mla_kv", "mla_v", hn[:, 4:6, :], 2)
            pe.wait_ge(lin_free, LIN["mla_v"] + 4)
            pe.wait_ge(hn_done, 16)
            attention(0, lambda i, q0, q1, k0, k1: (qT[0:QK, i, q0:q1], kT[0:QK, i, k0:k1]), False)
            pe.wait_ge(o_ready, 8)
            project("mla_o", "mla_o", (0, 4), oT, KD)

            norm_sums("ffn2_0", KD)
            normed("ffn2_0")
            gated("ffn2_0", FFC, 2)
            ple(0)

            norm_sums("ffn1_1", KD)
            normed("ffn1_1")
            gated("ffn1_1", FFC, 2)
            norm_sums("mix_1", KD)
            normed("mix_1")
            for c in range(2):
                for k in range(KD):
                    mm(B[3][:, c * H:(c + 1) * H], hn[:, k, c * P:(c + 1) * P],
                       params[:, COL["w_f"] + k * H:COL["w_f"] + (k + 1) * H], k == 0, k == KD - 1,
                       f_ready if k == KD - 1 and c == 1 else None)
            pe.wait_ge(logf_ready, 1)
            lf = [small[:, c * H:(c + 1) * H] for c in range(2)]
            mm(B[3][:, 0:H], upper[:], lf[0], True, True)
            mm(B[3][:, H:2 * H], ones[:], lf[0], True, False)
            mm(B[3][:, H:2 * H], upper[:], lf[1], False, True)
            mm(B[3][0:H, P:2 * P], lf[0], upper[:], True, True)
            mm(B[3][0:H, 2 * P:3 * P], lf[0], ones[:], True, False)
            mm(B[3][0:H, 2 * P:3 * P], lf[1], upper[:], False, True, dec_sum)
            pe.wait_ge(dec_ready, 1)
            tl = Tiles("fox_qk")
            for g in range(9):
                if g < 8:
                    bank = bank_free(LIN["fox_qk"] + g)
                    for j in range(2):
                        for k in range(KD):
                            mm(bank[:, j * T:(j + 1) * T], tl.next(), hn[:, k, :], k == 0, k == KD - 1,
                               lin_ready if k == KD - 1 and j == 1 else None)
                            tl.used()
                if g >= 1:
                    head_sums(HN["fox_qk"] + g - 1, ones64[:], P)
            tl.end()
            values("fox_v", "fox_v", hn, KD)
            pe.wait_ge(lin_free, LIN["fox_v"] + 4)

            def fox_qk(i, q0, q1, k0, k1):
                lo = 64 * (i % 2)
                return qT[lo:lo + 64, i // 2, q0:q1], kT[lo:lo + 64, i // 2, k0:k1]

            attention(H, fox_qk, True)
            pe.wait_ge(o_ready, 16)
            project("fox_o", "fox_o", (0, 4), oT, KD)
            norm_sums("ffn2_1", KD)
            normed("ffn2_1")
            gated("ffn2_1", FFC, 2)
            ple(1)

            norm_sums("mix2", KD)
            normed("mix2")
            for c in range(2):
                for k in range(KD):
                    mm(B[3][:, c * 8:(c + 1) * 8], hn[:, k, c * P:(c + 1) * P],
                       params[:, COL["w_ba"] + k * 8:COL["w_ba"] + (k + 1) * 8], k == 0, k == KD - 1,
                       ba_ready if k == KD - 1 and c == 1 else None)
            project("mix_in", "mix_in", (0, 14), hn, KD)
            pe.wait_ge(bg_ready, 1)
            for g in range(6):
                head_sums(HN["conv_a"] + g, ones64[:] if g < 2 else ones[:], P)
            pe.wait_ge(hn_rs, HN["dn_o"])
            beta, glog = small[:, 0:8], small[:, 8:16]
            for ch in range(8):
                mm(B[ch // 4][:, (ch % 4) * P:(ch % 4 + 1) * P], glog[:, ch:ch + 1].to_broadcast([P, P]), upper[:],
                   True, True)
            for ch in range(8):
                mm(B[2 + ch // 4][:, (ch % 4) * P:(ch % 4 + 1) * P], beta[:, ch:ch + 1].to_broadcast([P, P]),
                   ident[:], True, True)
            mm(B[4][:, 0:8], upper[:], glog, True, True)
            mm(B[4][:, 8:16], ones[:], glog, True, True, rows_ready)
            pe.wait_ge(dn_qk, 1)
            pe.wait_ge(gdiff, 1)
            for what in range(2):
                for ch in range(8):
                    c, hd = ch // 4, ch % 4
                    kc = qkv[:, 4 + hd, c * P:(c + 1) * P]
                    mm(B[4 + 2 * what + ch // 4][:, hd * P:(hd + 1) * P], kc,
                       kc if what == 0 else qkv[:, hd, c * P:(c + 1) * P], True, True,
                       dn_ready if ch == 7 else None)
            pe.wait_ge(gdecay, 1)
            pe.wait_ge(gdiff, 2)
            for ch in range(12):
                c, hd = (ch // 4, ch % 4) if ch < 8 else (0, ch % 4)
                src = qkv[:, (8 if ch < 8 else 4) + hd, c * P:(c + 1) * P]
                ins = nc.tensor.transpose(B[ch // 4][:, hd * P:(hd + 1) * P], src, ident[:])
            ins.then_inc(tok_ready, 1)
            pe.wait_ge(tok_scaled, 1)
            pe.wait_ge(inv_done, 1)
            for i in range(7):
                lw, x, xt, pm = DELTA["lw"], DELTA["x"], DELTA["xt"], DELTA["pm"]
                for ch in range(8):
                    mm(B[ch // 4][:, (ch % 4) * P:(ch % 4 + 1) * P], lw[:, ch, :], x[:, ch, :], True, True,
                       inv_p if ch == 7 else None)
                pe.wait_ge(inv_p_sb, i + 1)
                for what in range(0 if i < 6 else 1, 2):
                    for ch in range(8):
                        l, r = (xt, pm) if what == 0 else (pm, xt)
                        mm(B[4 + 2 * what + ch // 4][:, (ch % 4) * P:(ch % 4 + 1) * P], l[:, ch, :], r[:, ch, :],
                           True, True, inv_x if ch == 7 and what == 1 else None)
                pe.wait_ge(inv_done, i + 2)
            xt, vb, kd = DELTA["xt"], DELTA["vb"], DELTA["kd"]
            vn, state, intra, qd = DELTA["vn"], DELTA["state"], DELTA["intra"], DELTA["qd"]

            def four(bank, l, r, start=True, stop=True, inc=None):
                for hd in range(4):
                    mm(bank[:, hd * P:(hd + 1) * P], l(hd), r(hd), start and hd == 0, stop,
                       inc if hd == 3 else None)

            four(B[0], lambda d: xt[:, d, :], lambda d: vb[:, d, :], inc=dn_pe)
            pe.wait_ge(dn_sb, 1)
            four(B[2], lambda d: kd[:, d, :], lambda d: vn[:, d, :], inc=dn_pe)
            four(B[1], lambda d: vn[:, d, :], lambda d: intra[:, d, :], inc=dn_pe)
            pe.wait_ge(dn_sb, 2)
            four(B[3], lambda d: qkv[:, 4 + d, P:T], lambda d: state[:, d, :], inc=dn_pe)
            pe.wait_ge(dn_sb, 3)
            four(B[4], lambda d: xt[:, 4 + d, :], lambda d: vb[:, 4 + d, :], inc=dn_pe)
            pe.wait_ge(dn_sb, 4)
            four(B[5], lambda d: state[:, d, :], lambda d: qd[:, d, :], stop=False)
            four(B[5], lambda d: vn[:, 4 + d, :], lambda d: intra[:, 4 + d, :], start=False, inc=dn_pe)
            for g in range(2):
                head_sums(HN["dn_o"] + g, ones[:], P)
            pe.wait_ge(mix_ready, 1)
            project("mix_out", "mix_out", (0, 4), mixT, KD)

            norm_sums("ffn_2", KD)
            normed("ffn_2")
            for c in range(2):
                for k in range(KD):
                    mm(B[3][:, c * 36:(c + 1) * 36], hn[:, k, c * P:(c + 1) * P],
                       params[:, COL["w_router"] + k * 36:COL["w_router"] + (k + 1) * 36], k == 0, k == KD - 1,
                       rt_ready if k == KD - 1 and c == 1 else None)
            pe.wait_ge(rt_gate, 1)
            for e in range(NE):
                if e >= 4:
                    pe.wait_ge(rt_free, e // 2 - 1)
                for c in range(2):
                    mm(B[4 + (e // 2) % 2][:, (e % 2) * T + c * P:(e % 2) * T + (c + 1) * P],
                       route[:, c, 288 + e:289 + e].to_broadcast([P, P]), ident[:], True, True,
                       rt_rows if c == 1 and e % 2 == 1 else None)
            pe.wait_ge(rt_free, NE // 2)
            gated("moe", NE * EC, 4)
            norm_sums("final", KD)
            assert owed[0] <= 1


        @block.scalar
        def _(act_e):
            st = Steps(act_e, act_step)

            def norm(name, src, nk, dim, src_sem, src_count):
                n = NORM[name]
                act_e.wait_ge(src_sem, src_count)
                nc.scalar.activation(sq[:, 0:nk, :], src, ACT.Square).then_inc(norm_sq, 1)
                act_e.wait_ge(norm_sum, n + 1)
                st.link(nc.scalar.activation(lnv[:, n % 2, 0:T], B[2][:, 0:T], ACT.Ln, bias=eps_col[:, 0:1], scale=1.0 / dim))
                nc.scalar.activation(rstd[:, n % 2, :], lnv[:, n % 2, 0:T], ACT.Exp, scale=-0.5).then_inc(norm_rstd, 1)

            def residual_norm(name):
                norm(name, h[:], KD, D, h_ready, HREADY[name] - 1)

            def head_square(g, src, parts=P):
                nc.scalar.activation(sqh[0:parts, g % 2, :, :].rearrange("p a t -> p (a t)"), src,
                                     ACT.Square).then_inc(hn_sq, 1)

            def head_rstd(g, dim, done, count, parts=P):
                act_e.wait_ge(hn_sum, g + 1)
                if count > 0:
                    act_e.wait_ge(done, count)
                st.link(nc.scalar.activation(lnv[0:parts, g % 2, :], B[2 + g % 2][0:parts, :], ACT.Ln,
                                             bias=eps_col[0:parts, 0:1], scale=1.0 / dim))
                nc.scalar.activation(rsh[0:parts, g % 2, :], lnv[0:parts, g % 2, :], ACT.Exp, scale=-0.5).then_inc(hn_rs, 1)

            def gated(name, n_chunks):
                with act_e.Fori(0, n_chunks // 2) as r:
                    for j in range(2):
                        act_e.wait_ge(gu_ready, r * 2 + (GU[name] + j + 1))
                        nc.scalar.activation(expg[:, j, :], B[j][:, 0:T], ACT.Exp, scale=-1.0).then_inc(sig_ready, 1)

            def attention(first):
                for i in range(H + 1):
                    if i < H:
                        a = first + i
                        act_e.wait_ge(masked, a + 1)
                        if i >= 2:
                            act_e.wait_ge(turned, a - 1)
                        for b, (c0, c1) in enumerate(((0, P), (P, 3 * P))):
                            ins = nc.scalar.activation(probs[:, a % 2, c0:c1], logits[:, a % 2, c0:c1], ACT.Exp,
                                                       bias=nmax[:, a, b:b + 1], accum_out=psums[:, a, b:b + 1])
                        ins.then_inc(expd, 1)
                    if i >= 1:
                        a = first + i - 1
                        act_e.wait_ge(rcpd, a + 1)
                        for b, (c0, c1) in enumerate(((0, P), (P, 3 * P))):
                            ins = nc.scalar.activation(probs[:, a % 2, c0:c1], probs[:, a % 2, c0:c1], ACT.Copy,
                                                       scale=psums[:, a, b:b + 1])
                        ins.then_inc(prob_ready, 1)

            def ple(layer):
                name = f"ple_{layer}"
                residual_norm(name)
                for m in range(KD):
                    act_e.wait_ge(lin_ready, LIN[name] + m + 1)
                    if m >= 2:
                        act_e.wait_ge(lin_free, LIN[name] + m - 1)
                    nc.scalar.activation(expg[:, m % 2, :], OUTB[(LIN[name] + m) % 4][:, 0:T], ACT.Exp,
                                         scale=-1.0).then_inc(ple_e, 1)

            act_e.wait_ge(par_in, 16)
            act_e.wait_ge(consts, 1)
            act_e.wait_ge(rope_arg, 1)
            st.done(nc.scalar.activation(sinr[:], sinr[:], ACT.Sin))
            nc.scalar.activation(cosr[:], cosr[:], ACT.Sin).then_inc(rope_sin, 1)

            norm("ffn1_0", h[:], KD, D, x_in, 16)
            gated("ffn1_0", FFC)
            residual_norm("mix_0")
            norm("q_lat", cq, 4, QR, lin_free, LIN["mla_in"] + 2)
            norm("kv_lat", ckv, 2, KVR, lin_free, LIN["mla_in"] + 3)
            for g in range(9):
                if g < 8:
                    act_e.wait_ge(lin_ready, LIN["mla_q"] + g + 1)
                    head_square(g, OUTB[(LIN["mla_q"] + g) % 4][0:QK, :], QK)
                if g >= 1:
                    head_rstd(g - 1, QK, hn_done, g - 2, QK)
            for b in range(2):
                for j in range(2):
                    nc.scalar.activation(sqh[NOPE:QK, b, j, :], kpe[NOPE:QK, :], ACT.Square)
            for g in range(9):
                if g < 8:
                    act_e.wait_ge(lin_ready, LIN["mla_k"] + g + 1)
                    head_square(8 + g, OUTB[(LIN["mla_k"] + g) % 4][0:NOPE, :], NOPE)
                if g >= 1:
                    head_rstd(7 + g, QK, hn_done, 8 + g - 2, QK)
            attention(0)
            residual_norm("ffn2_0")
            gated("ffn2_0", FFC)
            ple(0)

            residual_norm("ffn1_1")
            gated("ffn1_1", FFC)
            residual_norm("mix_1")
            act_e.wait_ge(f_abs, 1)
            st.link(nc.scalar.activation(small[:, 96:128], small[:, 64:96], ACT.Exp, scale=-1.0))
            nc.scalar.activation(small[:, 128:160], small[:, 96:128], ACT.Ln, bias=ones[:, 0:1]).then_inc(f_ln, 1)
            for g in range(9):
                if g < 8:
                    act_e.wait_ge(lin_ready, LIN["fox_qk"] + g + 1)
                    head_square(16 + g, OUTB[(LIN["fox_qk"] + g) % 4][:, :])
                if g >= 1:
                    head_rstd(15 + g, 64, lin_free, LIN["fox_qk"] + g - 2)
            attention(H)
            residual_norm("ffn2_1")
            gated("ffn2_1", FFC)
            ple(1)

            residual_norm("mix2")
            act_e.wait_ge(ba_abs, 1)
            st.done(nc.scalar.activation(small[:, 64:72], small[:, 32:40], ACT.Exp, scale=-1.0))
            st.done(nc.scalar.activation(small[:, 88:92], col("a_log", 0, 4), ACT.Exp))
            st.link(nc.scalar.activation(small[:, 72:80], small[:, 48:56], ACT.Exp, scale=-1.0))
            nc.scalar.activation(small[:, 80:88], small[:, 72:80], ACT.Ln, bias=ones[:, 0:1]).then_inc(ba_ln, 1)
            for g in range(14):
                act_e.wait_ge(lin_ready, LIN["mix_in"] + g + 1)
                bank = OUTB[(LIN["mix_in"] + g) % 4][:, :].rearrange("p (a t) -> p a t", t=T)
                if g < 2:
                    dst = a_h[:, 2 * g:2 * g + 2, :]
                elif g < 4:
                    dst = convt[:, 2 * (g - 2):2 * (g - 2) + 2, :]
                elif g < 6:
                    dst = a_b[:, 2 * (g - 4):2 * (g - 4) + 2, :]
                elif g < 12:
                    dst = qkv_pad[:, 2 * (g - 6):2 * (g - 6) + 2, 3:PADQ]
                else:
                    dst = z_gate[:, 2 * (g - 12):2 * (g - 12) + 2, :]
                nc.scalar.activation(dst, bank, ACT.Copy).then_inc(lin_free, 1)
            act_e.wait_ge(lin_free, LIN["mix_in"] + 14)
            nc.scalar.activation(pin[:], z_gate, ACT.Exp, scale=-1.0).then_inc(z_exp, 1)
            act_e.wait_ge(hn_src, 1)
            for g in range(3):
                if g < 2:
                    head_square(24 + g, y_a[:, 2 * g:2 * g + 2, :].rearrange("p a t -> p (a t)"))
                if g >= 1:
                    head_rstd(23 + g, 64, hn_done, 15 + g - 1)
            for part in range(3):
                act_e.wait_ge(silu_in, part + 1)
                nc.scalar.activation(silu_tmp[part], qkv[:, 4 * part:4 * part + 4, :], ACT.Exp,
                                     scale=-1.0).then_inc(silu_e, 1)
            for g in range(5):
                if g < 4:
                    act_e.wait_ge(hn_src, 2 + g // 2)
                    head_square(26 + g, qkv[:, 2 * g:2 * g + 2, :].rearrange("p a t -> p (a t)"))
                if g >= 1:
                    head_rstd(25 + g, 1, hn_done, 17 + g - 1)
            act_e.wait_ge(gdiff, 1)
            st.done(nc.scalar.activation(DELTA["decay"], DELTA["decay"], ACT.Exp))
            st.done(nc.scalar.activation(DELTA["egrow"].rearrange("p c t -> p (c t)"), B[1][:, :], ACT.Exp))
            nc.scalar.activation(small[:, 144:160], small[:, 128:144], ACT.Exp).then_inc(gdecay, 1)
            for i in range(7):
                act_e.wait_ge(inv_p, i + 1)
                pm = DELTA["pm"].rearrange("p c t -> p (c t)")
                nc.scalar.activation(pm[:, 0:512], B[0][:, :], ACT.Copy)
                nc.scalar.activation(pm[:, 512:1024], B[1][:, :], ACT.Copy).then_inc(inv_p_sb, 1)
            act_e.wait_ge(hn_src, 4)
            for g in range(3):
                if g < 2:
                    head_square(30 + g, convt[:, 2 * g:2 * g + 2, :].rearrange("p a t -> p (a t)"))
                if g >= 1:
                    head_rstd(29 + g, 128, hn_done, 21 + g - 1)

            residual_norm("ffn_2")
            for i in range(2):
                act_e.wait_ge(rt_max, i + 1)
                c0, n, d0 = ((40, 4, 44), (200, 1, 201))[i]
                nc.scalar.activation(route[:, :, d0:d0 + n], route[:, :, c0:c0 + n], ACT.Exp).then_inc(rt_exp, 1)
            gated("moe", NE * EC)
            residual_norm("final")

        @block.vector
        def _(dve):
            st = Steps(dve, dve_step)
            V = nc.vector

            def norm_apply(name, src, nk, gain, dst):
                n = NORM[name]
                dve.wait_ge(norm_rstd, n + 1)
                for k in range(nk):
                    ins = V.scalar_tensor_tensor(out=dst[:, k, :], in0=src[:, k, :], scalar=col(gain, k),
                                                 in1=rstd[:, n % 2, :], op0=ALU.mult, op1=ALU.mult)
                ins.then_inc(norm_out, 1)

            def add_residual(bank, i, scale, inc):
                hh = h[:, 2 * i:2 * i + 2, :].rearrange("p a t -> p (a t)")
                ins = V.scalar_tensor_tensor(out=hh, in0=bank[:, :], scalar=scale, in1=hh, op0=ALU.mult, op1=ALU.add)
                if inc is not None:
                    ins.then_inc(inc, 1)
                return ins

            def gated(name, n_chunks, scale, moe=False):
                per = 4 if moe else 3
                unroll = EC if moe else 2
                step0 = 3 * GU[name]
                with dve.Fori(0, n_chunks // unroll) as r:
                    for j in range(unroll):
                        b = j % 2
                        g, u = B[b][:, 0:T], B[b][:, T:2 * T]
                        e, s, a = expg[:, b, :], gate_r[:, b, :], act[:, b, :]
                        dve.wait_ge(sig_ready, r * unroll + (GU[name] + j + 1))
                        at = step0 + per * j

                        def settled(k):
                            dve.wait_ge(glu_step, r * (per * unroll) + (at + k))

                        V.tensor_scalar_add(e, e, 1.0).then_inc(glu_step, 1)
                        settled(1)
                        V.reciprocal(s, e).then_inc(glu_step, 1)
                        settled(2)
                        V.tensor_tensor(s, g, s, ALU.mult).then_inc(glu_step, 1)
                        settled(3)
                        if moe:
                            V.tensor_tensor(s, u, s, ALU.mult).then_inc(glu_step, 1)
                            settled(4)
                            V.tensor_tensor(a, s, gate_rows[:, bass.ds(r * T, T)], ALU.mult).then_inc(act_ready, 1)
                        else:
                            V.tensor_tensor(a, u, s, ALU.mult).then_inc(act_ready, 1)
                dve.wait_ge(acc_ready, 1 + list(GU).index(name))
                for i in range(4):
                    add_residual(OUTB[i], i, scale, h_ready if i == 3 else None)

            def attention(first, fox):
                for i in range(H + 4):
                    if i < H:
                        a = first + i
                        dve.wait_ge(scores, a + 1)
                        s = B[a % 2]
                        lg = logits[:, a % 2, :]
                        if fox:
                            st.done(V.scalar_tensor_tensor(out=lg[:, 0:P], in0=s[:, 0:P], scalar=dtok[:, 0, i:i + 1],
                                                           in1=mask[:, 0:P], op0=ALU.add, op1=ALU.add))
                            st.link(V.scalar_tensor_tensor(out=lg[:, P:3 * P], in0=s[:, P:3 * P],
                                                           scalar=dtok[:, 1, i:i + 1], in1=mask[:, P:3 * P],
                                                           op0=ALU.add, op1=ALU.add))
                        else:
                            st.link(V.tensor_tensor(lg, s[:, 0:3 * P], mask[:], ALU.add))
                        st.done(V.tensor_reduce(nmax[:, a, 0:1], lg[:, 0:P], AXX, ALU.max))
                        st.link(V.tensor_reduce(nmax[:, a, 1:2], lg[:, P:3 * P], AXX, ALU.max))
                        V.tensor_scalar(nmax[:, a, :], nmax[:, a, :], -1.0, None, ALU.mult).then_inc(masked, 1)
                    if 1 <= i <= H:
                        a = first + i - 1
                        dve.wait_ge(expd, a + 1)
                        V.reciprocal(psums[:, a, :], psums[:, a, :]).then_inc(rcpd, 1)
                    if 2 <= i <= H + 1:
                        a = first + i - 2
                        dve.wait_ge(turned, a + 1)
                        V.tensor_copy(pT_sb[:, a % 2, :], B[2 + a % 2][:, 0:3 * P]).then_inc(pt_ready, 1)
                    if i >= 4 and i % 2 == 0:
                        pair = (first + i - 4) // 2
                        dve.wait_ge(pv_done, 2 * pair + 2)
                        V.tensor_copy(oT[:, (i - 4) // 2, :], B[4 + pair % 2][:, 0:T]).then_inc(o_ready, 1)

            def out_product(lin):
                for g in range(4):
                    dve.wait_ge(lin_ready, LIN[lin] + g + 1)
                    add_residual(OUTB[(LIN[lin] + g) % 4], g, 1.0, lin_free)
                dve.wait_ge(lin_free, LIN[lin] + 4)
                dve.sem_inc(h_ready, 1)

            def ple(layer):
                name = f"ple_{layer}"
                norm_apply(name, h, KD, f"g_ple_{layer}", hn)
                for m in range(KD):
                    bank = OUTB[(LIN[name] + m) % 4]
                    b = m % 2
                    dve.wait_ge(ple_e, KD * layer + m + 1)
                    st.link(V.tensor_scalar_add(expg[:, b, :], expg[:, b, :], 1.0))
                    st.link(V.reciprocal(gate_r[:, b, :], expg[:, b, :]))
                    V.tensor_tensor(act[:, b, :], bank[:, T:2 * T], gate_r[:, b, :], ALU.mult).then_inc(lin_free, 1)
                    dve.wait_ge(lin_free, LIN[name] + m + 1)
                    ins = V.tensor_tensor(h[:, m, :], h[:, m, :], act[:, b, :], ALU.add)
                ins.then_inc(h_ready, 1)

            def rotate(x, n):
                lo, hi = NOPE, QK
                xr = x.rearrange("p a t -> p (a t)")
                half = ROPE // 2
                turn = [(i + half) % ROPE for i in range(ROPE)]
                a = rope_t[lo:hi, 0, 0:n * T]
                b = rope_t[lo:hi, 1, 0:n * T]
                st.link(V.stream_shuffle(a, xr, turn))
                a3, b3 = (t.rearrange("p (a t) -> p a t", t=T) for t in (a, b))
                st.done(V.tensor_tensor(a3, a3, rep(sinr[lo:hi, :], n), ALU.mult))
                st.link(V.tensor_tensor(b3, x, rep(cosr[lo:hi, :], n), ALU.mult))
                st.link(V.tensor_tensor(x, a3, b3, ALU.add))

            dve.wait_ge(par_in, 16)
            dve.wait_ge(pos_in, 16)
            dve.wait_ge(consts, 1)
            ang, turns = rope_t[:, 0, 0:T], rope_t[:, 1, 0:T]
            st.link(V.tensor_copy(ang, posi))
            st.link(V.tensor_scalar(ang, ang, col("inv_freq"), None, ALU.mult))
            st.link(V.tensor_scalar(turns, ang, 1.0 / TWO_PI, None, ALU.mult))
            st.link(V.tensor_scalar_add(turns, turns, ROUND))
            st.link(V.tensor_scalar_add(turns, turns, -ROUND))
            for part in (PI2_A, PI2_B, PI2_C):
                st.link(V.scalar_tensor_tensor(out=ang, in0=turns, scalar=-part, in1=ang, op0=ALU.mult, op1=ALU.add))
            st.link(V.tensor_scalar(ang, ang, 3.1415925, -3.1415925, ALU.min, ALU.max))
            st.done(V.tensor_copy(sinr[:], ang))
            V.tensor_scalar(cosr[:], ang, 0.5, None, ALU.mult).then_inc(rope_arg, 1)
            st.done(V.tensor_scalar(gq[:, 0:1], col("mla_qn"), float(QK) ** -0.5, None, ALU.mult))
            st.done(V.tensor_scalar(gq[:, 1:2], col("fox_qn"), 0.125, None, ALU.mult))
            dve.wait_ge(rope_sin, 1)
            st.done(V.tensor_scalar(sinr[:], sinr[:], col("rope_sign"), None, ALU.mult))
            st.link(V.tensor_tensor(cosr[:], cosr[:], cosr[:], ALU.mult))
            st.link(V.tensor_scalar(cosr[:], cosr[:], -2.0, 1.0, ALU.mult, ALU.add))

            dve.wait_ge(x_in, 16)
            norm_apply("ffn1_0", h, KD, "g_ffn1_0", hn)
            gated("ffn1_0", FFC, 0.5)
            norm_apply("mix_0", h, KD, "g_mix_0", hn)
            L0 = LIN["mla_in"]
            for g in range(4):
                dve.wait_ge(lin_ready, L0 + g + 1)
                bank = OUTB[(L0 + g) % 4]
                if g < 3:
                    dst = (cq[:, 0:2, :], cq[:, 2:4, :], ckv)[g].rearrange("p a t -> p (a t)")
                    V.tensor_copy(dst, bank[:, :]).then_inc(lin_free, 1)
                else:
                    V.tensor_copy(kpe[:], bank[:, 0:T]).then_inc(lin_free, 1)
            norm_apply("q_lat", cq, 4, "g_q_lat", hn)
            norm_apply("kv_lat", ckv, 2, "g_kv_lat", hn[:, 4:6, :])
            dve.wait_ge(lin_free, L0 + 4)
            st.link(V.tensor_scalar(kr[NOPE:QK, :], kpe[NOPE:QK, :], col("mla_kn")[NOPE:QK], None, ALU.mult))
            rotate(kr[NOPE:QK, :].rearrange("p (a t) -> p a t", a=1), 1)
            for g in range(8):
                bank = OUTB[(LIN["mla_q"] + g) % 4]
                q2 = qT[0:QK, 2 * g:2 * g + 2, :].rearrange("p a t -> p (a t)")
                dve.wait_ge(hn_rs, HN["mla_q"] + g + 1)
                V.scalar_tensor_tensor(out=q2, in0=bank[0:QK, :], scalar=gq[0:QK, 0:1], in1=rsh[0:QK, g % 2, :],
                                       op0=ALU.mult, op1=ALU.mult).then_inc(lin_free, 1)
                dve.wait_ge(lin_free, LIN["mla_q"] + g + 1)
                rotate(qT[NOPE:QK, 2 * g:2 * g + 2, :], 2)
                dve.sem_inc(hn_done, 1)
            for g in range(8):
                bank = OUTB[(LIN["mla_k"] + g) % 4]
                gi = HN["mla_k"] + g
                dve.wait_ge(hn_rs, gi + 1)
                V.scalar_tensor_tensor(out=kT[0:NOPE, 2 * g:2 * g + 2, :].rearrange("p a t -> p (a t)"),
                                       in0=bank[0:NOPE, :], scalar=col("mla_kn")[0:NOPE], in1=rsh[0:NOPE, gi % 2, :],
                                       op0=ALU.mult, op1=ALU.mult).then_inc(lin_free, 1)
                V.tensor_tensor(kT[NOPE:QK, 2 * g:2 * g + 2, :], rep(kr[NOPE:QK, :], 2),
                                rsh[NOPE:QK, gi % 2, :].rearrange("p (a t) -> p a t", t=T), ALU.mult).then_inc(hn_done, 1)

            def copy_values(lin):
                for g in range(4):
                    dve.wait_ge(lin_ready, LIN[lin] + g + 1)
                    half, c = g // 2, g % 2
                    V.tensor_copy(v_tok[:, c, half * 512:(half + 1) * 512],
                                  OUTB[(LIN[lin] + g) % 4][:, :]).then_inc(lin_free, 1)

            copy_values("mla_v")
            attention(0, False)
            out_product("mla_o")
            norm_apply("ffn2_0", h, KD, "g_ffn2_0", hn)
            gated("ffn2_0", FFC, 0.5)
            ple(0)

            norm_apply("ffn1_1", h, KD, "g_ffn1_1", hn)
            gated("ffn1_1", FFC, 0.5)
            norm_apply("mix_1", h, KD, "g_mix_1", hn)
            dve.wait_ge(f_ready, 1)
            zf = small[:, 32:64]
            st.link(V.tensor_tensor(zf.rearrange("p (c n) -> p c n", n=H),
                                    B[3][:, 0:2 * H].rearrange("p (c n) -> p c n", n=H),
                                    rep(col("b_f", 0, H), 2), ALU.add))
            V.scalar_tensor_tensor(out=small[:, 64:96], in0=zf, scalar=-1.0, in1=zf, op0=ALU.mult,
                                   op1=ALU.max).then_inc(f_abs, 1)
            dve.wait_ge(f_ln, 1)
            V.scalar_tensor_tensor(out=small[:, 0:32], in0=zf, scalar=0.0, in1=small[:, 128:160], op0=ALU.min,
                                   op1=ALU.subtract).then_inc(logf_ready, 1)
            dve.wait_ge(dec_sum, 1)
            V.tensor_copy(dtok[:, :, :].rearrange("p c n -> p (c n)"), B[3][:, 0:2 * H])
            V.tensor_scalar(ndec[:], B[3][0:H, P:3 * P], -1.0, None, ALU.mult).then_inc(dec_ready, 1)
            for g in range(8):
                bank = OUTB[(LIN["fox_qk"] + g) % 4]
                gi = HN["fox_qk"] + g
                dst = (qT if g < 4 else kT)[:, 2 * (g % 4):2 * (g % 4) + 2, :].rearrange("p a t -> p (a t)")
                dve.wait_ge(hn_rs, gi + 1)
                V.scalar_tensor_tensor(out=dst, in0=bank[:, :], scalar=gq[:, 1:2] if g < 4 else col("fox_kn"),
                                       in1=rsh[:, gi % 2, :], op0=ALU.mult, op1=ALU.mult).then_inc(lin_free, 1)
            copy_values("fox_v")
            attention(H, True)
            out_product("fox_o")
            norm_apply("ffn2_1", h, KD, "g_ffn2_1", hn)
            gated("ffn2_1", FFC, 0.5)
            ple(1)

            norm_apply("mix2", h, KD, "g_mix2", hn)
            dve.wait_ge(ba_ready, 1)
            ba = B[3][:, 0:16].rearrange("p (c n) -> p c n", n=8)

            def s3(lo):
                return small[:, lo:lo + 8].rearrange("p (c n) -> p c n", n=4)

            st.done(V.tensor_copy(s3(32), ba[:, :, 0:4]))
            st.link(V.tensor_tensor(s3(40), ba[:, :, 4:8], rep(col("dt_bias", 0, 4), 2), ALU.add))
            V.scalar_tensor_tensor(out=small[:, 48:56], in0=small[:, 40:48], scalar=-1.0, in1=small[:, 40:48], op0=ALU.mult,
                                   op1=ALU.max).then_inc(ba_abs, 1)
            dve.wait_ge(ba_ln, 1)
            st.done(V.tensor_scalar_add(small[:, 64:72], small[:, 64:72], 1.0))
            st.link(V.scalar_tensor_tensor(out=small[:, 56:64], in0=small[:, 40:48], scalar=0.0, in1=small[:, 80:88],
                                           op0=ALU.max, op1=ALU.add))
            st.done(V.reciprocal(small[:, 0:8], small[:, 64:72]))
            st.link(V.tensor_tensor(s3(8), s3(56), rep(small[:, 88:92], 2), ALU.mult))
            V.tensor_scalar(small[:, 8:16], small[:, 8:16], -1.0, None, ALU.mult).then_inc(bg_ready, 1)
            L = LIN["mix_in"]
            dve.wait_ge(lin_free, L + 4)
            st.link(V.tensor_tensor(u_pad[:, :, 2:PADU], convt, a_h, ALU.mult))
            for n in range(4):
                st.done(V.tensor_scalar(y_a[:, n, :], u_pad[:, n, 0:T], col("conv_a_w", n), None, ALU.mult))
            for tap in range(1, 3):
                st.settled()
                for n in range(4):
                    st.done(V.scalar_tensor_tensor(out=y_a[:, n, :], in0=u_pad[:, n, tap:tap + T],
                                                   scalar=col("conv_a_w", 4 * tap + n), in1=y_a[:, n, :],
                                                   op0=ALU.mult, op1=ALU.add))
            st.settled()
            dve.wait_ge(lin_free, L + 6)
            V.tensor_tensor(y_a, y_a, a_b, ALU.mult).then_inc(hn_src, 1)
            for part in range(3):
                dve.wait_ge(lin_free, L + 6 + 2 * (part + 1))
                tiles = range(4 * part, 4 * part + 4)
                for n in tiles:
                    st.done(V.tensor_scalar(qkv[:, n, :], qkv_pad[:, n, 0:T], col("dn_conv_w", n), None, ALU.mult))
                for tap in range(1, 4):
                    st.settled()
                    for n in tiles:
                        ins = V.scalar_tensor_tensor(out=qkv[:, n, :], in0=qkv_pad[:, n, tap:tap + T],
                                                     scalar=col("dn_conv_w", 12 * tap + n), in1=qkv[:, n, :],
                                                     op0=ALU.mult, op1=ALU.add)
                        if tap == 3 and n == tiles[-1]:
                            ins.then_inc(silu_in, 1)
                        else:
                            st.done(ins)
            for part in range(3):
                x, e = qkv[:, 4 * part:4 * part + 4, :], silu_tmp[part]
                dve.wait_ge(silu_e, part + 1)
                st.link(V.tensor_scalar_add(e, e, 1.0))
                st.link(V.reciprocal(e, e))
                if part < 2:
                    V.tensor_tensor(x, x, e, ALU.mult).then_inc(hn_src, 1)
                else:
                    st.link(V.tensor_tensor(x, x, e, ALU.mult))
            dve.wait_ge(z_exp, 1)
            st.link(V.tensor_scalar_add(pin[:], pin[:], 1.0))
            st.link(V.reciprocal(pin[:], pin[:]))
            st.link(V.tensor_tensor(z_gate, z_gate, pin[:], ALU.mult))

            def flat(x):
                return x.rearrange("p a t -> p (a t)")

            for g in range(2):
                dve.wait_ge(hn_rs, 24 + g + 1)
                for j in range(2):
                    n = 2 * g + j
                    ins = V.scalar_tensor_tensor(out=mixT[:, n, :], in0=y_a[:, n, :], scalar=col("conv_a_g", n),
                                                 in1=rsh[:, g % 2, j * T:(j + 1) * T], op0=ALU.mult, op1=ALU.mult)
                ins.then_inc(hn_done, 1)
            for g in range(4):
                dve.wait_ge(hn_rs, 26 + g + 1)
                x = flat(qkv[:, 2 * g:2 * g + 2, :])
                V.scalar_tensor_tensor(out=x, in0=x, scalar=128.0 ** -0.5 if g < 2 else 1.0, in1=rsh[:, g % 2, :],
                                       op0=ALU.mult, op1=ALU.mult).then_inc(hn_done, 1)
            dve.wait_ge(hn_done, 22)
            dve.sem_inc(dn_qk, 1)
            decay, brow, lt, intra = DELTA["decay"], DELTA["brow"], DELTA["lt"], DELTA["intra"]
            dve.wait_ge(rows_ready, 1)
            st.link(V.tensor_copy(small[:, 128:136], B[4][:, 0:8]))
            for ch in range(8):
                st.done(V.tensor_scalar(decay[:, ch, :], B[ch // 4][:, (ch % 4) * P:(ch % 4 + 1) * P],
                                        small[:, 128 + ch:129 + ch], 0.0, ALU.subtract, ALU.min))
            V.tensor_tensor(small[:, 136:144], B[4][:, 8:16], small[:, 128:136], ALU.subtract).then_inc(gdiff, 1)
            bf = flat(brow)
            st.done(V.tensor_copy(bf[:, 0:512], B[2][:, :]))
            V.tensor_copy(bf[:, 512:1024], B[3][:, :]).then_inc(gdiff, 1)
            dve.wait_ge(gdecay, 1)
            st.link(V.tensor_tensor(decay, decay, rep(upper[:], 8), ALU.mult))
            st.done(V.tensor_tensor(DELTA["qd"], qkv[:, 0:4, P:T], DELTA["egrow"], ALU.mult))
            st.done(V.scalar_tensor_tensor(out=small[:, 160:168], in0=small[:, 0:8], scalar=-1.0,
                                           in1=small[:, 144:152], op0=ALU.mult, op1=ALU.mult))
            dve.wait_ge(dn_ready, 1)
            for b in range(2):
                st.done(V.tensor_tensor(flat(lt)[:, b * 512:(b + 1) * 512], B[4 + b][:, :],
                                        flat(decay)[:, b * 512:(b + 1) * 512], ALU.mult))
            dve.wait_ge(dn_ready, 2)
            for b in range(2):
                st.done(V.tensor_tensor(flat(intra)[:, b * 512:(b + 1) * 512], B[6 + b][:, :],
                                        flat(decay)[:, b * 512:(b + 1) * 512], ALU.mult))
            st.settled()
            st.link(V.tensor_tensor(lt, lt, brow, ALU.mult))
            vb, kd = DELTA["vb"], DELTA["kd"]
            dve.wait_ge(tok_ready, 1)
            for ch in range(8):
                st.done(V.tensor_scalar(vb[:, ch, :], B[ch // 4][:, (ch % 4) * P:(ch % 4 + 1) * P],
                                        small[:, ch:ch + 1], None, ALU.mult))
            for hd in range(4):
                ins = V.tensor_scalar(kd[:, hd, :], B[2][:, hd * P:(hd + 1) * P], small[:, 152 + hd:153 + hd], None,
                                      ALU.mult)
            ins.then_inc(tok_scaled, 1)
            x, xt, lw = DELTA["x"], DELTA["xt"], DELTA["lw"]
            st.done(V.tensor_copy(x, rep(ident[:], 8)))
            st.done(V.tensor_copy(xt, rep(ident[:], 8)))
            V.tensor_tensor(lw, lt, rep(level[:, 0, :], 8), ALU.mult).then_inc(inv_done, 1)
            st.settled()
            for i in range(7):
                if i < 6:
                    dve.wait_ge(inv_p, i + 1)
                    st.done(V.tensor_tensor(lw, lt, rep(level[:, i + 1, :], 8), ALU.mult))
                dve.wait_ge(inv_x, i + 1)
                if i < 6:
                    for b in range(2):
                        xb = flat(x)[:, b * 512:(b + 1) * 512]
                        st.done(V.tensor_tensor(xb, xb, B[4 + b][:, :], ALU.subtract))
                for b in range(2):
                    xb = flat(xt)[:, b * 512:(b + 1) * 512]
                    ins = V.tensor_tensor(xb, xb, B[6 + b][:, :], ALU.subtract)
                    if b == 1:
                        ins.then_inc(inv_done, 1)
                    else:
                        st.done(ins)
                st.settled()
                dve.wait_ge(inv_done, i + 2)
            vn, state = DELTA["vn"], DELTA["state"]
            dve.wait_ge(dn_pe, 1)
            V.tensor_copy(flat(vn)[:, 0:512], B[0][:, :]).then_inc(dn_sb, 1)
            dve.wait_ge(dn_pe, 2)
            V.tensor_copy(flat(state), B[2][:, :]).then_inc(dn_sb, 1)
            dve.wait_ge(dn_pe, 3)
            st.done(V.tensor_copy(convt[:, :, 0:P], B[1][:, :].rearrange("p (a t) -> p a t", t=P)))
            dve.wait_ge(dn_pe, 4)
            for hd in range(4):
                ins = V.scalar_tensor_tensor(out=vb[:, 4 + hd, :], in0=B[3][:, hd * P:(hd + 1) * P],
                                             scalar=small[:, 164 + hd:165 + hd], in1=vb[:, 4 + hd, :], op0=ALU.mult,
                                             op1=ALU.add)
            ins.then_inc(dn_sb, 1)
            dve.wait_ge(dn_pe, 5)
            V.tensor_copy(flat(vn)[:, 512:1024], B[4][:, :]).then_inc(dn_sb, 1)
            dve.wait_ge(dn_pe, 6)
            V.tensor_copy(convt[:, :, P:T], B[5][:, :].rearrange("p (a t) -> p a t", t=P)).then_inc(hn_src, 1)
            for g in range(2):
                dve.wait_ge(hn_rs, 30 + g + 1)
                y = flat(mixT[:, 4 + 2 * g:6 + 2 * g, :])
                V.scalar_tensor_tensor(out=y, in0=flat(convt[:, 2 * g:2 * g + 2, :]), scalar=col("dn_g"),
                                       in1=rsh[:, g % 2, :], op0=ALU.mult, op1=ALU.mult).then_inc(hn_done, 1)
                dve.wait_ge(hn_done, 22 + g + 1)
                ins = V.tensor_tensor(y, y, flat(z_gate[:, 2 * g:2 * g + 2, :]), ALU.mult)
            ins.then_inc(mix_ready, 1)
            out_product("mix_out")

            norm_apply("ffn_2", h, KD, "g_ffn_2", hn)
            dve.wait_ge(rt_ready, 1)

            def R(lo, n):
                return route[:, :, lo:lo + n]

            def wide(lo, n):
                return R(lo, 1).to_broadcast([P, 2, n])

            def both(x):
                return x.rearrange("p (a t) -> p a t", a=1).to_broadcast([P, 2, x.shape[1]])

            def first_best(x, n, best, tmp, hot):
                st.link(V.tensor_reduce(R(best, 1), R(x, n), AXX, ALU.max))
                st.link(V.tensor_tensor(R(tmp, n), R(x, n), wide(best, n), ALU.is_equal))
                st.link(V.tensor_tensor(R(tmp, n), R(tmp, n), both(col("first_wins", 0, n)), ALU.mult))
                st.link(V.tensor_reduce(R(best + 1, 1), R(tmp, n), AXX, ALU.max))
                st.link(V.tensor_tensor(R(hot, n), R(tmp, n), wide(best + 1, n), ALU.is_equal))

            st.link(V.tensor_copy(R(0, 36), B[3][:, 0:72].rearrange("p (c n) -> p c n", n=36)))
            first_best(0, 4, 36, 40, 48)
            V.tensor_tensor(R(40, 4), R(0, 4), wide(36, 4), ALU.subtract).then_inc(rt_max, 1)
            st.link(V.tensor_scalar(R(52, 4), R(48, 4), -1.0, -NEG, ALU.add, ALU.mult))
            for c in range(2):
                g3 = [route[:, c, lo:lo + 4].rearrange("p (g a) -> p g a", a=1).to_broadcast([P, NG, EPG])
                      for lo in (48, 52)]
                el = route[:, c, 4:36].rearrange("p (g e) -> p g e", e=EPG)
                ml = route[:, c, 64:96].rearrange("p (g e) -> p g e", e=EPG)
                st.link(V.tensor_tensor(ml, el, g3[0], ALU.mult))
                st.link(V.tensor_tensor(ml, ml, g3[1], ALU.add))
            first_best(64, 32, 192, 96, 128)
            st.link(V.scalar_tensor_tensor(out=R(224, 32), in0=R(128, 32), scalar=2.0 * NEG, in1=R(64, 32),
                                           op0=ALU.mult, op1=ALU.add))
            first_best(224, 32, 194, 96, 160)
            V.tensor_tensor(R(200, 1), R(194, 1), R(192, 1), ALU.subtract).then_inc(rt_max, 1)
            dve.wait_ge(rt_exp, 2)
            st.link(V.tensor_reduce(R(202, 1), R(44, 4), AXX, ALU.add))
            st.link(V.tensor_scalar_add(R(203, 1), R(201, 1), 1.0))
            st.link(V.tensor_tensor(R(202, 1), R(202, 1), R(203, 1), ALU.mult))
            st.link(V.reciprocal(R(204, 1), R(202, 1)))
            st.link(V.tensor_tensor(R(205, 1), R(204, 1), R(201, 1), ALU.mult))
            st.done(V.tensor_tensor(R(128, 32), R(128, 32), wide(204, 32), ALU.mult))
            st.link(V.tensor_tensor(R(160, 32), R(160, 32), wide(205, 32), ALU.mult))
            V.tensor_tensor(R(288, 32), R(128, 32), R(160, 32), ALU.add).then_inc(rt_gate, 1)
            for i in range(NE // 2):
                dve.wait_ge(rt_rows, i + 1)
                V.tensor_copy(gate_rows[:, i * 512:(i + 1) * 512], B[4 + i % 2][:, :]).then_inc(rt_free, 1)
            dve.wait_ge(rt_free, NE // 2)
            gated("moe", NE * EC, 1.0, moe=True)
            norm_apply("final", h, KD, "g_final", hn)


def _tiles(w):
    k, m = w.shape
    return w.reshape(k // P, P, m // P, P).transpose(2, 0, 1, 3).reshape(-1, P, P)


def _chunks(tiles):
    n = len(tiles)
    c = chunks_of(n)
    if c * CT > n:
        tiles = np.concatenate([tiles, np.zeros((c * CT - n, P, P), tiles.dtype)])
    return np.ascontiguousarray(tiles.reshape(c, CT, P, P).transpose(0, 2, 1, 3)).reshape(c, P, CT * P)


def _widen(w, width):
    k = w.shape[0]
    w = w.reshape(k, -1, width)
    return np.concatenate([w, np.zeros((k, w.shape[1], P - width), w.dtype)], axis=2).reshape(k, -1)


def _gated(w_gate, w_up, w_down, n):
    gate, up = _tiles(w_gate).reshape(n, KD, P, P), _tiles(w_up).reshape(n, KD, P, P)
    down = w_down.reshape(n, P, KD, P).transpose(0, 2, 1, 3)
    return _chunks(np.concatenate([gate, up, down], axis=1).reshape(-1, P, P))


def _wide(w):
    k = w.shape[0]
    return w.reshape(k // P, P, 2, 4, P).transpose(2, 0, 3, 1, 4).reshape(-1, P, P)


def kernel(**inputs):
    import concourse.bacc as bacc
    from concourse.bass_utils import run_bass_kernel_spmd

    a = {k: np.asarray(v) for k, v in inputs.items()}

    def ffn(which, layer):
        w = a[f"{which}_w_in"][layer]
        return _gated(w[:, :FF], w[:, FF:], a[f"{which}_w_out"][layer], FFC)

    def ple(layer):
        gate = _tiles(a["ple_w_gate"][layer]).reshape(KD, KD, P, P)
        proj = _tiles(a["ple_w_proj"][layer]).reshape(KD, 2, P, P)
        return _chunks(np.concatenate([gate, proj], axis=1).reshape(-1, P, P))

    w = a["mla_w_in"][0]
    k_pe = np.concatenate([np.zeros((D, NOPE), w.dtype), w[:, QR + KVR:], np.zeros((D, P - QK), w.dtype)], axis=1)
    mla_in = _chunks(_tiles(np.concatenate([w[:, :QR + KVR], k_pe], axis=1)))
    mla_q = _chunks(_tiles(_widen(a["mla_w_uq"][0], QK)))
    ukv = a["mla_w_ukv"][0].reshape(KVR, H, NOPE + DV)
    mla_kv = _chunks(np.concatenate([_tiles(ukv[:, :, :NOPE].reshape(KVR, -1)), _wide(ukv[:, :, NOPE:].reshape(KVR, -1))]))
    fox = a["fox_w_in"][0]
    w2 = a["w_in_2"][0]
    order = [0, 2, 1, 3, 4, 5, 6]
    mix_in = np.concatenate([w2[:, 512 * i:512 * (i + 1)] for i in order], axis=1)
    moe = np.concatenate([_gated(a["w_gate_2"][0, e], a["w_up_2"][0, e], a["w_down_2"][0, e], EC) for e in range(NE)])
    weights = np.concatenate([
        ffn("ffn1", 0), mla_in, mla_q, mla_kv, _chunks(_tiles(a["mla_w_o"][0])), ffn("ffn2", 0), ple(0),
        ffn("ffn1", 1), _chunks(_tiles(fox[:, :2048])), _chunks(_wide(fox[:, 2048:3072])),
        _chunks(_tiles(a["fox_w_o"][0])), ffn("ffn2", 1), ple(1),
        _chunks(_tiles(mix_in)), _chunks(_tiles(a["w_out_2"][0])), moe])
    assert weights.shape[0] == N_CHUNKS

    def cols(v):
        return v.reshape(-1, P).T

    def fill(v):
        return np.concatenate([v, np.zeros(P - len(v), v.dtype)])[:, None]

    def rows(v):
        return np.broadcast_to(v[None, :], (P, len(v)))

    def packed(v):
        return v.reshape(KD, P, -1).transpose(1, 0, 2).reshape(P, -1)

    f32 = np.float32
    half = ROPE // 2
    inv = (f32(10000.0) ** (-np.arange(0, ROPE, 2, dtype=f32) / f32(ROPE))).astype(f32)
    values = {
        "g_q_lat": cols(a["mla_g_q_lat"][0]), "g_kv_lat": cols(a["mla_g_kv_lat"][0]),
        "mla_qn": fill(a["mla_g_qn"][0]), "mla_kn": fill(a["mla_g_kn"][0]),
        "fox_qn": np.concatenate([a["fox_g_qn"][0]] * 2)[:, None],
        "fox_kn": np.concatenate([a["fox_g_kn"][0]] * 2)[:, None],
        "g_mix2": cols(a["mix_norm_g_2"][0]),
        "conv_a_w": np.concatenate([cols(a["conv_a_w_2"][0, j]) for j in range(3)], axis=1),
        "conv_a_g": cols(a["conv_a_norm_g_2"][0]),
        "dn_conv_w": np.concatenate([cols(a["dn_conv_w_2"][0, j]) for j in range(4)], axis=1),
        "dn_g": a["dn_norm_g_2"][0][:, None], "g_ffn_2": cols(a["ffn_norm_g_2"][0]),
        "g_final": cols(a["final_norm_g_2"]),
        "inv_freq": np.tile(inv, P // half)[:, None],
        "rope_sign": np.tile(np.repeat(np.array([-1.0, 1.0], f32), half), P // ROPE)[:, None],
        "b_f": rows(a["fox_b_f"][0]), "a_log": rows(a["dn_a_log_2"][0]), "dt_bias": rows(a["dn_dt_bias_2"][0]),
        "w_f": packed(fox[:, 3072:]), "w_ba": packed(w2[:, 3584:]),
        "w_router": packed(np.concatenate([a["router_group_w_2"][0], a["router_expert_w_2"][0]], axis=1)),
        "first_wins": np.broadcast_to(np.arange(32, 0, -1, dtype=f32)[None, :], (P, 32)),
    }
    for layer in range(DEPTH):
        for g in ("ffn1", "mix", "ffn2", "ple"):
            values[f"g_{g}_{layer}"] = cols(a[f"g_{g}"][layer])
    par = np.ascontiguousarray(np.concatenate([values[n] for n, _ in PARAMS], axis=1).astype(f32))

    def feature_major(x):
        return np.ascontiguousarray(x.T.reshape(-1, P, T).transpose(1, 0, 2))

    arrays = {
        "xT": feature_major(a["x"][0]),
        "pT": np.ascontiguousarray(np.concatenate([feature_major(a["p"][i, 0]) for i in range(DEPTH)], axis=1)),
        "pos": np.ascontiguousarray(np.broadcast_to(a["positions"], (P, T))),
        "par": par, "weights": weights,
    }
    nc = bacc.Bacc("TRN2", target_bir_lowering=False, num_devices=1)
    aps = [nc.dram_tensor(n, v.shape, mybir.dt.from_np(v.dtype), kind="ExternalInput").ap() for n, v in arrays.items()]
    out = nc.dram_tensor("outT", (P, KD, T), F32, kind="ExternalOutput").ap()
    two_block_kernel(nc, *aps, out)
    r = run_bass_kernel_spmd(nc, [arrays], core_ids=[0])
    y = np.asarray(r.results[0]["outT"])
    return np.ascontiguousarray(y.transpose(1, 0, 2).reshape(D, T).T)[None]
```

```python
from contextlib import ExitStack

import numpy as np
import concourse.bass as bass
from concourse import mybir

P = 128
T = 256
D = 1024
KD = D // P
DEPTH = 2
FF = 2816
FFC = FF // P
PLE = 256
EPS = 1e-6
H = 16
QR, KVR, NOPE, ROPE, DV = 512, 256, 64, 32, 64
QK = NOPE + ROPE
DNH = 4
CG = 512
NE, NG, EPG, EFF = 32, 4, 8, 512
EC = EFF // P
EXPERT_TILES = 3 * KD * EC
CAP = 32
QUAD = P // CAP
CT = 24
RING = 4
HIGH = 2
NEG = -1.0e30

F32 = mybir.dt.float32
F32R = mybir.dt.float32r
I32 = mybir.dt.int32
ALU = mybir.AluOpType
ACT = mybir.ActivationFunctionType
AXX = mybir.AxisListType.X


def chunks_of(tiles):
    return -(-tiles // CT)


def stream_plan():
    sizes = []
    for layer in range(DEPTH):
        sizes.append((f"ffn1_{layer}", FFC + 1))
        if layer == 0:
            sizes += [("mla_in", chunks_of(7 * KD)), ("mla_q", chunks_of(H * 4)), ("mla_kv", chunks_of(32)),
                      ("mla_o", chunks_of(64))]
        else:
            sizes += [("fox_qk", chunks_of(128)), ("fox_v", chunks_of(64)), ("fox_o", chunks_of(64))]
        sizes += [(f"ffn2_{layer}", FFC + 1), (f"ple_{layer}", chunks_of(80))]
    sizes += [("mix_in", chunks_of(28 * KD)), ("mix_out", chunks_of(64)), ("moe", NE * EC)]
    plan, at = {}, 0
    for name, n in sizes:
        plan[name] = at
        at += n
    return plan, at


PLAN, N_CHUNKS = stream_plan()

PARAMS = [("g_ffn1_0", 8), ("g_mix_0", 8), ("g_ffn2_0", 8), ("g_ple_0", 8), ("g_ffn1_1", 8), ("g_mix_1", 8),
          ("g_ffn2_1", 8), ("g_ple_1", 8), ("g_q_lat", 4), ("g_kv_lat", 2), ("mla_qn", 1), ("mla_kn", 1),
          ("fox_qn", 1), ("fox_kn", 1), ("g_mix2", 8), ("conv_a_w", 12), ("conv_a_g", 4), ("dn_conv_w", 48),
          ("dn_g", 1), ("g_ffn_2", 8), ("g_final", 8), ("inv_freq", 1), ("rope_sign", 1), ("b_f", 16),
          ("a_log", 4), ("dt_bias", 4), ("w_f", 128), ("w_ba", 64), ("w_router", 8 * 36), ("first_wins", 32)]
COL, NPAR = {}, 0
for _name, _n in PARAMS:
    COL[_name] = NPAR
    NPAR += _n

LIN, _at = {}, 0
for _name, _n in [("mla_in", 4), ("mla_q", 8), ("mla_k", 8), ("mla_v", 4), ("mla_o", 4), ("ple_0", 8),
                  ("fox_qk", 8), ("fox_v", 4), ("fox_o", 4), ("ple_1", 8), ("mix_in", 14), ("mix_out", 4)]:
    LIN[_name] = _at
    _at += _n

HN = {"mla_q": 0, "mla_k": 8, "fox_qk": 16, "conv_a": 24, "dn_q": 26, "dn_k": 28, "dn_o": 30}
NORM = {n: i for i, n in enumerate(["ffn1_0", "mix_0", "q_lat", "kv_lat", "ffn2_0", "ple_0", "ffn1_1", "mix_1",
                                    "ffn2_1", "ple_1", "mix2", "ffn_2", "final"])}
WHOLE = {n: i for i, n in enumerate(n for n in NORM if n not in ("ffn1_0", "ffn2_0", "ffn1_1", "ffn2_1"))}
FFNS = ["ffn1_0", "ffn2_0", "ffn1_1", "ffn2_1"]
GU = {"ffn1_0": 0, "ffn2_0": FFC, "ffn1_1": 2 * FFC, "ffn2_1": 3 * FFC, "moe": 4 * FFC}
HREADY = {"ffn1_0": 1, "mix_0": 2, "ffn2_0": 3, "ple_0": 4, "ffn1_1": 5, "mix_1": 6, "ffn2_1": 7, "ple_1": 8,
          "mix2": 9, "ffn_2": 10, "final": 11}
TWO_PI = 6.283185307179586
PI2_A = 6.28125
PI2_B = 0.0019350051879882812
PI2_C = TWO_PI - PI2_A - PI2_B
ROUND = 1.5 * 2 ** 23


class Steps:

    def __init__(self, eng, sem):
        self.eng, self.sem, self.n = eng, sem, 0

    def done(self, ins):
        self.n += 1
        ins.then_inc(self.sem, 1)

    def settled(self):
        self.eng.wait_ge(self.sem, self.n)

    def link(self, ins):
        self.done(ins)
        self.settled()


def two_block_kernel(nc, xT, pT, pos, par, weights, out):
    with ExitStack() as ctx:
        def sb(name, shape, dt=F32):
            return ctx.enter_context(nc.sbuf_tensor("sb_" + name, shape, dt))

        def rounded_view(name, shape):
            with nc.sbuf_tensor("sb_" + name, shape, F32R) as view:
                return view

        def sem(name):
            return ctx.enter_context(nc.semaphore(name))

        ring_lo = rounded_view("ring_lo", [P, RING, CT * P])
        ring = sb("ring", [P, RING, CT * P])
        high = sb("high", [P, HIGH, CT * P], F32R)
        act_hi = sb("act_hi", [P, 2, T], F32R)
        h = sb("h", [P, KD, T])
        x_hi = rounded_view("x_hi", [P, KD, T])
        hn = sb("hn", [P, KD, T])
        x_lo = rounded_view("x_lo", [P, KD, T])
        sq = sb("sq", [P, KD, T])
        lnv = sb("lnv", [P, 2, 2 * T])
        rstd = sb("rstd", [P, 2, T])
        params = sb("params", [P, NPAR])
        pin = sb("pin", [P, 2 * DEPTH, T])
        ones = sb("ones", [P, P])
        ones64 = sb("ones64", [P, P])
        ident = sb("ident", [P, P])
        stack = sb("stack", [P, P])
        upper = sb("upper", [P, P])
        mask = sb("mask", [P, 3 * P])
        eps_col = sb("eps_col", [P, 1])
        level = sb("level", [P, 7, P])
        expg = sb("expg", [P, 2, T])
        gate_r = sb("gate_r", [P, 2, T])
        act_lo = rounded_view("act_lo", [P, 2, T])
        act = sb("act", [P, 2, T])
        qk = sb("qk", [P, 2 * H, T])
        qT, kT = qk[:, 0:H, :], qk[:, H:2 * H, :]
        v_tok = sb("v_tok", [P, 2, D])
        oT = sb("oT", [P, KD, T])
        sqh = sb("sqh", [P, 2, 2, T])
        rsh = sb("rsh", [P, 2, 2 * T])
        cosr = sb("cosr", [P, T])
        sinr = sb("sinr", [P, T])
        kpe, kr = gate_r[:, 0, :], gate_r[:, 1, :]
        gq = sb("gq", [P, 4])
        attn = sb("attn", [P, 18 * P + 4 * T + H * P])
        logits, probs, pT_sb = (attn[:, i * 6 * P:(i + 1) * 6 * P].rearrange("p (b n) -> p b n", b=2) for i in range(3))
        rope_t = attn[:, 18 * P:18 * P + 4 * T].rearrange("p (b n) -> p b n", b=2)
        head_row = attn[0:H, 18 * P + 4 * T:18 * P + 4 * T + H * P].rearrange("p (h n) -> p h n", n=P)
        scratch = attn
        nmax = sb("nmax", [P, 2 * H, 2])
        psums = sb("psums", [P, 2 * H, 2])
        small = sb("small", [P, 512])
        ndec = sb("ndec", [H, T])
        dtok = sb("dtok", [P, 2, H])
        route = sqh[:, :, :, :].rearrange("p a b t -> p (a b t)")[:, 0:2 * 352].rearrange("p (c n) -> p c n", c=2)
        peak = sb("peak", [P, 1], I32)

        posi = v_tok[:, 0, 0:T].bitcast(I32)
        cq = oT[:, 0:4, :]
        ckv = oT[:, 4:6, :]
        PADQ = T + 3
        PADU = T + 2
        gate_rows = qk[:, :, :].rearrange("p e t -> p (e t)")
        slots = gate_rows[:, 0:2048].rearrange("p (c s) -> p c s", c=2)
        gated_slots = gate_rows[:, 2048:4096].rearrange("p (c s) -> p c s", c=2)
        slots_T = gate_rows[:, 4096:6144]
        gathered = gate_rows[:, 6144:7168].rearrange("p (k s) -> p k s", s=P)
        y_slots = gate_rows[:, 7168:8192]
        h_tok = v_tok
        partial = sq[:, 0:4, :].rearrange("p a t -> p (a t)").rearrange("p (b n) -> p b n", b=2)
        qkv_pad = scratch[:, 0:12 * PADQ].rearrange("p (n t) -> p n t", t=PADQ)
        u_pad = scratch[:, 12 * PADQ:12 * PADQ + 4 * PADU].rearrange("p (n t) -> p n t", t=PADU)
        a_h = qT[:, 0:4, :]
        a_b = qT[:, 4:8, :]
        z_gate = qT[:, 8:12, :]
        y_a = qT[:, 12:16, :]
        qkv = kT[:, 0:12, :]
        convt = kT[:, 12:16, :]
        mixT = oT

        B = [ctx.enter_context(nc.psum_tensor(f"bank{i}", [P, 512], F32)) for i in range(8)]
        OUTB = B[4:8]

        def turned_part(part):
            return B[2 + part][:, :].rearrange("p (m s) -> p m s", s=P)[:, :, 0:CAP]


        par_in, x_in, p_in, pos_in = sem("par_in"), sem("x_in"), sem("p_in"), sem("pos_in")
        slot_in = [sem(f"slot_in{j}") for j in range(RING)]
        ring_free = sem("ring_free")
        consts = sem("consts")
        pool_step = sem("pool_step")
        act_step = sem("act_step")
        dve_step = sem("dve_step")
        h_ready = sem("h_ready")
        norm_sq, norm_sum, norm_rstd, norm_out = sem("norm_sq"), sem("norm_sum"), sem("norm_rstd"), sem("norm_out")
        high_in, low_in, x_full, x_high, x_low, act_parts = (
            sem("high_in"), sem("low_in"), sem("x_full"), sem("x_high"), sem("x_low"), sem("act_parts"))
        gu_ready, sig_ready, glu_step, act_ready, acc_ready = (
            sem("gu_ready"), sem("sig_ready"), sem("glu_step"), sem("act_ready"), sem("acc_ready"))
        lin_ready, lin_free = sem("lin_ready"), sem("lin_free")
        hn_src, hn_sq, hn_sum, hn_rs, hn_done = sem("hn_src"), sem("hn_sq"), sem("hn_sum"), sem("hn_rs"), sem("hn_done")
        rope_arg, rope_sin = sem("rope_arg"), sem("rope_sin")
        scores, masked, expd, rcpd, prob_ready = sem("scores"), sem("masked"), sem("expd"), sem("rcpd"), sem("prob_ready")
        turned, pt_ready, pv_done, o_ready = sem("turned"), sem("pt_ready"), sem("pv_done"), sem("o_ready")
        f_ready, f_abs, f_ln, logf_ready, dec_sum, dec_ready = (
            sem("f_ready"), sem("f_abs"), sem("f_ln"), sem("logf_ready"), sem("dec_sum"), sem("dec_ready"))
        ple_e = sem("ple_e")
        silu_in, silu_e, z_exp = sem("silu_in"), sem("silu_e"), sem("z_exp")
        ba_ready, ba_abs, ba_ln, bg_ready = sem("ba_ready"), sem("ba_abs"), sem("ba_ln"), sem("bg_ready")
        rows_ready, gdiff, gdecay, dn_qk, dn_ready = (
            sem("rows_ready"), sem("gdiff"), sem("gdecay"), sem("dn_qk"), sem("dn_ready"))
        tok_ready, tok_scaled = sem("tok_ready"), sem("tok_scaled")
        inv_p, inv_p_sb, inv_x, inv_done = sem("inv_p"), sem("inv_p_sb"), sem("inv_x"), sem("inv_done")
        dn_pe, dn_sb = sem("dn_pe"), sem("dn_sb")
        mix_ready = sem("mix_ready")
        rt_ready, rt_max, rt_exp, rt_gate, rt_rows, rt_free = (
            sem("rt_ready"), sem("rt_max"), sem("rt_exp"), sem("rt_gate"), sem("rt_rows"), sem("rt_free"))
        turn_h, h_tok_in, counted, slots_in, slots_turned, slots_T_in, peak_in = (
            sem("turn_h"), sem("h_tok_in"), sem("counted"), sem("slots_in"), sem("slots_turned"), sem("slots_T_in"),
            sem("peak_in"))
        gather_sum, gather_act, gather_dve = sem("gather_sum"), sem("gather_act"), sem("gather_dve")
        ex_gu, ex_exp, ex_step, ex_act, ex_down, y_act, y_dve, ex_scatter, ex_added = (
            sem("ex_gu"), sem("ex_exp"), sem("ex_step"), sem("ex_act"), sem("ex_down"), sem("y_act"), sem("y_dve"),
            sem("ex_scatter"), sem("ex_added"))
        part_in, ex_turned = [sem("part_in_gate"), sem("part_in_up")], sem("ex_turned")
        out_done = sem("out_done")

        def col(name, i=0, n=1):
            return params[:, COL[name] + i:COL[name] + i + n]

        def rep(ap, n):
            return ap.rearrange("p (a t) -> p a t", a=1).to_broadcast([ap.shape[0], n, ap.shape[1]])

        silu_tmp = [v_tok[:, 0, :].rearrange("p (n t) -> p n t", t=T), v_tok[:, 1, :].rearrange("p (n t) -> p n t", t=T),
                    mixT[:, 4:8, :]]
        vflat = v_tok[:, :, :].rearrange("p a n -> p (a n)")
        DELTA = {
            "decay": sq[:, 0:4, :].rearrange("p a t -> p (a t)").rearrange("p (c t) -> p c t", t=P),
            "brow": sq[:, 4:8, :].rearrange("p a t -> p (a t)").rearrange("p (c t) -> p c t", t=P),
            "lt": hn[:, 0:4, :].rearrange("p a t -> p (a t)").rearrange("p (c t) -> p c t", t=P),
            "intra": hn[:, 4:8, :].rearrange("p a t -> p (a t)").rearrange("p (c t) -> p c t", t=P),
            "x": vflat[:, 0:1024].rearrange("p (c t) -> p c t", t=P),
            "xt": vflat[:, 1024:2048].rearrange("p (c t) -> p c t", t=P),
            "lw": pin[:, :, :].rearrange("p a t -> p (a t)").rearrange("p (c t) -> p c t", t=P),
            "pm": mixT[:, 4:8, :].rearrange("p a t -> p (a t)").rearrange("p (c t) -> p c t", t=P),
            "vb": scratch[:, 4200:5224].rearrange("p (c t) -> p c t", t=P),
            "vn": scratch[:, 0:1024].rearrange("p (c t) -> p c t", t=P),
            "kd": scratch[:, 1024:1536].rearrange("p (c t) -> p c t", t=P),
            "state": scratch[:, 1536:2048].rearrange("p (c t) -> p c t", t=P),
            "qd": scratch[:, 2048:2560].rearrange("p (c t) -> p c t", t=P),
            "egrow": scratch[:, 2560:3072].rearrange("p (c t) -> p c t", t=P),
        }

        block = ctx.enter_context(nc.Block())

        @block.sync
        def _(sp):
            sp.dma_start(params[:], par).then_inc(par_in, 16)
            sp.dma_start(h[:], xT).then_inc(x_in, 16)
            for j in range(RING):
                sp.dma_start(ring[:, j, :], weights[j]).then_inc(slot_in[j], 16)
            sp.dma_start(pin[:], pT).then_inc(p_in, 16)
            sp.dma_start(posi, pos).then_inc(pos_in, 16)
            whole = N_CHUNKS // RING
            with sp.Fori(1, whole) as r:
                for j in range(RING):
                    sp.wait_ge(ring_free, r * RING + (j - RING + 1))
                    sp.dma_start(ring[:, j, :], weights[r * RING + j]).then_inc(slot_in[j], 16)
            for n in range(whole * RING, N_CHUNKS):
                sp.wait_ge(ring_free, n - RING + 1)
                sp.dma_start(ring[:, n % RING, :], weights[n]).then_inc(slot_in[n % RING], 16)
            sp.wait_ge(norm_out, WHOLE["final"] + 1)
            sp.dma_start(out, hn[:]).then_inc(out_done, 16)
            sp.wait_ge(out_done, 16)

        @block.gpsimd
        def _(pool):
            st = Steps(pool, pool_step)
            for t, v in ((ones, 1.0), (ones64, 0.0), (ident, 0.0), (stack, 0.0), (upper, 1.0), (mask, 0.0), 
                         (eps_col, EPS), (level, 1.0)):
                st.link(nc.gpsimd.memset(t[:], v))
            st.link(nc.gpsimd.memset(head_row, 0.0))
            st.settled()
            for g in range(2):
                st.link(nc.gpsimd.memset(ones64[64 * g:64 * g + 64, 64 * g:64 * g + 64], 1.0))
            st.link(nc.gpsimd.affine_select(out=ident[:], in_=ident[:], compare_op=ALU.not_equal, fill=1.0, base=0,
                                            pattern=[[-1, P]], channel_multiplier=1))
            for i in range(1 - QUAD, QUAD):
                st.link(nc.gpsimd.affine_select(out=stack[:], in_=stack[:], compare_op=ALU.not_equal, fill=1.0,
                                                base=CAP * i, pattern=[[-1, P]], channel_multiplier=1))
            st.link(nc.gpsimd.affine_select(out=upper[:], in_=upper[:], compare_op=ALU.is_ge, fill=0.0, base=0,
                                            pattern=[[1, P]], channel_multiplier=-1))
            for c in (0, 2):
                m = mask[:, c * P:(c + 1) * P]
                st.link(nc.gpsimd.affine_select(out=m, in_=m, compare_op=ALU.is_ge, fill=NEG, base=0,
                                                pattern=[[-1, P]], channel_multiplier=1))
            st.link(nc.gpsimd.affine_select(out=head_row, in_=head_row, compare_op=ALU.not_equal, fill=1.0,
                                            base=0, pattern=[[-1, H], [0, P]], channel_multiplier=1))
            for i in range(7):
                w = 1 << i
                v = level[:, i, :].rearrange("p (b a r) -> p b a r", a=2, r=w)
                st.link(nc.gpsimd.memset(v[:, :, 0, :], 0.0))
                up = v[:, :, 1, :]
                st.link(nc.gpsimd.affine_select(out=up, in_=up, compare_op=ALU.is_ge, fill=0.0, base=0,
                                                pattern=[[-2 * w, P // (2 * w)], [0, w]], channel_multiplier=1))
                st.link(nc.gpsimd.affine_select(out=up, in_=up, compare_op=ALU.is_ge, fill=0.0, base=w - 1,
                                                pattern=[[2 * w, P // (2 * w)], [0, w]], channel_multiplier=-1))
            st.settled()
            nc.gpsimd.memset(small[:, 511:512], 0.0).then_inc(consts, 1)

        @block.tensor
        def _(pe):
            owed = [0]

            def mm(o, l, r, start, stop, inc=None):
                ins = nc.tensor.matmul(o, l, r, start=start, stop=stop, skip_group_check=True)
                if inc is not None:
                    ins.then_inc(inc, 1)
                elif owed[0]:
                    ins.then_inc(ring_free, owed[0])
                    owed[0] = 0
                return ins

            def chunk_in(n):
                pe.wait_ge(slot_in[n % RING], 16 * (n // RING + 1))

            def tile(n, i, c0=0, c1=P):
                return ring[:, n % RING, i * P + c0:i * P + c1]

            class Tiles:

                def __init__(self, name):
                    self.at, self.i = PLAN[name], 0

                def next(self, c0=0, c1=P, width=1, hold=False):
                    n, i = self.at + self.i // CT, self.i % CT
                    if i == 0:
                        chunk_in(n)
                    self.i += width
                    return ring[:, n % RING, i * P + c0:(i + width - 1) * P + c1]

                def used(self):
                    if self.i % CT == 0:
                        owed[0] += 1

                def end(self):
                    if self.i % CT:
                        owed[0] += 1

            def norm_sums(name, nk):
                n = NORM[name]
                pe.wait_ge(norm_sq, n + 1)
                for k in range(nk):
                    mm(B[2][:, 0:T], ones[:], sq[:, k, :], k == 0, k == nk - 1, norm_sum if k == nk - 1 else None)

            def normed(name):
                pe.wait_ge(norm_out, WHOLE[name] + 1)

            def bank_free(g):
                if g >= 4:
                    pe.wait_ge(lin_free, g - 3)
                return OUTB[g % 4]

            def project(name, lin, groups, rhs, nk, per=2, cols=P):
                tl = Tiles(name)
                for g in range(groups[0], groups[1]):
                    bank = bank_free(LIN[lin] + g)
                    n_tiles = per(g) if callable(per) else per
                    for j in range(n_tiles):
                        for k in range(nk):
                            mm(bank[0:cols, j * T:(j + 1) * T], tl.next(0, cols), rhs[:, k, :], k == 0, k == nk - 1,
                               lin_ready if k == nk - 1 and j == n_tiles - 1 else None)
                            tl.used()
                tl.end()

            def head_sums(g, lhsT, parts):
                pe.wait_ge(hn_sq, g + 1)
                mm(B[2 + g % 2][0:parts, :], lhsT, sqh[0:parts, g % 2, :, :].rearrange("p a t -> p (a t)"), True, True,
                   hn_sum)

            def gated(name):
                base, gu0, f = PLAN[name], GU[name], FFNS.index(name)

                def mm3(o, slot, i, x_hi, x_lo, start, stop, inc):
                    w_hi = high[:, slot % HIGH, i * P:(i + 1) * P]
                    w_lo = ring_lo[:, slot % RING, i * P:(i + 1) * P]
                    mm(o, w_hi, x_hi, start, False)
                    mm(o, w_hi, x_lo, False, False)
                    mm(o, w_lo, x_hi, False, stop, inc)

                def gate_up(slot, par, first):
                    for part in range(2):
                        for k in range(KD):
                            if first and part == 0:
                                pe.wait_ge(x_low, KD * f + k + 1)
                            mm3(B[par][:, part * T:(part + 1) * T], slot, part * KD + k, x_hi[:, k, :],
                                x_lo[:, k, :], k == 0, k == KD - 1,
                                gu_ready if part == 1 and k == KD - 1 else None)

                def down(slot, par, start, stop):
                    for m in range(KD):
                        inc = (acc_ready if stop else ring_free) if m == KD - 1 else None
                        mm3(OUTB[m // 2][:, (m % 2) * T:(m % 2 + 1) * T], slot, 2 * KD + m, act_hi[:, par, :],
                            act_lo[:, par, :], start and m % 2 == 0, stop, inc)

                chunks0 = f * (FFC + 1)
                pe.wait_ge(low_in, chunks0 + 1)
                gate_up(base, 0, True)
                owed[0] += 1
                pe.wait_ge(low_in, chunks0 + 2)
                gate_up(base + 1, 1, False)
                pe.wait_ge(act_parts, gu0 + 1)
                down(base + 1, 0, True, False)
                with pe.Fori(0, (FFC - 2) // RING) as r:
                    for j in range(RING):
                        c = 2 + j
                        pe.wait_ge(low_in, r * RING + (chunks0 + c + 1))
                        gate_up(base + c, c % 2, False)
                        pe.wait_ge(act_parts, r * RING + (gu0 + c))
                        down(base + c, (c - 1) % 2, False, False)
                pe.wait_ge(low_in, chunks0 + FFC + 1)
                pe.wait_ge(act_parts, gu0 + FFC)
                down(base + FFC, (FFC - 1) % 2, False, True)
                owed[0] += 1

            def attention(first, kq, fox):
                for i in range(H + 2):
                    if i < H:
                        a = first + i
                        if i >= 2:
                            pe.wait_ge(masked, a - 1)
                        s = B[a % 2]
                        for cols, q0, k1 in ((0, 0, P), (P, P, T)):
                            ql, kl = kq(i, q0, q0 + P, 0, k1)
                            mm(s[:, cols:cols + k1], ql, kl, True, not fox,
                               None if fox or cols == 0 else scores)
                            if fox:
                                mm(s[:, cols:cols + k1], head_row[:, i, :], ndec[:, 0:k1], False, True,
                                   None if cols == 0 else scores)
                    if 1 <= i <= H:
                        a = first + i - 1
                        pe.wait_ge(prob_ready, a + 1)
                        for j in range(3):
                            ins = nc.tensor.transpose(B[2 + a % 2][:, j * P:(j + 1) * P],
                                                      probs[:, a % 2, j * P:(j + 1) * P], ident[:])
                        ins.then_inc(turned, 1)
                    if i >= 2:
                        hd = i - 2
                        a = first + hd
                        pair = a // 2
                        pe.wait_ge(pt_ready, a + 1)
                        if hd % 2 == 0 and hd >= 4:
                            pe.wait_ge(o_ready, pair - 1)
                        ob = B[4 + pair % 2]
                        lo = 64 * (hd % 2)
                        v0, v1 = (v_tok[:, c, hd * DV:(hd + 1) * DV] for c in range(2))
                        mm(ob[lo:lo + DV, 0:P], v0, pT_sb[:, a % 2, 0:P], True, True)
                        mm(ob[lo:lo + DV, P:T], v0, pT_sb[:, a % 2, P:2 * P], True, False)
                        mm(ob[lo:lo + DV, P:T], v1, pT_sb[:, a % 2, 2 * P:3 * P], False, True, pv_done)

            def ple(layer):
                name = f"ple_{layer}"
                norm_sums(name, KD)
                normed(name)
                if layer == 0:
                    pe.wait_ge(p_in, 16)
                tl = Tiles(name)
                for m in range(KD):
                    bank = bank_free(LIN[name] + m)
                    for k in range(KD):
                        mm(bank[:, 0:T], tl.next(), hn[:, k, :], k == 0, k == KD - 1)
                        tl.used()
                    for k in range(2):
                        mm(bank[:, T:2 * T], tl.next(), pin[:, 2 * layer + k, :], k == 0, k == 1,
                           lin_ready if k == 1 else None)
                        tl.used()
                tl.end()

            def values(name, lin, src, nk):
                tl = Tiles(name)
                tl.i = 0 if name != "mla_kv" else 16
                for half in range(2):
                    t0 = tl.i
                    w = []
                    for k in range(nk):
                        n, i = tl.at + tl.i // CT, tl.i % CT
                        if i == 0:
                            chunk_in(n)
                        w.append(ring[:, n % RING, i * P:(i + 4) * P])
                        tl.i += 4
                    for c in range(2):
                        bank = bank_free(LIN[lin] + 2 * half + c)
                        for k in range(nk):
                            mm(bank[:, :], src[:, k, c * P:(c + 1) * P], w[k], k == 0, k == nk - 1,
                               lin_ready if k == nk - 1 else None)
                    owed[0] += tl.i // CT - t0 // CT
                tl.end()

            pe.wait_ge(consts, 1)
            norm_sums("ffn1_0", KD)
            gated("ffn1_0")

            norm_sums("mix_0", KD)
            normed("mix_0")
            project("mla_in", "mla_in", (0, 4), hn, KD, per=lambda g: 2 if g < 3 else 1)
            norm_sums("q_lat", 4)
            norm_sums("kv_lat", 2)
            normed("q_lat")
            tl = Tiles("mla_q")
            for g in range(9):
                if g < 8:
                    bank = bank_free(LIN["mla_q"] + g)
                    for j in range(2):
                        for k in range(4):
                            mm(bank[0:QK, j * T:(j + 1) * T], tl.next(0, QK), hn[:, k, :], k == 0, k == 3,
                               lin_ready if k == 3 and j == 1 else None)
                            tl.used()
                if g >= 1:
                    head_sums(HN["mla_q"] + g - 1, ones[0:QK, 0:QK], QK)
            tl.end()
            normed("kv_lat")
            n = PLAN["mla_kv"]
            chunk_in(n)
            for g in range(9):
                if g < 8:
                    bank = bank_free(LIN["mla_k"] + g)
                    for j in range(2):
                        for k in range(2):
                            mm(bank[0:NOPE, j * T:(j + 1) * T], tile(n, 2 * g + k, 64 * j, 64 * j + NOPE),
                               hn[:, 4 + k, :], k == 0, k == 1, lin_ready if k == 1 and j == 1 else None)
                if g >= 1:
                    head_sums(HN["mla_k"] + g - 1, ones[0:QK, 0:QK], QK)
            values("mla_kv", "mla_v", hn[:, 4:6, :], 2)
            pe.wait_ge(lin_free, LIN["mla_v"] + 4)
            pe.wait_ge(hn_done, 16)
            attention(0, lambda i, q0, q1, k0, k1: (qT[0:QK, i, q0:q1], kT[0:QK, i, k0:k1]), False)
            pe.wait_ge(o_ready, 8)
            project("mla_o", "mla_o", (0, 4), oT, KD)

            norm_sums("ffn2_0", KD)
            gated("ffn2_0")
            ple(0)

            norm_sums("ffn1_1", KD)
            gated("ffn1_1")
            norm_sums("mix_1", KD)
            normed("mix_1")
            for c in range(2):
                for k in range(KD):
                    mm(B[3][:, c * H:(c + 1) * H], hn[:, k, c * P:(c + 1) * P],
                       params[:, COL["w_f"] + k * H:COL["w_f"] + (k + 1) * H], k == 0, k == KD - 1,
                       f_ready if k == KD - 1 and c == 1 else None)
            pe.wait_ge(logf_ready, 1)
            lf = [small[:, c * H:(c + 1) * H] for c in range(2)]
            mm(B[3][:, 0:H], upper[:], lf[0], True, True)
            mm(B[3][:, H:2 * H], ones[:], lf[0], True, False)
            mm(B[3][:, H:2 * H], upper[:], lf[1], False, True)
            mm(B[3][0:H, P:2 * P], lf[0], upper[:], True, True)
            mm(B[3][0:H, 2 * P:3 * P], lf[0], ones[:], True, False)
            mm(B[3][0:H, 2 * P:3 * P], lf[1], upper[:], False, True, dec_sum)
            pe.wait_ge(dec_ready, 1)
            tl = Tiles("fox_qk")
            for g in range(9):
                if g < 8:
                    bank = bank_free(LIN["fox_qk"] + g)
                    for j in range(2):
                        for k in range(KD):
                            mm(bank[:, j * T:(j + 1) * T], tl.next(), hn[:, k, :], k == 0, k == KD - 1,
                               lin_ready if k == KD - 1 and j == 1 else None)
                            tl.used()
                if g >= 1:
                    head_sums(HN["fox_qk"] + g - 1, ones64[:], P)
            tl.end()
            values("fox_v", "fox_v", hn, KD)
            pe.wait_ge(lin_free, LIN["fox_v"] + 4)

            def fox_qk(i, q0, q1, k0, k1):
                lo = 64 * (i % 2)
                return qT[lo:lo + 64, i // 2, q0:q1], kT[lo:lo + 64, i // 2, k0:k1]

            attention(H, fox_qk, True)
            pe.wait_ge(o_ready, 16)
            project("fox_o", "fox_o", (0, 4), oT, KD)
            norm_sums("ffn2_1", KD)
            gated("ffn2_1")
            ple(1)

            norm_sums("mix2", KD)
            normed("mix2")
            for c in range(2):
                for k in range(KD):
                    mm(B[3][:, c * 8:(c + 1) * 8], hn[:, k, c * P:(c + 1) * P],
                       params[:, COL["w_ba"] + k * 8:COL["w_ba"] + (k + 1) * 8], k == 0, k == KD - 1,
                       ba_ready if k == KD - 1 and c == 1 else None)
            project("mix_in", "mix_in", (0, 14), hn, KD)
            pe.wait_ge(bg_ready, 1)
            for g in range(6):
                head_sums(HN["conv_a"] + g, ones64[:] if g < 2 else ones[:], P)
            pe.wait_ge(hn_rs, HN["dn_o"])
            beta, glog = small[:, 0:8], small[:, 8:16]
            for ch in range(8):
                mm(B[ch // 4][:, (ch % 4) * P:(ch % 4 + 1) * P], glog[:, ch:ch + 1].to_broadcast([P, P]), upper[:],
                   True, True)
            for ch in range(8):
                mm(B[2 + ch // 4][:, (ch % 4) * P:(ch % 4 + 1) * P], beta[:, ch:ch + 1].to_broadcast([P, P]),
                   ident[:], True, True)
            mm(B[4][:, 0:8], upper[:], glog, True, True)
            mm(B[4][:, 8:16], ones[:], glog, True, True, rows_ready)
            pe.wait_ge(dn_qk, 1)
            pe.wait_ge(gdiff, 1)
            for what in range(2):
                for ch in range(8):
                    c, hd = ch // 4, ch % 4
                    kc = qkv[:, 4 + hd, c * P:(c + 1) * P]
                    mm(B[4 + 2 * what + ch // 4][:, hd * P:(hd + 1) * P], kc,
                       kc if what == 0 else qkv[:, hd, c * P:(c + 1) * P], True, True,
                       dn_ready if ch == 7 else None)
            pe.wait_ge(gdecay, 1)
            pe.wait_ge(gdiff, 2)
            for ch in range(12):
                c, hd = (ch // 4, ch % 4) if ch < 8 else (0, ch % 4)
                src = qkv[:, (8 if ch < 8 else 4) + hd, c * P:(c + 1) * P]
                ins = nc.tensor.transpose(B[ch // 4][:, hd * P:(hd + 1) * P], src, ident[:])
            ins.then_inc(tok_ready, 1)
            pe.wait_ge(tok_scaled, 1)
            pe.wait_ge(inv_done, 1)
            for i in range(7):
                lw, x, xt, pm = DELTA["lw"], DELTA["x"], DELTA["xt"], DELTA["pm"]
                for ch in range(8):
                    mm(B[ch // 4][:, (ch % 4) * P:(ch % 4 + 1) * P], lw[:, ch, :], x[:, ch, :], True, True,
                       inv_p if ch == 7 else None)
                pe.wait_ge(inv_p_sb, i + 1)
                for what in range(0 if i < 6 else 1, 2):
                    for ch in range(8):
                        l, r = (xt, pm) if what == 0 else (pm, xt)
                        mm(B[4 + 2 * what + ch // 4][:, (ch % 4) * P:(ch % 4 + 1) * P], l[:, ch, :], r[:, ch, :],
                           True, True, inv_x if ch == 7 and what == 1 else None)
                pe.wait_ge(inv_done, i + 2)
            xt, vb, kd = DELTA["xt"], DELTA["vb"], DELTA["kd"]
            vn, state, intra, qd = DELTA["vn"], DELTA["state"], DELTA["intra"], DELTA["qd"]

            def four(bank, l, r, start=True, stop=True, inc=None):
                for hd in range(4):
                    mm(bank[:, hd * P:(hd + 1) * P], l(hd), r(hd), start and hd == 0, stop,
                       inc if hd == 3 else None)

            four(B[0], lambda d: xt[:, d, :], lambda d: vb[:, d, :], inc=dn_pe)
            pe.wait_ge(dn_sb, 1)
            four(B[2], lambda d: kd[:, d, :], lambda d: vn[:, d, :], inc=dn_pe)
            four(B[1], lambda d: vn[:, d, :], lambda d: intra[:, d, :], inc=dn_pe)
            pe.wait_ge(dn_sb, 2)
            four(B[3], lambda d: qkv[:, 4 + d, P:T], lambda d: state[:, d, :], inc=dn_pe)
            pe.wait_ge(dn_sb, 3)
            four(B[4], lambda d: xt[:, 4 + d, :], lambda d: vb[:, 4 + d, :], inc=dn_pe)
            pe.wait_ge(dn_sb, 4)
            four(B[5], lambda d: state[:, d, :], lambda d: qd[:, d, :], stop=False)
            four(B[5], lambda d: vn[:, 4 + d, :], lambda d: intra[:, 4 + d, :], start=False, inc=dn_pe)
            for g in range(2):
                head_sums(HN["dn_o"] + g, ones[:], P)
            pe.wait_ge(mix_ready, 1)
            project("mix_out", "mix_out", (0, 4), mixT, KD)

            norm_sums("ffn_2", KD)
            normed("ffn_2")
            for c in range(2):
                for k in range(KD):
                    mm(B[3][:, c * 36:(c + 1) * 36], hn[:, k, c * P:(c + 1) * P],
                       params[:, COL["w_router"] + k * 36:COL["w_router"] + (k + 1) * 36], k == 0, k == KD - 1,
                       rt_ready if k == KD - 1 and c == 1 else None)
            for n in range(4):
                for i in range(4):
                    m = 4 * n + i
                    ins = nc.tensor.transpose(OUTB[n][:, i * P:(i + 1) * P],
                                              hn[:, m % KD, (m // KD) * P:(m // KD + 1) * P], ident[:])
            ins.then_inc(turn_h, 1)
            pe.wait_ge(rt_gate, 1)
            chosen = [route[:, c, 320:352] for c in range(2)]
            mm(B[3][:, 0:NE], upper[:], chosen[0], True, True)
            mm(B[3][:, NE:2 * NE], ones[:], chosen[0], True, False)
            mm(B[3][:, NE:2 * NE], upper[:], chosen[1], False, True)
            mm(B[3][:, 2 * NE:3 * NE], ones[:], chosen[0], True, False)
            mm(B[3][:, 2 * NE:3 * NE], ones[:], chosen[1], False, True, counted)

            def moe_gathered():
                pe.wait_ge(slots_in, 1)
                pe.wait_ge(h_tok_in, 2)
                for n in range(4):
                    for i in range(4):
                        qd, c = divmod(4 * n + i, 2)
                        ins = nc.tensor.transpose(OUTB[n][:, i * P:(i + 1) * P],
                                                  gated_slots[:, c, qd * P:(qd + 1) * P], ident[:])
                ins.then_inc(slots_turned, 1)
                pe.wait_ge(slots_T_in, 1)
                base = PLAN["moe"]
                per = EXPERT_TILES // CT * QUAD
                with pe.Fori(0, NE // QUAD) as r:

                    def arrived(i):
                        n = base + i
                        pe.wait_ge(slot_in[n % RING], r * (16 * per // RING) + 16 * (n // RING + 1))

                    def four_tiles(e, t):
                        n, i = base + (e * EXPERT_TILES + t) // CT, t % CT
                        return ring[:, n % RING, i * P:(i + 4) * P]

                    for k in range(KD):
                        for c in range(2):
                            mm(B[6 + k // 4][:, (k % 4) * P:(k % 4 + 1) * P], h_tok[:, c, k * P:(k + 1) * P],
                               slots[:, c, bass.ds(r * P, P)], c == 0, c == 1,
                               gather_sum if k == KD - 1 and c == 1 else None)
                    pe.wait_ge(gather_act, r + 1)
                    pe.wait_ge(gather_dve, r + 1)
                    for e in range(QUAD):
                        s0, n_e = CAP * e, r * QUAD + (e + 1)
                        for k in range(KD):
                            if 8 * k % CT == 0:
                                arrived(e * EC + 8 * k // CT)
                            g = CAP * (k % QUAD)
                            for part in range(2):
                                inc = None
                                if part == 1:
                                    inc = ex_gu if k == KD - 1 else ring_free if 8 * (k + 1) % CT == 0 else None
                                mm(B[part][g:g + CAP, :], gathered[:, k, s0:s0 + CAP], four_tiles(e, 8 * k + 4 * part),
                                   k < QUAD, k >= KD - QUAD, inc)
                        for part in range(2):
                            pe.wait_ge(part_in[part], n_e)
                            for m in range(EC):
                                mm(B[2 + part][:, m * P:(m + 1) * P], partial[:, part, m * P:(m + 1) * P], stack[:],
                                   True, True, ex_turned if m == EC - 1 and part == 1 else None)
                        pe.wait_ge(ex_act, n_e)
                        for m in range(EC):
                            if m == 1:
                                arrived(e * EC + 3)
                            for half in range(2):
                                inc = None
                                if half == 1:
                                    inc = (ring_free if m == 0 or (m == EC - 1 and e < QUAD - 1) else
                                           ex_down if m == EC - 1 else None)
                                mm(B[4 + half][s0:s0 + CAP, :], act[:, 0, m * CAP:(m + 1) * CAP],
                                   four_tiles(e, 64 + 8 * m + 4 * half), m == 0, m == EC - 1, inc)
                    owed[0] += 1
                    pe.wait_ge(y_act, r + 1)
                    pe.wait_ge(y_dve, r + 1)
                    for m in range(KD):
                        mm(B[m // 2][:, (m % 2) * T:(m % 2 + 1) * T], y_slots[:, m * P:(m + 1) * P],
                           slots_T[:, bass.ds(r * T, T)], True, True, ex_scatter if m == KD - 1 else None)
                    pe.wait_ge(ex_added, r + 1)

            def moe_dense():
                pe.wait_ge(h_tok_in, 2)
                for e in range(NE):
                    if e >= 4:
                        pe.wait_ge(rt_free, e // 2 - 1)
                    for c in range(2):
                        mm(B[4 + (e // 2) % 2][:, (e % 2) * T + c * P:(e % 2) * T + (c + 1) * P],
                           route[:, c, 288 + e:289 + e].to_broadcast([P, P]), ident[:], True, True,
                           rt_rows if c == 1 and e % 2 == 1 else None)
                pe.wait_ge(rt_free, NE // 2)
                base = PLAN["moe"]

                def expert(r, first):
                    def place(t):
                        n = base + t // CT
                        return ring[:, n % RING, (t % CT) * P:(t % CT + 1) * P]

                    for i in range(EC):
                        n = base + i
                        pe.wait_ge(slot_in[n % RING], r * 16 + 16 * (n // RING + 1))
                    for m in range(EC + 1):
                        if m < EC:
                            for part in range(2):
                                for k in range(KD):
                                    mm(B[m % 2][:, part * T:(part + 1) * T], place(8 * k + 4 * part + m), hn[:, k, :],
                                       k == 0, k == KD - 1, gu_ready if part == 1 and k == KD - 1 else None)
                        if m >= 1:
                            pe.wait_ge(act_ready, r * EC + m)
                            for o in range(KD):
                                ins = mm(OUTB[o // 2][:, (o % 2) * T:(o % 2 + 1) * T], place(64 + 8 * (m - 1) + o),
                                         act[:, (m - 1) % 2, :], first and m == 1 and o % 2 == 0, True)
                            if m == EC:
                                ins.then_inc(ring_free, EC)

                expert(0, True)
                with pe.Fori(1, NE) as r:
                    expert(r, False)
                nc.tensor.transpose(B[0][:, 0:P], ident[:], ident[:]).then_inc(acc_ready, 1)

            assert owed[0] == 0
            pe.wait_ge(peak_in, 1)
            most = pe.value_load(peak[0:1, 0:1])
            with pe.If(most < CAP + 1):
                moe_gathered()
            with pe.Else():
                moe_dense()
            norm_sums("final", KD)
            assert owed[0] <= 1


        @block.scalar
        def _(act_e):
            st = Steps(act_e, act_step)

            def norm(name, src, nk, dim, src_sem, src_count):
                n = NORM[name]
                act_e.wait_ge(src_sem, src_count)
                nc.scalar.activation(sq[:, 0:nk, :], src, ACT.Square).then_inc(norm_sq, 1)
                act_e.wait_ge(norm_sum, n + 1)
                st.link(nc.scalar.activation(lnv[:, n % 2, 0:T], B[2][:, 0:T], ACT.Ln, bias=eps_col[:, 0:1], scale=1.0 / dim))
                nc.scalar.activation(rstd[:, n % 2, :], lnv[:, n % 2, 0:T], ACT.Exp, scale=-0.5).then_inc(norm_rstd, 1)

            def residual_norm(name):
                norm(name, h[:], KD, D, h_ready, HREADY[name] - 1)

            def head_square(g, src, parts=P):
                nc.scalar.activation(sqh[0:parts, g % 2, :, :].rearrange("p a t -> p (a t)"), src,
                                     ACT.Square).then_inc(hn_sq, 1)

            def head_rstd(g, dim, done, count, parts=P):
                act_e.wait_ge(hn_sum, g + 1)
                if count > 0:
                    act_e.wait_ge(done, count)
                st.link(nc.scalar.activation(lnv[0:parts, g % 2, :], B[2 + g % 2][0:parts, :], ACT.Ln,
                                             bias=eps_col[0:parts, 0:1], scale=1.0 / dim))
                nc.scalar.activation(rsh[0:parts, g % 2, :], lnv[0:parts, g % 2, :], ACT.Exp, scale=-0.5).then_inc(hn_rs, 1)

            def high_part(n, f, reg=0, wait=True):
                act_e.wait_ge(slot_in[n % RING], reg * 16 + 16 * (n // RING + 1))
                if wait:
                    act_e.wait_ge(ring_free, reg * RING + (n - 1))
                nc.scalar.activation(high[:, n % HIGH, :], ring[:, n % RING, :], ACT.Copy).then_inc(high_in, 1)

            def dense_ffn(name, src_sem, src_count):
                base, f = PLAN[name], FFNS.index(name)
                if f:
                    act_e.wait_ge(acc_ready, f)
                high_part(base, f, wait=False)
                high_part(base + 1, f, wait=False)
                norm(name, h[:], KD, D, src_sem, src_count)
                for k in range(KD):
                    act_e.wait_ge(x_full, KD * f + k + 1)
                    nc.scalar.activation(x_hi[:, k, :], sq[:, k, :], ACT.Copy).then_inc(x_high, 1)

                def sigmoid_part(c, b, reg=0):
                    act_e.wait_ge(gu_ready, reg + (GU[name] + c + 1))
                    nc.scalar.activation(expg[:, b, :], B[b][:, 0:T], ACT.Exp, scale=-1.0).then_inc(sig_ready, 1)

                sigmoid_part(0, 0)
                with act_e.Fori(0, (FFC - 2) // RING) as r:
                    for j in range(RING):
                        high_part(base + 2 + j, f, reg=r)
                        sigmoid_part(1 + j, (1 + j) % 2, r * RING)
                for c in range(FFC - 1, FFC + 1):
                    if c + 1 <= FFC:
                        high_part(base + c + 1, f)
                    if c < FFC:
                        sigmoid_part(c, c % 2)

            def attention(first):
                for i in range(H + 1):
                    if i < H:
                        a = first + i
                        act_e.wait_ge(masked, a + 1)
                        if i >= 2:
                            act_e.wait_ge(turned, a - 1)
                        for b, (c0, c1) in enumerate(((0, P), (P, 3 * P))):
                            ins = nc.scalar.activation(probs[:, a % 2, c0:c1], logits[:, a % 2, c0:c1], ACT.Exp,
                                                       bias=nmax[:, a, b:b + 1], accum_out=psums[:, a, b:b + 1])
                        ins.then_inc(expd, 1)
                    if i >= 1:
                        a = first + i - 1
                        act_e.wait_ge(rcpd, a + 1)
                        for b, (c0, c1) in enumerate(((0, P), (P, 3 * P))):
                            ins = nc.scalar.activation(probs[:, a % 2, c0:c1], probs[:, a % 2, c0:c1], ACT.Copy,
                                                       scale=psums[:, a, b:b + 1])
                        ins.then_inc(prob_ready, 1)

            def ple(layer):
                name = f"ple_{layer}"
                residual_norm(name)
                for m in range(KD):
                    act_e.wait_ge(lin_ready, LIN[name] + m + 1)
                    if m >= 2:
                        act_e.wait_ge(lin_free, LIN[name] + m - 1)
                    nc.scalar.activation(expg[:, m % 2, :], OUTB[(LIN[name] + m) % 4][:, 0:T], ACT.Exp,
                                         scale=-1.0).then_inc(ple_e, 1)

            act_e.wait_ge(par_in, 16)
            act_e.wait_ge(consts, 1)
            act_e.wait_ge(rope_arg, 1)
            st.done(nc.scalar.activation(sinr[:], sinr[:], ACT.Sin))
            nc.scalar.activation(cosr[:], cosr[:], ACT.Sin).then_inc(rope_sin, 1)

            dense_ffn("ffn1_0", x_in, 16)
            residual_norm("mix_0")
            norm("q_lat", cq, 4, QR, lin_free, LIN["mla_in"] + 2)
            norm("kv_lat", ckv, 2, KVR, lin_free, LIN["mla_in"] + 3)
            for g in range(9):
                if g < 8:
                    act_e.wait_ge(lin_ready, LIN["mla_q"] + g + 1)
                    head_square(g, OUTB[(LIN["mla_q"] + g) % 4][0:QK, :], QK)
                if g >= 1:
                    head_rstd(g - 1, QK, hn_done, g - 2, QK)
            for b in range(2):
                for j in range(2):
                    nc.scalar.activation(sqh[NOPE:QK, b, j, :], kpe[NOPE:QK, :], ACT.Square)
            for g in range(9):
                if g < 8:
                    act_e.wait_ge(lin_ready, LIN["mla_k"] + g + 1)
                    head_square(8 + g, OUTB[(LIN["mla_k"] + g) % 4][0:NOPE, :], NOPE)
                if g >= 1:
                    head_rstd(7 + g, QK, hn_done, 8 + g - 2, QK)
            attention(0)
            dense_ffn("ffn2_0", h_ready, HREADY["ffn2_0"] - 1)
            ple(0)

            dense_ffn("ffn1_1", h_ready, HREADY["ffn1_1"] - 1)
            residual_norm("mix_1")
            act_e.wait_ge(f_abs, 1)
            st.link(nc.scalar.activation(small[:, 96:128], small[:, 64:96], ACT.Exp, scale=-1.0))
            nc.scalar.activation(small[:, 128:160], small[:, 96:128], ACT.Ln, bias=ones[:, 0:1]).then_inc(f_ln, 1)
            for g in range(9):
                if g < 8:
                    act_e.wait_ge(lin_ready, LIN["fox_qk"] + g + 1)
                    head_square(16 + g, OUTB[(LIN["fox_qk"] + g) % 4][:, :])
                if g >= 1:
                    head_rstd(15 + g, 64, lin_free, LIN["fox_qk"] + g - 2)
            attention(H)
            dense_ffn("ffn2_1", h_ready, HREADY["ffn2_1"] - 1)
            ple(1)

            residual_norm("mix2")
            act_e.wait_ge(ba_abs, 1)
            st.done(nc.scalar.activation(small[:, 64:72], small[:, 32:40], ACT.Exp, scale=-1.0))
            st.done(nc.scalar.activation(small[:, 88:92], col("a_log", 0, 4), ACT.Exp))
            st.link(nc.scalar.activation(small[:, 72:80], small[:, 48:56], ACT.Exp, scale=-1.0))
            nc.scalar.activation(small[:, 80:88], small[:, 72:80], ACT.Ln, bias=ones[:, 0:1]).then_inc(ba_ln, 1)
            for g in range(14):
                act_e.wait_ge(lin_ready, LIN["mix_in"] + g + 1)
                bank = OUTB[(LIN["mix_in"] + g) % 4][:, :].rearrange("p (a t) -> p a t", t=T)
                if g < 2:
                    dst = a_h[:, 2 * g:2 * g + 2, :]
                elif g < 4:
                    dst = convt[:, 2 * (g - 2):2 * (g - 2) + 2, :]
                elif g < 6:
                    dst = a_b[:, 2 * (g - 4):2 * (g - 4) + 2, :]
                elif g < 12:
                    dst = qkv_pad[:, 2 * (g - 6):2 * (g - 6) + 2, 3:PADQ]
                else:
                    dst = z_gate[:, 2 * (g - 12):2 * (g - 12) + 2, :]
                nc.scalar.activation(dst, bank, ACT.Copy).then_inc(lin_free, 1)
            act_e.wait_ge(lin_free, LIN["mix_in"] + 14)
            nc.scalar.activation(pin[:], z_gate, ACT.Exp, scale=-1.0).then_inc(z_exp, 1)
            act_e.wait_ge(hn_src, 1)
            for g in range(3):
                if g < 2:
                    head_square(24 + g, y_a[:, 2 * g:2 * g + 2, :].rearrange("p a t -> p (a t)"))
                if g >= 1:
                    head_rstd(23 + g, 64, hn_done, 15 + g - 1)
            for part in range(3):
                act_e.wait_ge(silu_in, part + 1)
                nc.scalar.activation(silu_tmp[part], qkv[:, 4 * part:4 * part + 4, :], ACT.Exp,
                                     scale=-1.0).then_inc(silu_e, 1)
            for g in range(5):
                if g < 4:
                    act_e.wait_ge(hn_src, 2 + g // 2)
                    head_square(26 + g, qkv[:, 2 * g:2 * g + 2, :].rearrange("p a t -> p (a t)"))
                if g >= 1:
                    head_rstd(25 + g, 1, hn_done, 17 + g - 1)
            act_e.wait_ge(gdiff, 1)
            st.done(nc.scalar.activation(DELTA["decay"], DELTA["decay"], ACT.Exp))
            st.done(nc.scalar.activation(DELTA["egrow"].rearrange("p c t -> p (c t)"), B[1][:, :], ACT.Exp))
            nc.scalar.activation(small[:, 144:160], small[:, 128:144], ACT.Exp).then_inc(gdecay, 1)
            for i in range(7):
                act_e.wait_ge(inv_p, i + 1)
                pm = DELTA["pm"].rearrange("p c t -> p (c t)")
                nc.scalar.activation(pm[:, 0:512], B[0][:, :], ACT.Copy)
                nc.scalar.activation(pm[:, 512:1024], B[1][:, :], ACT.Copy).then_inc(inv_p_sb, 1)
            act_e.wait_ge(hn_src, 4)
            for g in range(3):
                if g < 2:
                    head_square(30 + g, convt[:, 2 * g:2 * g + 2, :].rearrange("p a t -> p (a t)"))
                if g >= 1:
                    head_rstd(29 + g, 128, hn_done, 21 + g - 1)

            residual_norm("ffn_2")
            for i in range(2):
                act_e.wait_ge(rt_max, i + 1)
                c0, n, d0 = ((40, 4, 44), (200, 1, 201))[i]
                nc.scalar.activation(route[:, :, d0:d0 + n], route[:, :, c0:c0 + n], ACT.Exp).then_inc(rt_exp, 1)
            act_e.wait_ge(turn_h, 1)
            for c in range(2):
                ins = nc.scalar.activation(h_tok[:, c, 512:1024], OUTB[2 * c + 1][:, :], ACT.Copy)
            ins.then_inc(h_tok_in, 1)

            def moe_gathered():
                with act_e.Fori(0, NE // QUAD) as r:
                    act_e.wait_ge(gather_sum, r + 1)
                    nc.scalar.activation(gathered[:, 4:8, :].rearrange("p k s -> p (k s)"), B[7][:, :],
                                         ACT.Copy).then_inc(gather_act, 1)
                    for e in range(QUAD):
                        act_e.wait_ge(ex_gu, r * QUAD + (e + 1))
                        nc.scalar.activation(partial[:, 0, :], B[0][:, :], ACT.Copy).then_inc(part_in[0], 1)
                        act_e.wait_ge(ex_turned, r * QUAD + (e + 1))
                        nc.scalar.activation(expg[:, 0, 0:P].rearrange("p (m s) -> p m s", s=CAP), turned_part(0),
                                             ACT.Exp, scale=-1.0).then_inc(ex_exp, 1)
                    act_e.wait_ge(ex_down, r + 1)
                    nc.scalar.activation(y_slots[:, 512:1024], B[5][:, :], ACT.Copy).then_inc(y_act, 1)

            act_e.wait_ge(peak_in, 1)
            most = act_e.value_load(peak[0:1, 0:1])
            with act_e.If(most < CAP + 1):
                moe_gathered()
            with act_e.Else():
                with act_e.Fori(0, NE * EC // 2) as r:
                    for j in range(2):
                        act_e.wait_ge(gu_ready, r * 2 + (GU["moe"] + j + 1))
                        nc.scalar.activation(expg[:, j, :], B[j][:, 0:T], ACT.Exp, scale=-1.0).then_inc(sig_ready, 1)
            residual_norm("final")

        @block.vector
        def _(dve):
            st = Steps(dve, dve_step)
            V = nc.vector

            def norm_apply(name, src, nk, gain, dst):
                n = NORM[name]
                dve.wait_ge(norm_rstd, n + 1)
                for k in range(nk):
                    ins = V.scalar_tensor_tensor(out=dst[:, k, :], in0=src[:, k, :], scalar=col(gain, k),
                                                 in1=rstd[:, n % 2, :], op0=ALU.mult, op1=ALU.mult)
                ins.then_inc(norm_out, 1)

            def add_residual(bank, i, scale, inc):
                hh = h[:, 2 * i:2 * i + 2, :].rearrange("p a t -> p (a t)")
                ins = V.scalar_tensor_tensor(out=hh, in0=bank[:, :], scalar=scale, in1=hh, op0=ALU.mult, op1=ALU.add)
                if inc is not None:
                    ins.then_inc(inc, 1)
                return ins

            def low_part(n, f, c, reg=0):
                dve.wait_ge(high_in, reg * RING + (f * (FFC + 1) + c + 1))
                V.tensor_tensor(ring_lo[:, n % RING, :], ring[:, n % RING, :], high[:, n % HIGH, :].bitcast(F32),
                                ALU.subtract).then_inc(low_in, 1)

            def silu_times_up(b, wait_sig, at, reg, last):
                g, u = B[b][:, 0:T], B[b][:, T:2 * T]
                e, s = expg[:, b, :], gate_r[:, b, :]
                dve.wait_ge(sig_ready, wait_sig)
                V.tensor_scalar_add(e, e, 1.0).then_inc(glu_step, 1)
                dve.wait_ge(glu_step, reg + (at + 1))
                V.reciprocal(s, e).then_inc(glu_step, 1)
                dve.wait_ge(glu_step, reg + (at + 2))
                V.tensor_tensor(s, g, s, ALU.mult).then_inc(glu_step, 1)
                dve.wait_ge(glu_step, reg + (at + 3))
                V.tensor_tensor(act[:, b, :] if last is None else s, u, s, ALU.mult).then_inc(glu_step, 1)
                dve.wait_ge(glu_step, reg + (at + 4))
                if last is not None:
                    V.tensor_tensor(act[:, b, :], s, last, ALU.mult).then_inc(act_ready, 1)

            def dense_ffn(name):
                base, f, gu0 = PLAN[name], FFNS.index(name), GU[name]
                n = NORM[name]
                low_part(base, f, 0)
                low_part(base + 1, f, 1)
                dve.wait_ge(norm_rstd, n + 1)
                for k in range(KD + 2):
                    if k < KD:
                        V.scalar_tensor_tensor(out=sq[:, k, :], in0=h[:, k, :], scalar=col("g_" + name, k),
                                               in1=rstd[:, n % 2, :], op0=ALU.mult, op1=ALU.mult).then_inc(x_full, 1)
                    if k >= 2:
                        dve.wait_ge(x_high, KD * f + k - 1)
                        V.tensor_tensor(x_lo[:, k - 2, :], sq[:, k - 2, :], x_hi[:, k - 2, :].bitcast(F32),
                                        ALU.subtract).then_inc(x_low, 1)

                def act_part(c, b, reg=0):
                    i = gu0 + c
                    silu_times_up(b, reg + (i + 1), 5 * i, reg * 5, None)
                    V.tensor_copy(act_hi[:, b, :], act[:, b, :]).then_inc(glu_step, 1)
                    dve.wait_ge(glu_step, reg * 5 + (5 * i + 5))
                    V.tensor_tensor(act_lo[:, b, :], act[:, b, :], act_hi[:, b, :].bitcast(F32),
                                    ALU.subtract).then_inc(act_parts, 1)

                act_part(0, 0)
                with dve.Fori(0, (FFC - 2) // RING) as r:
                    for j in range(RING):
                        low_part(base + 2 + j, f, 2 + j, r)
                        act_part(1 + j, (1 + j) % 2, r * RING)
                low_part(base + FFC, f, FFC)
                act_part(FFC - 1, (FFC - 1) % 2)
                dve.wait_ge(acc_ready, f + 1)
                for i in range(4):
                    add_residual(OUTB[i], i, 0.5, h_ready if i == 3 else None)

            def attention(first, fox):
                for i in range(H + 4):
                    if i < H:
                        a = first + i
                        dve.wait_ge(scores, a + 1)
                        s = B[a % 2]
                        lg = logits[:, a % 2, :]
                        if fox:
                            st.done(V.scalar_tensor_tensor(out=lg[:, 0:P], in0=s[:, 0:P], scalar=dtok[:, 0, i:i + 1],
                                                           in1=mask[:, 0:P], op0=ALU.add, op1=ALU.add))
                            st.link(V.scalar_tensor_tensor(out=lg[:, P:3 * P], in0=s[:, P:3 * P],
                                                           scalar=dtok[:, 1, i:i + 1], in1=mask[:, P:3 * P],
                                                           op0=ALU.add, op1=ALU.add))
                        else:
                            st.link(V.tensor_tensor(lg, s[:, 0:3 * P], mask[:], ALU.add))
                        st.done(V.tensor_reduce(nmax[:, a, 0:1], lg[:, 0:P], AXX, ALU.max))
                        st.link(V.tensor_reduce(nmax[:, a, 1:2], lg[:, P:3 * P], AXX, ALU.max))
                        V.tensor_scalar(nmax[:, a, :], nmax[:, a, :], -1.0, None, ALU.mult).then_inc(masked, 1)
                    if 1 <= i <= H:
                        a = first + i - 1
                        dve.wait_ge(expd, a + 1)
                        V.reciprocal(psums[:, a, :], psums[:, a, :]).then_inc(rcpd, 1)
                    if 2 <= i <= H + 1:
                        a = first + i - 2
                        dve.wait_ge(turned, a + 1)
                        V.tensor_copy(pT_sb[:, a % 2, :], B[2 + a % 2][:, 0:3 * P]).then_inc(pt_ready, 1)
                    if i >= 4 and i % 2 == 0:
                        pair = (first + i - 4) // 2
                        dve.wait_ge(pv_done, 2 * pair + 2)
                        V.tensor_copy(oT[:, (i - 4) // 2, :], B[4 + pair % 2][:, 0:T]).then_inc(o_ready, 1)

            def out_product(lin):
                for g in range(4):
                    dve.wait_ge(lin_ready, LIN[lin] + g + 1)
                    add_residual(OUTB[(LIN[lin] + g) % 4], g, 1.0, lin_free)
                dve.wait_ge(lin_free, LIN[lin] + 4)
                dve.sem_inc(h_ready, 1)

            def ple(layer):
                name = f"ple_{layer}"
                norm_apply(name, h, KD, f"g_ple_{layer}", hn)
                for m in range(KD):
                    bank = OUTB[(LIN[name] + m) % 4]
                    b = m % 2
                    dve.wait_ge(ple_e, KD * layer + m + 1)
                    st.link(V.tensor_scalar_add(expg[:, b, :], expg[:, b, :], 1.0))
                    st.link(V.reciprocal(gate_r[:, b, :], expg[:, b, :]))
                    V.tensor_tensor(act[:, b, :], bank[:, T:2 * T], gate_r[:, b, :], ALU.mult).then_inc(lin_free, 1)
                    dve.wait_ge(lin_free, LIN[name] + m + 1)
                    ins = V.tensor_tensor(h[:, m, :], h[:, m, :], act[:, b, :], ALU.add)
                ins.then_inc(h_ready, 1)

            def rotate(x, n):
                lo, hi = NOPE, QK
                xr = x.rearrange("p a t -> p (a t)")
                half = ROPE // 2
                turn = [(i + half) % ROPE for i in range(ROPE)]
                a = rope_t[lo:hi, 0, 0:n * T]
                b = rope_t[lo:hi, 1, 0:n * T]
                st.link(V.stream_shuffle(a, xr, turn))
                a3, b3 = (t.rearrange("p (a t) -> p a t", t=T) for t in (a, b))
                st.done(V.tensor_tensor(a3, a3, rep(sinr[lo:hi, :], n), ALU.mult))
                st.link(V.tensor_tensor(b3, x, rep(cosr[lo:hi, :], n), ALU.mult))
                st.link(V.tensor_tensor(x, a3, b3, ALU.add))

            dve.wait_ge(par_in, 16)
            dve.wait_ge(pos_in, 16)
            dve.wait_ge(consts, 1)
            ang, turns = rope_t[:, 0, 0:T], rope_t[:, 1, 0:T]
            st.link(V.tensor_copy(ang, posi))
            st.link(V.tensor_scalar(ang, ang, col("inv_freq"), None, ALU.mult))
            st.link(V.tensor_scalar(turns, ang, 1.0 / TWO_PI, None, ALU.mult))
            st.link(V.tensor_scalar_add(turns, turns, ROUND))
            st.link(V.tensor_scalar_add(turns, turns, -ROUND))
            for part in (PI2_A, PI2_B, PI2_C):
                st.link(V.scalar_tensor_tensor(out=ang, in0=turns, scalar=-part, in1=ang, op0=ALU.mult, op1=ALU.add))
            st.link(V.tensor_scalar(ang, ang, 3.1415925, -3.1415925, ALU.min, ALU.max))
            st.done(V.tensor_copy(sinr[:], ang))
            V.tensor_scalar(cosr[:], ang, 0.5, None, ALU.mult).then_inc(rope_arg, 1)
            st.done(V.tensor_scalar(gq[:, 0:1], col("mla_qn"), float(QK) ** -0.5, None, ALU.mult))
            st.done(V.tensor_scalar(gq[:, 1:2], col("fox_qn"), 0.125, None, ALU.mult))
            dve.wait_ge(rope_sin, 1)
            st.done(V.tensor_scalar(sinr[:], sinr[:], col("rope_sign"), None, ALU.mult))
            st.link(V.tensor_tensor(cosr[:], cosr[:], cosr[:], ALU.mult))
            st.link(V.tensor_scalar(cosr[:], cosr[:], -2.0, 1.0, ALU.mult, ALU.add))

            dve.wait_ge(x_in, 16)
            dense_ffn("ffn1_0")
            norm_apply("mix_0", h, KD, "g_mix_0", hn)
            L0 = LIN["mla_in"]
            for g in range(4):
                dve.wait_ge(lin_ready, L0 + g + 1)
                bank = OUTB[(L0 + g) % 4]
                if g < 3:
                    dst = (cq[:, 0:2, :], cq[:, 2:4, :], ckv)[g].rearrange("p a t -> p (a t)")
                    V.tensor_copy(dst, bank[:, :]).then_inc(lin_free, 1)
                else:
                    V.tensor_copy(kpe, bank[:, 0:T]).then_inc(lin_free, 1)
            norm_apply("q_lat", cq, 4, "g_q_lat", hn)
            norm_apply("kv_lat", ckv, 2, "g_kv_lat", hn[:, 4:6, :])
            dve.wait_ge(lin_free, L0 + 4)
            st.link(V.tensor_scalar(kr[NOPE:QK, :], kpe[NOPE:QK, :], col("mla_kn")[NOPE:QK], None, ALU.mult))
            rotate(kr[NOPE:QK, :].rearrange("p (a t) -> p a t", a=1), 1)
            for g in range(8):
                bank = OUTB[(LIN["mla_q"] + g) % 4]
                q2 = qT[0:QK, 2 * g:2 * g + 2, :].rearrange("p a t -> p (a t)")
                dve.wait_ge(hn_rs, HN["mla_q"] + g + 1)
                V.scalar_tensor_tensor(out=q2, in0=bank[0:QK, :], scalar=gq[0:QK, 0:1], in1=rsh[0:QK, g % 2, :],
                                       op0=ALU.mult, op1=ALU.mult).then_inc(lin_free, 1)
                dve.wait_ge(lin_free, LIN["mla_q"] + g + 1)
                rotate(qT[NOPE:QK, 2 * g:2 * g + 2, :], 2)
                dve.sem_inc(hn_done, 1)
            for g in range(8):
                bank = OUTB[(LIN["mla_k"] + g) % 4]
                gi = HN["mla_k"] + g
                dve.wait_ge(hn_rs, gi + 1)
                V.scalar_tensor_tensor(out=kT[0:NOPE, 2 * g:2 * g + 2, :].rearrange("p a t -> p (a t)"),
                                       in0=bank[0:NOPE, :], scalar=col("mla_kn")[0:NOPE], in1=rsh[0:NOPE, gi % 2, :],
                                       op0=ALU.mult, op1=ALU.mult).then_inc(lin_free, 1)
                V.tensor_tensor(kT[NOPE:QK, 2 * g:2 * g + 2, :], rep(kr[NOPE:QK, :], 2),
                                rsh[NOPE:QK, gi % 2, :].rearrange("p (a t) -> p a t", t=T), ALU.mult).then_inc(hn_done, 1)

            def copy_values(lin):
                for g in range(4):
                    dve.wait_ge(lin_ready, LIN[lin] + g + 1)
                    half, c = g // 2, g % 2
                    V.tensor_copy(v_tok[:, c, half * 512:(half + 1) * 512],
                                  OUTB[(LIN[lin] + g) % 4][:, :]).then_inc(lin_free, 1)

            copy_values("mla_v")
            attention(0, False)
            out_product("mla_o")
            dense_ffn("ffn2_0")
            ple(0)

            dense_ffn("ffn1_1")
            norm_apply("mix_1", h, KD, "g_mix_1", hn)
            dve.wait_ge(f_ready, 1)
            zf = small[:, 32:64]
            st.link(V.tensor_tensor(zf.rearrange("p (c n) -> p c n", n=H),
                                    B[3][:, 0:2 * H].rearrange("p (c n) -> p c n", n=H),
                                    rep(col("b_f", 0, H), 2), ALU.add))
            V.scalar_tensor_tensor(out=small[:, 64:96], in0=zf, scalar=-1.0, in1=zf, op0=ALU.mult,
                                   op1=ALU.max).then_inc(f_abs, 1)
            dve.wait_ge(f_ln, 1)
            V.scalar_tensor_tensor(out=small[:, 0:32], in0=zf, scalar=0.0, in1=small[:, 128:160], op0=ALU.min,
                                   op1=ALU.subtract).then_inc(logf_ready, 1)
            dve.wait_ge(dec_sum, 1)
            V.tensor_copy(dtok[:, :, :].rearrange("p c n -> p (c n)"), B[3][:, 0:2 * H])
            V.tensor_scalar(ndec[:], B[3][0:H, P:3 * P], -1.0, None, ALU.mult).then_inc(dec_ready, 1)
            for g in range(8):
                bank = OUTB[(LIN["fox_qk"] + g) % 4]
                gi = HN["fox_qk"] + g
                dst = (qT if g < 4 else kT)[:, 2 * (g % 4):2 * (g % 4) + 2, :].rearrange("p a t -> p (a t)")
                dve.wait_ge(hn_rs, gi + 1)
                V.scalar_tensor_tensor(out=dst, in0=bank[:, :], scalar=gq[:, 1:2] if g < 4 else col("fox_kn"),
                                       in1=rsh[:, gi % 2, :], op0=ALU.mult, op1=ALU.mult).then_inc(lin_free, 1)
            copy_values("fox_v")
            attention(H, True)
            out_product("fox_o")
            dense_ffn("ffn2_1")
            ple(1)

            norm_apply("mix2", h, KD, "g_mix2", hn)
            st.done(V.memset(qkv_pad[:, :, 0:3], 0.0))
            st.done(V.memset(u_pad[:, :, 0:2], 0.0))
            dve.wait_ge(ba_ready, 1)
            ba = B[3][:, 0:16].rearrange("p (c n) -> p c n", n=8)

            def s3(lo):
                return small[:, lo:lo + 8].rearrange("p (c n) -> p c n", n=4)

            st.done(V.tensor_copy(s3(32), ba[:, :, 0:4]))
            st.link(V.tensor_tensor(s3(40), ba[:, :, 4:8], rep(col("dt_bias", 0, 4), 2), ALU.add))
            V.scalar_tensor_tensor(out=small[:, 48:56], in0=small[:, 40:48], scalar=-1.0, in1=small[:, 40:48], op0=ALU.mult,
                                   op1=ALU.max).then_inc(ba_abs, 1)
            dve.wait_ge(ba_ln, 1)
            st.done(V.tensor_scalar_add(small[:, 64:72], small[:, 64:72], 1.0))
            st.link(V.scalar_tensor_tensor(out=small[:, 56:64], in0=small[:, 40:48], scalar=0.0, in1=small[:, 80:88],
                                           op0=ALU.max, op1=ALU.add))
            st.done(V.reciprocal(small[:, 0:8], small[:, 64:72]))
            st.link(V.tensor_tensor(s3(8), s3(56), rep(small[:, 88:92], 2), ALU.mult))
            V.tensor_scalar(small[:, 8:16], small[:, 8:16], -1.0, None, ALU.mult).then_inc(bg_ready, 1)
            L = LIN["mix_in"]
            dve.wait_ge(lin_free, L + 4)
            st.link(V.tensor_tensor(u_pad[:, :, 2:PADU], convt, a_h, ALU.mult))
            for n in range(4):
                st.done(V.tensor_scalar(y_a[:, n, :], u_pad[:, n, 0:T], col("conv_a_w", n), None, ALU.mult))
            for tap in range(1, 3):
                st.settled()
                for n in range(4):
                    st.done(V.scalar_tensor_tensor(out=y_a[:, n, :], in0=u_pad[:, n, tap:tap + T],
                                                   scalar=col("conv_a_w", 4 * tap + n), in1=y_a[:, n, :],
                                                   op0=ALU.mult, op1=ALU.add))
            st.settled()
            dve.wait_ge(lin_free, L + 6)
            V.tensor_tensor(y_a, y_a, a_b, ALU.mult).then_inc(hn_src, 1)
            for part in range(3):
                dve.wait_ge(lin_free, L + 6 + 2 * (part + 1))
                tiles = range(4 * part, 4 * part + 4)
                for n in tiles:
                    st.done(V.tensor_scalar(qkv[:, n, :], qkv_pad[:, n, 0:T], col("dn_conv_w", n), None, ALU.mult))
                for tap in range(1, 4):
                    st.settled()
                    for n in tiles:
                        ins = V.scalar_tensor_tensor(out=qkv[:, n, :], in0=qkv_pad[:, n, tap:tap + T],
                                                     scalar=col("dn_conv_w", 12 * tap + n), in1=qkv[:, n, :],
                                                     op0=ALU.mult, op1=ALU.add)
                        if tap == 3 and n == tiles[-1]:
                            ins.then_inc(silu_in, 1)
                        else:
                            st.done(ins)
            for part in range(3):
                x, e = qkv[:, 4 * part:4 * part + 4, :], silu_tmp[part]
                dve.wait_ge(silu_e, part + 1)
                st.link(V.tensor_scalar_add(e, e, 1.0))
                st.link(V.reciprocal(e, e))
                if part < 2:
                    V.tensor_tensor(x, x, e, ALU.mult).then_inc(hn_src, 1)
                else:
                    st.link(V.tensor_tensor(x, x, e, ALU.mult))
            dve.wait_ge(z_exp, 1)
            st.link(V.tensor_scalar_add(pin[:], pin[:], 1.0))
            st.link(V.reciprocal(pin[:], pin[:]))
            st.link(V.tensor_tensor(z_gate, z_gate, pin[:], ALU.mult))

            def flat(x):
                return x.rearrange("p a t -> p (a t)")

            for g in range(2):
                dve.wait_ge(hn_rs, 24 + g + 1)
                for j in range(2):
                    n = 2 * g + j
                    ins = V.scalar_tensor_tensor(out=mixT[:, n, :], in0=y_a[:, n, :], scalar=col("conv_a_g", n),
                                                 in1=rsh[:, g % 2, j * T:(j + 1) * T], op0=ALU.mult, op1=ALU.mult)
                ins.then_inc(hn_done, 1)
            for g in range(4):
                dve.wait_ge(hn_rs, 26 + g + 1)
                x = flat(qkv[:, 2 * g:2 * g + 2, :])
                V.scalar_tensor_tensor(out=x, in0=x, scalar=128.0 ** -0.5 if g < 2 else 1.0, in1=rsh[:, g % 2, :],
                                       op0=ALU.mult, op1=ALU.mult).then_inc(hn_done, 1)
            dve.wait_ge(hn_done, 22)
            dve.sem_inc(dn_qk, 1)
            decay, brow, lt, intra = DELTA["decay"], DELTA["brow"], DELTA["lt"], DELTA["intra"]
            dve.wait_ge(rows_ready, 1)
            st.link(V.tensor_copy(small[:, 128:136], B[4][:, 0:8]))
            for ch in range(8):
                st.done(V.tensor_scalar(decay[:, ch, :], B[ch // 4][:, (ch % 4) * P:(ch % 4 + 1) * P],
                                        small[:, 128 + ch:129 + ch], 0.0, ALU.subtract, ALU.min))
            V.tensor_tensor(small[:, 136:144], B[4][:, 8:16], small[:, 128:136], ALU.subtract).then_inc(gdiff, 1)
            bf = flat(brow)
            st.done(V.tensor_copy(bf[:, 0:512], B[2][:, :]))
            V.tensor_copy(bf[:, 512:1024], B[3][:, :]).then_inc(gdiff, 1)
            dve.wait_ge(gdecay, 1)
            st.link(V.tensor_tensor(decay, decay, rep(upper[:], 8), ALU.mult))
            st.done(V.tensor_tensor(DELTA["qd"], qkv[:, 0:4, P:T], DELTA["egrow"], ALU.mult))
            st.done(V.scalar_tensor_tensor(out=small[:, 160:168], in0=small[:, 0:8], scalar=-1.0,
                                           in1=small[:, 144:152], op0=ALU.mult, op1=ALU.mult))
            dve.wait_ge(dn_ready, 1)
            for b in range(2):
                st.done(V.tensor_tensor(flat(lt)[:, b * 512:(b + 1) * 512], B[4 + b][:, :],
                                        flat(decay)[:, b * 512:(b + 1) * 512], ALU.mult))
            dve.wait_ge(dn_ready, 2)
            for b in range(2):
                st.done(V.tensor_tensor(flat(intra)[:, b * 512:(b + 1) * 512], B[6 + b][:, :],
                                        flat(decay)[:, b * 512:(b + 1) * 512], ALU.mult))
            st.settled()
            st.link(V.tensor_tensor(lt, lt, brow, ALU.mult))
            vb, kd = DELTA["vb"], DELTA["kd"]
            dve.wait_ge(tok_ready, 1)
            for ch in range(8):
                st.done(V.tensor_scalar(vb[:, ch, :], B[ch // 4][:, (ch % 4) * P:(ch % 4 + 1) * P],
                                        small[:, ch:ch + 1], None, ALU.mult))
            for hd in range(4):
                ins = V.tensor_scalar(kd[:, hd, :], B[2][:, hd * P:(hd + 1) * P], small[:, 152 + hd:153 + hd], None,
                                      ALU.mult)
            ins.then_inc(tok_scaled, 1)
            x, xt, lw = DELTA["x"], DELTA["xt"], DELTA["lw"]
            st.done(V.tensor_copy(x, rep(ident[:], 8)))
            st.done(V.tensor_copy(xt, rep(ident[:], 8)))
            V.tensor_tensor(lw, lt, rep(level[:, 0, :], 8), ALU.mult).then_inc(inv_done, 1)
            st.settled()
            for i in range(7):
                if i < 6:
                    dve.wait_ge(inv_p, i + 1)
                    st.done(V.tensor_tensor(lw, lt, rep(level[:, i + 1, :], 8), ALU.mult))
                dve.wait_ge(inv_x, i + 1)
                if i < 6:
                    for b in range(2):
                        xb = flat(x)[:, b * 512:(b + 1) * 512]
                        st.done(V.tensor_tensor(xb, xb, B[4 + b][:, :], ALU.subtract))
                for b in range(2):
                    xb = flat(xt)[:, b * 512:(b + 1) * 512]
                    ins = V.tensor_tensor(xb, xb, B[6 + b][:, :], ALU.subtract)
                    if b == 1:
                        ins.then_inc(inv_done, 1)
                    else:
                        st.done(ins)
                st.settled()
                dve.wait_ge(inv_done, i + 2)
            vn, state = DELTA["vn"], DELTA["state"]
            dve.wait_ge(dn_pe, 1)
            V.tensor_copy(flat(vn)[:, 0:512], B[0][:, :]).then_inc(dn_sb, 1)
            dve.wait_ge(dn_pe, 2)
            V.tensor_copy(flat(state), B[2][:, :]).then_inc(dn_sb, 1)
            dve.wait_ge(dn_pe, 3)
            st.done(V.tensor_copy(convt[:, :, 0:P], B[1][:, :].rearrange("p (a t) -> p a t", t=P)))
            dve.wait_ge(dn_pe, 4)
            for hd in range(4):
                ins = V.scalar_tensor_tensor(out=vb[:, 4 + hd, :], in0=B[3][:, hd * P:(hd + 1) * P],
                                             scalar=small[:, 164 + hd:165 + hd], in1=vb[:, 4 + hd, :], op0=ALU.mult,
                                             op1=ALU.add)
            ins.then_inc(dn_sb, 1)
            dve.wait_ge(dn_pe, 5)
            V.tensor_copy(flat(vn)[:, 512:1024], B[4][:, :]).then_inc(dn_sb, 1)
            dve.wait_ge(dn_pe, 6)
            V.tensor_copy(convt[:, :, P:T], B[5][:, :].rearrange("p (a t) -> p a t", t=P)).then_inc(hn_src, 1)
            for g in range(2):
                dve.wait_ge(hn_rs, 30 + g + 1)
                y = flat(mixT[:, 4 + 2 * g:6 + 2 * g, :])
                V.scalar_tensor_tensor(out=y, in0=flat(convt[:, 2 * g:2 * g + 2, :]), scalar=col("dn_g"),
                                       in1=rsh[:, g % 2, :], op0=ALU.mult, op1=ALU.mult).then_inc(hn_done, 1)
                dve.wait_ge(hn_done, 22 + g + 1)
                ins = V.tensor_tensor(y, y, flat(z_gate[:, 2 * g:2 * g + 2, :]), ALU.mult)
            ins.then_inc(mix_ready, 1)
            out_product("mix_out")

            norm_apply("ffn_2", h, KD, "g_ffn_2", hn)
            dve.wait_ge(rt_ready, 1)

            def R(lo, n):
                return route[:, :, lo:lo + n]

            def wide(lo, n):
                return R(lo, 1).to_broadcast([P, 2, n])

            def both(x):
                return x.rearrange("p (a t) -> p a t", a=1).to_broadcast([P, 2, x.shape[1]])

            def first_best(x, n, best, tmp, hot):
                st.link(V.tensor_reduce(R(best, 1), R(x, n), AXX, ALU.max))
                st.link(V.tensor_tensor(R(tmp, n), R(x, n), wide(best, n), ALU.is_equal))
                st.link(V.tensor_tensor(R(tmp, n), R(tmp, n), both(col("first_wins", 0, n)), ALU.mult))
                st.link(V.tensor_reduce(R(best + 1, 1), R(tmp, n), AXX, ALU.max))
                st.link(V.tensor_tensor(R(hot, n), R(tmp, n), wide(best + 1, n), ALU.is_equal))

            dve.wait_ge(turn_h, 1)
            for c in range(2):
                ins = V.tensor_copy(h_tok[:, c, 0:512], OUTB[2 * c][:, :])
            ins.then_inc(h_tok_in, 1)
            st.link(V.tensor_copy(R(0, 36), B[3][:, 0:72].rearrange("p (c n) -> p c n", n=36)))
            first_best(0, 4, 36, 40, 48)
            V.tensor_tensor(R(40, 4), R(0, 4), wide(36, 4), ALU.subtract).then_inc(rt_max, 1)
            st.link(V.tensor_scalar(R(52, 4), R(48, 4), -1.0, -NEG, ALU.add, ALU.mult))
            for c in range(2):
                g3 = [route[:, c, lo:lo + 4].rearrange("p (g a) -> p g a", a=1).to_broadcast([P, NG, EPG])
                      for lo in (48, 52)]
                el = route[:, c, 4:36].rearrange("p (g e) -> p g e", e=EPG)
                ml = route[:, c, 64:96].rearrange("p (g e) -> p g e", e=EPG)
                st.link(V.tensor_tensor(ml, el, g3[0], ALU.mult))
                st.link(V.tensor_tensor(ml, ml, g3[1], ALU.add))
            first_best(64, 32, 192, 96, 128)
            st.link(V.scalar_tensor_tensor(out=R(224, 32), in0=R(128, 32), scalar=2.0 * NEG, in1=R(64, 32),
                                           op0=ALU.mult, op1=ALU.add))
            first_best(224, 32, 194, 96, 160)
            V.tensor_tensor(R(200, 1), R(194, 1), R(192, 1), ALU.subtract).then_inc(rt_max, 1)
            dve.wait_ge(rt_exp, 2)
            st.link(V.tensor_reduce(R(202, 1), R(44, 4), AXX, ALU.add))
            st.link(V.tensor_scalar_add(R(203, 1), R(201, 1), 1.0))
            st.link(V.tensor_tensor(R(202, 1), R(202, 1), R(203, 1), ALU.mult))
            st.link(V.reciprocal(R(204, 1), R(202, 1)))
            st.link(V.tensor_tensor(R(205, 1), R(204, 1), R(201, 1), ALU.mult))
            st.done(V.tensor_tensor(R(320, 32), R(128, 32), R(160, 32), ALU.add))
            st.done(V.tensor_tensor(R(64, 32), R(128, 32), wide(204, 32), ALU.mult))
            st.link(V.tensor_tensor(R(96, 32), R(160, 32), wide(205, 32), ALU.mult))
            V.tensor_tensor(R(288, 32), R(64, 32), R(96, 32), ALU.add).then_inc(rt_gate, 1)
            dve.wait_ge(counted, 1)
            st.link(V.tensor_reduce(small[:, 0:1], B[3][:, 2 * NE:3 * NE], AXX, ALU.max))
            V.tensor_copy(peak[:], small[:, 0:1]).then_inc(peak_in, 1)
            dve.wait_ge(rt_gate, 1)
            st.settled()
            st.link(V.tensor_tensor(R(0, 32), B[3][:, 0:2 * NE].rearrange("p (c e) -> p c e", e=NE), R(320, 32), ALU.mult))
            st.link(V.tensor_scalar(R(0, 32), R(0, 32), -1.0, CAP + 1.0, ALU.mult, ALU.add))

            def moe_gathered():
                def of_expert(lo, c):
                    return route[:, c, lo:lo + NE].rearrange("p (e a) -> p e a", a=1).to_broadcast([P, NE, CAP])

                for c in range(2):
                    s3_, g3_ = (x[:, c, :].rearrange("p (e s) -> p e s", s=CAP) for x in (slots, gated_slots))
                    st.link(V.tensor_tensor(s3_, rep(col("first_wins", 0, CAP), NE), of_expert(0, c), ALU.is_equal))
                    ins = V.tensor_tensor(g3_, s3_, of_expert(288, c), ALU.mult)
                ins.then_inc(slots_in, 1)
                dve.wait_ge(slots_turned, 1)
                for n in range(4):
                    ins = V.tensor_copy(slots_T[:, n * 512:(n + 1) * 512], OUTB[n][:, :])
                ins.then_inc(slots_T_in, 1)
                with dve.Fori(0, NE // QUAD) as r:
                    dve.wait_ge(gather_sum, r + 1)
                    V.tensor_copy(gathered[:, 0:4, :].rearrange("p k s -> p (k s)"), B[6][:, :]).then_inc(gather_dve, 1)
                    for e in range(QUAD):
                        dve.wait_ge(ex_gu, r * QUAD + (e + 1))
                        V.tensor_copy(partial[:, 1, :], B[1][:, :]).then_inc(part_in[1], 1)
                        x, sg, a = expg[:, 0, 0:P], gate_r[:, 0, 0:P], act[:, 0, 0:P]
                        sg3, a3 = (t.rearrange("p (m s) -> p m s", s=CAP) for t in (sg, a))
                        dve.wait_ge(ex_exp, r * QUAD + (e + 1))
                        V.tensor_scalar_add(x, x, 1.0).then_inc(ex_step, 1)
                        dve.wait_ge(ex_step, r * (3 * QUAD) + 3 * e + 1)
                        V.reciprocal(sg, x).then_inc(ex_step, 1)
                        dve.wait_ge(ex_step, r * (3 * QUAD) + 3 * e + 2)
                        V.tensor_tensor(sg3, turned_part(0), sg3, ALU.mult).then_inc(ex_step, 1)
                        dve.wait_ge(ex_step, r * (3 * QUAD) + 3 * e + 3)
                        V.tensor_tensor(a3, turned_part(1), sg3, ALU.mult).then_inc(ex_act, 1)
                    dve.wait_ge(ex_down, r + 1)
                    V.tensor_copy(y_slots[:, 0:512], B[4][:, :]).then_inc(y_dve, 1)
                    dve.wait_ge(ex_scatter, r + 1)
                    for i in range(4):
                        add_residual(B[i], i, 1.0, ex_added if i == 3 else None)
                dve.wait_ge(ex_added, NE // QUAD)
                dve.sem_inc(h_ready, 1)

            def moe_dense():
                for i in range(NE // 2):
                    dve.wait_ge(rt_rows, i + 1)
                    V.tensor_copy(gate_rows[:, i * 512:(i + 1) * 512], B[4 + i % 2][:, :]).then_inc(rt_free, 1)
                dve.wait_ge(rt_free, NE // 2)
                with dve.Fori(0, NE) as r:
                    for j in range(EC):
                        i = GU["moe"] + j
                        silu_times_up(j % 2, r * EC + (i + 1), 5 * GU["moe"] + 4 * j, r * (4 * EC),
                                      gate_rows[:, bass.ds(r * T, T)])
                dve.wait_ge(acc_ready, len(FFNS) + 1)
                for i in range(4):
                    add_residual(OUTB[i], i, 1.0, h_ready if i == 3 else None)

            most = dve.value_load(peak[0:1, 0:1])
            with dve.If(most < CAP + 1):
                moe_gathered()
            with dve.Else():
                moe_dense()
            norm_apply("final", h, KD, "g_final", hn)


def _tiles(w):
    k, m = w.shape
    return w.reshape(k // P, P, m // P, P).transpose(2, 0, 1, 3).reshape(-1, P, P)


def _chunks(tiles):
    n = len(tiles)
    c = chunks_of(n)
    if c * CT > n:
        tiles = np.concatenate([tiles, np.zeros((c * CT - n, P, P), tiles.dtype)])
    return np.ascontiguousarray(tiles.reshape(c, CT, P, P).transpose(0, 2, 1, 3)).reshape(c, P, CT * P)


def _widen(w, width):
    k = w.shape[0]
    w = w.reshape(k, -1, width)
    return np.concatenate([w, np.zeros((k, w.shape[1], P - width), w.dtype)], axis=2).reshape(k, -1)


def _gated(w_gate, w_up, w_down, n):
    gate, up = _tiles(w_gate).reshape(n, KD, P, P), _tiles(w_up).reshape(n, KD, P, P)
    down = w_down.reshape(n, P, KD, P).transpose(0, 2, 1, 3)
    none = np.zeros((1, KD, P, P), gate.dtype)
    parts = [np.concatenate([gate, none]), np.concatenate([up, none]), np.concatenate([none, down])]
    return _chunks(np.concatenate(parts, axis=1).reshape(-1, P, P))


def _wide(w):
    k = w.shape[0]
    return w.reshape(k // P, P, 2, 4, P).transpose(2, 0, 3, 1, 4).reshape(-1, P, P)


def kernel(**inputs):
    import concourse.bacc as bacc
    from concourse.bass_utils import run_bass_kernel_spmd

    a = {k: np.asarray(v) for k, v in inputs.items()}

    def ffn(which, layer):
        w = a[f"{which}_w_in"][layer]
        return _gated(w[:, :FF], w[:, FF:], a[f"{which}_w_out"][layer], FFC)

    def ple(layer):
        gate = _tiles(a["ple_w_gate"][layer]).reshape(KD, KD, P, P)
        proj = _tiles(a["ple_w_proj"][layer]).reshape(KD, 2, P, P)
        return _chunks(np.concatenate([gate, proj], axis=1).reshape(-1, P, P))

    w = a["mla_w_in"][0]
    k_pe = np.concatenate([np.zeros((D, NOPE), w.dtype), w[:, QR + KVR:], np.zeros((D, P - QK), w.dtype)], axis=1)
    mla_in = _chunks(_tiles(np.concatenate([w[:, :QR + KVR], k_pe], axis=1)))
    mla_q = _chunks(_tiles(_widen(a["mla_w_uq"][0], QK)))
    ukv = a["mla_w_ukv"][0].reshape(KVR, H, NOPE + DV)
    mla_kv = _chunks(np.concatenate([_tiles(ukv[:, :, :NOPE].reshape(KVR, -1)), _wide(ukv[:, :, NOPE:].reshape(KVR, -1))]))
    fox = a["fox_w_in"][0]
    w2 = a["w_in_2"][0]
    order = [0, 2, 1, 3, 4, 5, 6]
    mix_in = np.concatenate([w2[:, 512 * i:512 * (i + 1)] for i in order], axis=1)
    def rows_of(w):
        e, k, m = w.shape
        return w.reshape(e, k // P, P, m // P, P).transpose(0, 1, 3, 2, 4)

    gate_up = np.concatenate([rows_of(a["w_gate_2"][0]), rows_of(a["w_up_2"][0])], axis=2).reshape(NE, -1, P, P)
    moe = _chunks(np.concatenate([gate_up, rows_of(a["w_down_2"][0]).reshape(NE, -1, P, P)], axis=1).reshape(-1, P, P))
    weights = np.concatenate([
        ffn("ffn1", 0), mla_in, mla_q, mla_kv, _chunks(_tiles(a["mla_w_o"][0])), ffn("ffn2", 0), ple(0),
        ffn("ffn1", 1), _chunks(_tiles(fox[:, :2048])), _chunks(_wide(fox[:, 2048:3072])),
        _chunks(_tiles(a["fox_w_o"][0])), ffn("ffn2", 1), ple(1),
        _chunks(_tiles(mix_in)), _chunks(_tiles(a["w_out_2"][0])), moe])
    assert weights.shape[0] == N_CHUNKS

    def cols(v):
        return v.reshape(-1, P).T

    def fill(v):
        return np.concatenate([v, np.zeros(P - len(v), v.dtype)])[:, None]

    def rows(v):
        return np.broadcast_to(v[None, :], (P, len(v)))

    def packed(v):
        return v.reshape(KD, P, -1).transpose(1, 0, 2).reshape(P, -1)

    f32 = np.float32
    half = ROPE // 2
    inv = (f32(10000.0) ** (-np.arange(0, ROPE, 2, dtype=f32) / f32(ROPE))).astype(f32)
    values = {
        "g_q_lat": cols(a["mla_g_q_lat"][0]), "g_kv_lat": cols(a["mla_g_kv_lat"][0]),
        "mla_qn": fill(a["mla_g_qn"][0]), "mla_kn": fill(a["mla_g_kn"][0]),
        "fox_qn": np.concatenate([a["fox_g_qn"][0]] * 2)[:, None],
        "fox_kn": np.concatenate([a["fox_g_kn"][0]] * 2)[:, None],
        "g_mix2": cols(a["mix_norm_g_2"][0]),
        "conv_a_w": np.concatenate([cols(a["conv_a_w_2"][0, j]) for j in range(3)], axis=1),
        "conv_a_g": cols(a["conv_a_norm_g_2"][0]),
        "dn_conv_w": np.concatenate([cols(a["dn_conv_w_2"][0, j]) for j in range(4)], axis=1),
        "dn_g": a["dn_norm_g_2"][0][:, None], "g_ffn_2": cols(a["ffn_norm_g_2"][0]),
        "g_final": cols(a["final_norm_g_2"]),
        "inv_freq": np.tile(inv, P // half)[:, None],
        "rope_sign": np.tile(np.repeat(np.array([-1.0, 1.0], f32), half), P // ROPE)[:, None],
        "b_f": rows(a["fox_b_f"][0]), "a_log": rows(a["dn_a_log_2"][0]), "dt_bias": rows(a["dn_dt_bias_2"][0]),
        "w_f": packed(fox[:, 3072:]), "w_ba": packed(w2[:, 3584:]),
        "w_router": packed(np.concatenate([a["router_group_w_2"][0], a["router_expert_w_2"][0]], axis=1)),
        "first_wins": np.broadcast_to(np.arange(32, 0, -1, dtype=f32)[None, :], (P, 32)),
    }
    for layer in range(DEPTH):
        for g in ("ffn1", "mix", "ffn2", "ple"):
            values[f"g_{g}_{layer}"] = cols(a[f"g_{g}"][layer])
    par = np.ascontiguousarray(np.concatenate([values[n] for n, _ in PARAMS], axis=1).astype(f32))

    def feature_major(x):
        return np.ascontiguousarray(x.T.reshape(-1, P, T).transpose(1, 0, 2))

    arrays = {
        "xT": feature_major(a["x"][0]),
        "pT": np.ascontiguousarray(np.concatenate([feature_major(a["p"][i, 0]) for i in range(DEPTH)], axis=1)),
        "pos": np.ascontiguousarray(np.broadcast_to(a["positions"], (P, T))),
        "par": par, "weights": weights,
    }
    nc = bacc.Bacc("TRN2", target_bir_lowering=False, num_devices=1)
    aps = [nc.dram_tensor(n, v.shape, mybir.dt.from_np(v.dtype), kind="ExternalInput").ap() for n, v in arrays.items()]
    out = nc.dram_tensor("outT", (P, KD, T), F32, kind="ExternalOutput").ap()
    two_block_kernel(nc, *aps, out)
    r = run_bass_kernel_spmd(nc, [arrays], core_ids=[0])
    y = np.asarray(r.results[0]["outT"])
    return np.ascontiguousarray(y.transpose(1, 0, 2).reshape(D, T).T)[None]
```

```python
from contextlib import ExitStack

import numpy as np
import concourse.bass as bass
from concourse import mybir

P = 128
T = 256
D = 1024
KD = D // P
DEPTH = 2
FF = 2816
FFC = FF // P
PLE = 256
EPS = 1e-6
H = 16
QR, KVR, NOPE, ROPE, DV = 512, 256, 64, 32, 64
QK = NOPE + ROPE
DNH = 4
CG = 512
NE, NG, EPG, EFF = 32, 4, 8, 512
EC = EFF // P
EXPERT_TILES = 3 * KD * EC
CAP = 32
QUAD = P // CAP
CT = 24
RING = 4
HIGH = 2
NEG = -1.0e30

F32 = mybir.dt.float32
F32R = mybir.dt.float32r
I32 = mybir.dt.int32
ALU = mybir.AluOpType
ACT = mybir.ActivationFunctionType
AXX = mybir.AxisListType.X


def chunks_of(tiles):
    return -(-tiles // CT)


def stream_plan():
    sizes = []
    for layer in range(DEPTH):
        sizes.append((f"ffn1_{layer}", FFC + 1))
        if layer == 0:
            sizes += [("mla_in", chunks_of(7 * KD)), ("mla_q", chunks_of(H * 4)), ("mla_kv", chunks_of(32)),
                      ("mla_o", chunks_of(64))]
        else:
            sizes += [("fox_qk", chunks_of(128)), ("fox_v", chunks_of(64)), ("fox_o", chunks_of(64))]
        sizes += [(f"ffn2_{layer}", FFC + 1), (f"ple_{layer}", chunks_of(80))]
    sizes += [("mix_in", chunks_of(28 * KD)), ("mix_out", chunks_of(64)), ("moe", NE * EC)]
    plan, at = {}, 0
    for name, n in sizes:
        plan[name] = at
        at += n
    return plan, at


PLAN, N_CHUNKS = stream_plan()

PARAMS = [("g_ffn1_0", 8), ("g_mix_0", 8), ("g_ffn2_0", 8), ("g_ple_0", 8), ("g_ffn1_1", 8), ("g_mix_1", 8),
          ("g_ffn2_1", 8), ("g_ple_1", 8), ("g_q_lat", 4), ("g_kv_lat", 2), ("mla_qn", 1), ("mla_kn", 1),
          ("fox_qn", 1), ("fox_kn", 1), ("g_mix2", 8), ("conv_a_w", 12), ("conv_a_g", 4), ("dn_conv_w", 48),
          ("dn_g", 1), ("g_ffn_2", 8), ("g_final", 8), ("inv_freq", 1), ("rope_sign", 1), ("b_f", 16),
          ("a_log", 4), ("dt_bias", 4), ("w_f", 128), ("w_ba", 64), ("w_router", 8 * 36), ("first_wins", 32)]
COL, NPAR = {}, 0
for _name, _n in PARAMS:
    COL[_name] = NPAR
    NPAR += _n

LIN, _at = {}, 0
for _name, _n in [("mla_in", 4), ("mla_q", 8), ("mla_k", 8), ("mla_v", 4), ("mla_o", 4), ("ple_0", 8),
                  ("fox_qk", 8), ("fox_v", 4), ("fox_o", 4), ("ple_1", 8), ("mix_in", 14), ("mix_out", 4)]:
    LIN[_name] = _at
    _at += _n

HN = {"mla_q": 0, "mla_k": 8, "fox_qk": 16, "conv_a": 24, "dn_q": 26, "dn_k": 28, "dn_o": 30}
NORM = {n: i for i, n in enumerate(["ffn1_0", "mix_0", "q_lat", "kv_lat", "ffn2_0", "ple_0", "ffn1_1", "mix_1",
                                    "ffn2_1", "ple_1", "mix2", "ffn_2", "final"])}
WHOLE = [n for n in NORM if n not in ("ffn1_0", "ffn2_0", "ffn1_1", "ffn2_1")]
SPLIT_AT, _at = {}, 0
for _name, _n in [("ffn1_0", FFC + 1), ("ffn2_0", FFC + 1), ("ffn1_1", FFC + 1), ("fox_qk", chunks_of(128)),
                  ("fox_v", chunks_of(64)), ("ffn2_1", FFC + 1), ("mix_in", chunks_of(28 * KD))]:
    SPLIT_AT[_name] = _at
    _at += _n
X_AT = {n: i * KD for i, n in enumerate(["ffn1_0", "ffn2_0", "ffn1_1", "mix_1", "ffn2_1", "mix2"])}
FFNS = ["ffn1_0", "ffn2_0", "ffn1_1", "ffn2_1"]
GU = {"ffn1_0": 0, "ffn2_0": FFC, "ffn1_1": 2 * FFC, "ffn2_1": 3 * FFC, "moe": 4 * FFC}
SQ_AT, OUT_AT, _sq, _out = {}, {}, 0, 0
for _name in NORM:
    SQ_AT[_name], OUT_AT[_name] = _sq, _out
    _n = {"q_lat": 4, "kv_lat": 2}.get(_name, KD)
    _sq += _n // 2
    _out += _n if _name in WHOLE else 0
H_AT = {"mix_0": 0, "ple_0": 4, "ffn1_1": 8, "mix_1": 12, "ple_1": 16, "mix2": 20, "final": 24}
TWO_PI = 6.283185307179586
PI2_A = 6.28125
PI2_B = 0.0019350051879882812
PI2_C = TWO_PI - PI2_A - PI2_B
ROUND = 1.5 * 2 ** 23


class Steps:

    def __init__(self, eng, sem):
        self.eng, self.sem, self.n = eng, sem, 0

    def done(self, ins):
        self.n += 1
        ins.then_inc(self.sem, 1)

    def settled(self):
        self.eng.wait_ge(self.sem, self.n)

    def link(self, ins):
        self.done(ins)
        self.settled()


def two_block_kernel(nc, xT, pT, pos, par, weights, out):
    with ExitStack() as ctx:
        def sb(name, shape, dt=F32):
            return ctx.enter_context(nc.sbuf_tensor("sb_" + name, shape, dt))

        def rounded_view(name, shape):
            with nc.sbuf_tensor("sb_" + name, shape, F32R) as view:
                return view

        def sem(name):
            return ctx.enter_context(nc.semaphore(name))

        ring_lo = rounded_view("ring_lo", [P, RING, CT * P])
        ring = sb("ring", [P, RING, CT * P])
        high = sb("high", [P, HIGH, CT * P], F32R)
        act_hi = sb("act_hi", [P, 2, T], F32R)
        h = sb("h", [P, KD, T])
        x_hi = rounded_view("x_hi", [P, KD, T])
        hn = sb("hn", [P, KD, T])
        x_lo = rounded_view("x_lo", [P, KD, T])
        sq = sb("sq", [P, KD, T])
        lnv = sb("lnv", [P, 2, 2 * T])
        rstd = sb("rstd", [P, 2, T])
        params = sb("params", [P, NPAR])
        pin = sb("pin", [P, 2 * DEPTH, T])
        ones = sb("ones", [P, P])
        ones64 = sb("ones64", [P, P])
        ident = sb("ident", [P, P])
        stack = sb("stack", [P, P])
        upper = sb("upper", [P, P])
        mask = sb("mask", [P, 3 * P])
        eps_col = sb("eps_col", [P, 1])
        level = sb("level", [P, 7, P])
        expg = sb("expg", [P, 2, T])
        gate_r = sb("gate_r", [P, 2, T])
        act_lo = rounded_view("act_lo", [P, 2, T])
        act = sb("act", [P, 2, T])
        qk = sb("qk", [P, 2 * H, T])
        qT, kT = qk[:, 0:H, :], qk[:, H:2 * H, :]
        v_tok = sb("v_tok", [P, 2, D])
        oT = sb("oT", [P, KD, T])
        sqh = sb("sqh", [P, 2, 2, T])
        rsh = sb("rsh", [P, 2, 2 * T])
        cosr = sb("cosr", [P, T])
        sinr = sb("sinr", [P, T])
        kpe, kr = gate_r[:, 0, :], gate_r[:, 1, :]
        gq = sb("gq", [P, 4])
        attn = sb("attn", [P, 18 * P + 4 * T + H * P])
        logits, probs, pT_sb = (attn[:, i * 6 * P:(i + 1) * 6 * P].rearrange("p (b n) -> p b n", b=2) for i in range(3))
        rope_t = attn[:, 18 * P:18 * P + 4 * T].rearrange("p (b n) -> p b n", b=2)
        head_row = attn[0:H, 18 * P + 4 * T:18 * P + 4 * T + H * P].rearrange("p (h n) -> p h n", n=P)
        scratch = attn
        nmax = sb("nmax", [P, 2 * H, 2])
        psums = sb("psums", [P, 2 * H, 2])
        small = sb("small", [P, 512])
        ndec = sb("ndec", [H, T])
        dtok = sb("dtok", [P, 2, H])
        route = sqh[:, :, :, :].rearrange("p a b t -> p (a b t)")[:, 0:2 * 352].rearrange("p (c n) -> p c n", c=2)
        peak = sb("peak", [P, 1], I32)

        posi = v_tok[:, 0, 0:T].bitcast(I32)
        cq = oT[:, 0:4, :]
        ckv = oT[:, 4:6, :]
        PADQ = T + 3
        PADU = T + 2
        gate_rows = qk[:, :, :].rearrange("p e t -> p (e t)")
        slots = gate_rows[:, 0:2048].rearrange("p (c s) -> p c s", c=2)
        gated_slots = gate_rows[:, 2048:4096].rearrange("p (c s) -> p c s", c=2)
        slots_T = gate_rows[:, 4096:6144]
        gathered = gate_rows[:, 6144:7168].rearrange("p (k s) -> p k s", s=P)
        y_slots = gate_rows[:, 7168:8192]
        h_tok = v_tok
        partial = sq[:, 0:4, :].rearrange("p a t -> p (a t)").rearrange("p (b n) -> p b n", b=2)
        qkv_pad = scratch[:, 0:12 * PADQ].rearrange("p (n t) -> p n t", t=PADQ)
        u_pad = scratch[:, 12 * PADQ:12 * PADQ + 4 * PADU].rearrange("p (n t) -> p n t", t=PADU)
        a_h = qT[:, 0:4, :]
        a_b = qT[:, 4:8, :]
        z_gate = qT[:, 8:12, :]
        y_a = qT[:, 12:16, :]
        qkv = kT[:, 0:12, :]
        convt = kT[:, 12:16, :]
        mixT = oT

        B = [ctx.enter_context(nc.psum_tensor(f"bank{i}", [P, 512], F32)) for i in range(8)]
        OUTB = B[4:8]

        def turned_part(part):
            return B[2 + part][:, :].rearrange("p (m s) -> p m s", s=P)[:, :, 0:CAP]


        par_in, x_in, p_in, pos_in = sem("par_in"), sem("x_in"), sem("p_in"), sem("pos_in")
        slot_in = [sem(f"slot_in{j}") for j in range(RING)]
        ring_free = sem("ring_free")
        consts = sem("consts")
        pool_step = sem("pool_step")
        act_step = sem("act_step")
        dve_step = sem("dve_step")
        h_ready = sem("h_ready")
        norm_sq, norm_sum, norm_rstd, norm_out = sem("norm_sq"), sem("norm_sum"), sem("norm_rstd"), sem("norm_out")
        high_in, low_in, x_full, x_high, x_low, act_parts = (
            sem("high_in"), sem("low_in"), sem("x_full"), sem("x_high"), sem("x_low"), sem("act_parts"))
        gu_ready, sig_ready, glu_step, act_ready, acc_ready = (
            sem("gu_ready"), sem("sig_ready"), sem("glu_step"), sem("act_ready"), sem("acc_ready"))
        lin_ready, lin_free = sem("lin_ready"), sem("lin_free")
        hn_src, hn_sq, hn_sum, hn_rs, hn_done = sem("hn_src"), sem("hn_sq"), sem("hn_sum"), sem("hn_rs"), sem("hn_done")
        rope_arg, rope_sin = sem("rope_arg"), sem("rope_sin")
        scores, masked, expd, rcpd, prob_ready = sem("scores"), sem("masked"), sem("expd"), sem("rcpd"), sem("prob_ready")
        turned, pt_ready, pv_done, o_ready = sem("turned"), sem("pt_ready"), sem("pv_done"), sem("o_ready")
        f_ready, f_abs, f_ln, logf_ready, dec_sum, dec_ready = (
            sem("f_ready"), sem("f_abs"), sem("f_ln"), sem("logf_ready"), sem("dec_sum"), sem("dec_ready"))
        ple_e = sem("ple_e")
        silu_in, silu_e, z_exp = sem("silu_in"), sem("silu_e"), sem("z_exp")
        ba_ready, ba_abs, ba_ln, bg_ready = sem("ba_ready"), sem("ba_abs"), sem("ba_ln"), sem("bg_ready")
        rows_ready, gdiff, gdecay, dn_qk, dn_ready = (
            sem("rows_ready"), sem("gdiff"), sem("gdecay"), sem("dn_qk"), sem("dn_ready"))
        tok_ready, tok_scaled = sem("tok_ready"), sem("tok_scaled")
        inv_p, inv_p_sb, inv_x, inv_done = sem("inv_p"), sem("inv_p_sb"), sem("inv_x"), sem("inv_done")
        dn_pe, dn_sb = sem("dn_pe"), sem("dn_sb")
        mix_ready = sem("mix_ready")
        rt_ready, rt_max, rt_exp, rt_gate, rt_rows, rt_free = (
            sem("rt_ready"), sem("rt_max"), sem("rt_exp"), sem("rt_gate"), sem("rt_rows"), sem("rt_free"))
        turn_h, h_tok_in, counted, slots_in, slots_turned, slots_T_in, peak_in = (
            sem("turn_h"), sem("h_tok_in"), sem("counted"), sem("slots_in"), sem("slots_turned"), sem("slots_T_in"),
            sem("peak_in"))
        gather_sum, gather_act, gather_dve = sem("gather_sum"), sem("gather_act"), sem("gather_dve")
        ex_gu, ex_exp, ex_step, ex_act, y_act, y_dve, ex_scatter, ex_added = (
            sem("ex_gu"), sem("ex_exp"), sem("ex_step"), sem("ex_act"), sem("y_act"), sem("y_dve"),
            sem("ex_scatter"), sem("ex_added"))
        part_in, ex_turned = [sem("part_in_gate"), sem("part_in_up")], sem("ex_turned")
        out_done = sem("out_done")

        def col(name, i=0, n=1):
            return params[:, COL[name] + i:COL[name] + i + n]

        def rep(ap, n):
            return ap.rearrange("p (a t) -> p a t", a=1).to_broadcast([ap.shape[0], n, ap.shape[1]])

        silu_tmp = [v_tok[:, 0, :].rearrange("p (n t) -> p n t", t=T), v_tok[:, 1, :].rearrange("p (n t) -> p n t", t=T),
                    mixT[:, 4:8, :]]
        vflat = v_tok[:, :, :].rearrange("p a n -> p (a n)")
        DELTA = {
            "decay": sq[:, 0:4, :].rearrange("p a t -> p (a t)").rearrange("p (c t) -> p c t", t=P),
            "brow": sq[:, 4:8, :].rearrange("p a t -> p (a t)").rearrange("p (c t) -> p c t", t=P),
            "lt": hn[:, 0:4, :].rearrange("p a t -> p (a t)").rearrange("p (c t) -> p c t", t=P),
            "intra": hn[:, 4:8, :].rearrange("p a t -> p (a t)").rearrange("p (c t) -> p c t", t=P),
            "x": vflat[:, 0:1024].rearrange("p (c t) -> p c t", t=P),
            "xt": vflat[:, 1024:2048].rearrange("p (c t) -> p c t", t=P),
            "lw": pin[:, :, :].rearrange("p a t -> p (a t)").rearrange("p (c t) -> p c t", t=P),
            "pm": mixT[:, 4:8, :].rearrange("p a t -> p (a t)").rearrange("p (c t) -> p c t", t=P),
            "vb": scratch[:, 4200:5224].rearrange("p (c t) -> p c t", t=P),
            "vn": scratch[:, 0:1024].rearrange("p (c t) -> p c t", t=P),
            "kd": scratch[:, 1024:1536].rearrange("p (c t) -> p c t", t=P),
            "state": scratch[:, 1536:2048].rearrange("p (c t) -> p c t", t=P),
            "qd": scratch[:, 2048:2560].rearrange("p (c t) -> p c t", t=P),
            "egrow": scratch[:, 2560:3072].rearrange("p (c t) -> p c t", t=P),
        }

        block = ctx.enter_context(nc.Block())

        @block.sync
        def _(sp):
            sp.dma_start(params[:], par).then_inc(par_in, 16)
            sp.dma_start(posi, pos).then_inc(pos_in, 16)
            sp.dma_start(h[:], xT).then_inc(x_in, 16)
            for j in range(RING):
                sp.dma_start(ring[:, j, :], weights[j]).then_inc(slot_in[j], 16)
            sp.dma_start(pin[:], pT).then_inc(p_in, 16)
            whole = N_CHUNKS // RING
            with sp.Fori(1, whole) as r:
                for j in range(RING):
                    sp.wait_ge(ring_free, r * RING + (j - RING + 1))
                    sp.dma_start(ring[:, j, :], weights[r * RING + j]).then_inc(slot_in[j], 16)
            for n in range(whole * RING, N_CHUNKS):
                sp.wait_ge(ring_free, n - RING + 1)
                sp.dma_start(ring[:, n % RING, :], weights[n]).then_inc(slot_in[n % RING], 16)
            sp.wait_ge(norm_out, OUT_AT["final"] + KD)
            sp.dma_start(out, hn[:]).then_inc(out_done, 16)
            sp.wait_ge(out_done, 16)

        @block.gpsimd
        def _(pool):
            st = Steps(pool, pool_step)
            st.link(nc.gpsimd.memset(eps_col[:], EPS))
            nc.gpsimd.memset(ones[:], 1.0).then_inc(consts, 1)
            for t, v in ((ones64, 0.0), (ident, 0.0), (stack, 0.0), (upper, 1.0), (mask, 0.0), (level, 1.0)):
                st.done(nc.gpsimd.memset(t[:], v))
            st.link(nc.gpsimd.memset(head_row, 0.0))
            st.settled()
            for g in range(2):
                st.link(nc.gpsimd.memset(ones64[64 * g:64 * g + 64, 64 * g:64 * g + 64], 1.0))
            st.link(nc.gpsimd.affine_select(out=ident[:], in_=ident[:], compare_op=ALU.not_equal, fill=1.0, base=0,
                                            pattern=[[-1, P]], channel_multiplier=1))
            for i in range(1 - QUAD, QUAD):
                st.link(nc.gpsimd.affine_select(out=stack[:], in_=stack[:], compare_op=ALU.not_equal, fill=1.0,
                                                base=CAP * i, pattern=[[-1, P]], channel_multiplier=1))
            st.link(nc.gpsimd.affine_select(out=upper[:], in_=upper[:], compare_op=ALU.is_ge, fill=0.0, base=0,
                                            pattern=[[1, P]], channel_multiplier=-1))
            for c in (0, 2):
                m = mask[:, c * P:(c + 1) * P]
                st.link(nc.gpsimd.affine_select(out=m, in_=m, compare_op=ALU.is_ge, fill=NEG, base=0,
                                                pattern=[[-1, P]], channel_multiplier=1))
            st.link(nc.gpsimd.affine_select(out=head_row, in_=head_row, compare_op=ALU.not_equal, fill=1.0,
                                            base=0, pattern=[[-1, H], [0, P]], channel_multiplier=1))
            for i in range(7):
                w = 1 << i
                v = level[:, i, :].rearrange("p (b a r) -> p b a r", a=2, r=w)
                st.link(nc.gpsimd.memset(v[:, :, 0, :], 0.0))
                up = v[:, :, 1, :]
                st.link(nc.gpsimd.affine_select(out=up, in_=up, compare_op=ALU.is_ge, fill=0.0, base=0,
                                                pattern=[[-2 * w, P // (2 * w)], [0, w]], channel_multiplier=1))
                st.link(nc.gpsimd.affine_select(out=up, in_=up, compare_op=ALU.is_ge, fill=0.0, base=w - 1,
                                                pattern=[[2 * w, P // (2 * w)], [0, w]], channel_multiplier=-1))
            st.settled()
            nc.gpsimd.memset(small[:, 511:512], 0.0).then_inc(consts, 1)

        @block.tensor
        def _(pe):
            owed = [0]

            def mm(o, l, r, start, stop, inc=None):
                ins = nc.tensor.matmul(o, l, r, start=start, stop=stop, skip_group_check=True)
                if inc is not None:
                    ins.then_inc(inc, 1)
                elif owed[0]:
                    ins.then_inc(ring_free, owed[0])
                    owed[0] = 0
                return ins

            def chunk_in(n):
                pe.wait_ge(slot_in[n % RING], 16 * (n // RING + 1))

            def tile(n, i, c0=0, c1=P):
                return ring[:, n % RING, i * P + c0:i * P + c1]

            def three(o, l, r, start, stop, inc=None):
                mm(o, l[0], r[0], start, False)
                mm(o, l[0], r[1], False, False)
                mm(o, l[1], r[0], False, stop, inc)

            def split_tile(n, i, width=1):
                return high[:, n % HIGH, i * P:(i + width) * P], ring_lo[:, n % RING, i * P:(i + width) * P]

            def split_x(k, c0=0, c1=T):
                return x_hi[:, k, c0:c1], x_lo[:, k, c0:c1]

            class Tiles:

                def __init__(self, name, split=False):
                    self.at, self.i, self.name, self.split = PLAN[name], 0, name, split

                def next(self, c0=0, c1=P, width=1, hold=False):
                    n, i = self.at + self.i // CT, self.i % CT
                    if self.split:
                        if i == 0:
                            pe.wait_ge(low_in, SPLIT_AT[self.name] + self.i // CT + 1)
                        self.i += width
                        return split_tile(n, i, width)
                    if i == 0:
                        chunk_in(n)
                    self.i += width
                    return ring[:, n % RING, i * P + c0:(i + width - 1) * P + c1]

                def used(self):
                    if self.i % CT == 0:
                        owed[0] += 1

                def end(self):
                    if self.i % CT:
                        owed[0] += 1

            def norm_sums(name, nk):
                for k in range(nk):
                    if k % 2 == 0:
                        pe.wait_ge(norm_sq, SQ_AT[name] + k // 2 + 1)
                    mm(B[2][:, 0:T], ones[:], sq[:, k, :], k == 0, k == nk - 1, norm_sum if k == nk - 1 else None)

            def normed(name, k=KD - 1):
                pe.wait_ge(norm_out, OUT_AT[name] + k + 1)

            def bank_free(g):
                if g >= 4:
                    pe.wait_ge(lin_free, g - 3)
                return OUTB[g % 4]

            def project(name, lin, groups, rhs, nk, per=2, cols=P, after=None):
                tl = Tiles(name)
                for g in range(groups[0], groups[1]):
                    bank = bank_free(LIN[lin] + g)
                    n_tiles = per(g) if callable(per) else per
                    for j in range(n_tiles):
                        for k in range(nk):
                            if after and g == groups[0] and j == 0:
                                normed(after, k)
                            mm(bank[0:cols, j * T:(j + 1) * T], tl.next(0, cols), rhs[:, k, :], k == 0, k == nk - 1,
                               lin_ready if k == nk - 1 and j == n_tiles - 1 else None)
                            tl.used()
                tl.end()

            def head_sums(g, lhsT, parts):
                pe.wait_ge(hn_sq, g + 1)
                if g >= 2:
                    pe.wait_ge(hn_rs, g - 1)
                mm(B[2 + g % 2][0:parts, :], lhsT, sqh[0:parts, g % 2, :, :].rearrange("p a t -> p (a t)"), True, True,
                   hn_sum)

            def gated(name):
                base, gu0, f = PLAN[name], GU[name], FFNS.index(name)

                def gate_up(slot, par, first):
                    for part in range(2):
                        for k in range(KD):
                            if first and part == 0:
                                pe.wait_ge(x_low, X_AT[name] + k + 1)
                            three(B[par][:, part * T:(part + 1) * T], split_tile(slot, part * KD + k), split_x(k),
                                  k == 0, k == KD - 1, gu_ready if part == 1 and k == KD - 1 else None)

                def down(slot, par, start, stop):
                    for m in range(KD):
                        inc = (acc_ready if stop else ring_free) if m == KD - 1 else None
                        three(OUTB[m // 2][:, (m % 2) * T:(m % 2 + 1) * T], split_tile(slot, 2 * KD + m),
                              (act_hi[:, par, :], act_lo[:, par, :]), start and m % 2 == 0, stop, inc)

                chunks0 = SPLIT_AT[name]
                pe.wait_ge(low_in, chunks0 + 1)
                gate_up(base, 0, True)
                owed[0] += 1
                pe.wait_ge(low_in, chunks0 + 2)
                gate_up(base + 1, 1, False)
                pe.wait_ge(act_parts, gu0 + 1)
                down(base + 1, 0, True, False)
                with pe.Fori(0, (FFC - 2) // RING) as r:
                    for j in range(RING):
                        c = 2 + j
                        pe.wait_ge(low_in, r * RING + (chunks0 + c + 1))
                        gate_up(base + c, c % 2, False)
                        pe.wait_ge(act_parts, r * RING + (gu0 + c))
                        down(base + c, (c - 1) % 2, False, False)
                pe.wait_ge(low_in, chunks0 + FFC + 1)
                pe.wait_ge(act_parts, gu0 + FFC)
                down(base + FFC, (FFC - 1) % 2, False, True)
                owed[0] += 1

            def attention(first, kq, fox):
                for i in range(H + 3):
                    if i < H:
                        a = first + i
                        if i >= 2:
                            pe.wait_ge(masked, a - 1)
                        s = B[a % 2]
                        for cols, q0, k1 in ((0, 0, P), (P, P, T)):
                            ql, kl = kq(i, q0, q0 + P, 0, k1)
                            mm(s[:, cols:cols + k1], ql, kl, True, not fox,
                               None if fox or cols == 0 else scores)
                            if fox:
                                mm(s[:, cols:cols + k1], head_row[:, i, :], ndec[:, 0:k1], False, True,
                                   None if cols == 0 else scores)
                    if 2 <= i <= H + 1:
                        a = first + i - 2
                        pe.wait_ge(prob_ready, a + 1)
                        for j in range(3):
                            ins = nc.tensor.transpose(B[2 + a % 2][:, j * P:(j + 1) * P],
                                                      probs[:, a % 2, j * P:(j + 1) * P], ident[:])
                        ins.then_inc(turned, 1)
                    if i >= 3:
                        hd = i - 3
                        a = first + hd
                        pair = a // 2
                        pe.wait_ge(pt_ready, a + 1)
                        if hd % 2 == 0 and hd >= 4:
                            pe.wait_ge(o_ready, pair - 1)
                        ob = B[4 + pair % 2]
                        lo = 64 * (hd % 2)
                        v0, v1 = (v_tok[:, c, hd * DV:(hd + 1) * DV] for c in range(2))
                        mm(ob[lo:lo + DV, 0:P], v0, pT_sb[:, a % 2, 0:P], True, True)
                        mm(ob[lo:lo + DV, P:T], v0, pT_sb[:, a % 2, P:2 * P], True, False)
                        mm(ob[lo:lo + DV, P:T], v1, pT_sb[:, a % 2, 2 * P:3 * P], False, True, pv_done)

            def ple(layer):
                name = f"ple_{layer}"
                norm_sums(name, KD)
                if layer == 0:
                    pe.wait_ge(p_in, 16)
                tl = Tiles(name)
                for m in range(KD):
                    bank = bank_free(LIN[name] + m)
                    for k in range(KD):
                        if m == 0:
                            normed(name, k)
                        mm(bank[:, 0:T], tl.next(), hn[:, k, :], k == 0, k == KD - 1)
                        tl.used()
                    for k in range(2):
                        mm(bank[:, T:2 * T], tl.next(), pin[:, 2 * layer + k, :], k == 0, k == 1,
                           lin_ready if k == 1 else None)
                        tl.used()
                tl.end()

            def values(name, lin, src, nk):
                tl = Tiles(name)
                tl.i = 0 if name != "mla_kv" else 16
                for half in range(2):
                    t0 = tl.i
                    w = []
                    for k in range(nk):
                        n, i = tl.at + tl.i // CT, tl.i % CT
                        if i == 0:
                            chunk_in(n)
                        w.append(ring[:, n % RING, i * P:(i + 4) * P])
                        tl.i += 4
                    for c in range(2):
                        bank = bank_free(LIN[lin] + 2 * half + c)
                        for k in range(nk):
                            mm(bank[:, :], src[:, k, c * P:(c + 1) * P], w[k], k == 0, k == nk - 1,
                               lin_ready if k == nk - 1 else None)
                    owed[0] += tl.i // CT - t0 // CT
                tl.end()

            pe.wait_ge(consts, 1)
            norm_sums("ffn1_0", KD)
            gated("ffn1_0")

            pe.wait_ge(consts, 2)
            norm_sums("mix_0", KD)
            project("mla_in", "mla_in", (0, 4), hn, KD, per=lambda g: 2 if g < 3 else 1, after="mix_0")
            norm_sums("q_lat", 4)
            norm_sums("kv_lat", 2)
            normed("q_lat", 3)
            tl = Tiles("mla_q")
            for g in range(9):
                if g < 8:
                    bank = bank_free(LIN["mla_q"] + g)
                    for j in range(2):
                        for k in range(4):
                            mm(bank[0:QK, j * T:(j + 1) * T], tl.next(0, QK), hn[:, k, :], k == 0, k == 3,
                               lin_ready if k == 3 and j == 1 else None)
                            tl.used()
                if g >= 1:
                    head_sums(HN["mla_q"] + g - 1, ones[0:QK, 0:QK], QK)
            tl.end()
            normed("kv_lat", 1)
            n = PLAN["mla_kv"]
            chunk_in(n)
            for g in range(9):
                if g < 8:
                    bank = bank_free(LIN["mla_k"] + g)
                    for j in range(2):
                        for k in range(2):
                            mm(bank[0:NOPE, j * T:(j + 1) * T], tile(n, 2 * g + k, 64 * j, 64 * j + NOPE),
                               hn[:, 4 + k, :], k == 0, k == 1, lin_ready if k == 1 and j == 1 else None)
                if g >= 1:
                    head_sums(HN["mla_k"] + g - 1, ones[0:QK, 0:QK], QK)
            values("mla_kv", "mla_v", hn[:, 4:6, :], 2)
            pe.wait_ge(lin_free, LIN["mla_v"] + 4)
            pe.wait_ge(hn_done, 16)
            attention(0, lambda i, q0, q1, k0, k1: (qT[0:QK, i, q0:q1], kT[0:QK, i, k0:k1]), False)
            pe.wait_ge(o_ready, 8)
            project("mla_o", "mla_o", (0, 4), oT, KD)

            norm_sums("ffn2_0", KD)
            gated("ffn2_0")
            ple(0)

            norm_sums("ffn1_1", KD)
            gated("ffn1_1")
            norm_sums("mix_1", KD)
            for c in range(2):
                for k in range(KD):
                    normed("mix_1", k)
                    mm(B[3][:, c * H:(c + 1) * H], oT[:, k, c * P:(c + 1) * P],
                       params[:, COL["w_f"] + k * H:COL["w_f"] + (k + 1) * H], k == 0, k == KD - 1,
                       f_ready if k == KD - 1 and c == 1 else None)
            pe.wait_ge(logf_ready, 1)
            lf = [small[:, c * H:(c + 1) * H] for c in range(2)]
            mm(B[3][:, 0:H], upper[:], lf[0], True, True)
            mm(B[3][:, H:2 * H], ones[:], lf[0], True, False)
            mm(B[3][:, H:2 * H], upper[:], lf[1], False, True)
            mm(B[3][0:H, P:2 * P], lf[0], upper[:], True, True)
            mm(B[3][0:H, 2 * P:3 * P], lf[0], ones[:], True, False)
            mm(B[3][0:H, 2 * P:3 * P], lf[1], upper[:], False, True, dec_sum)
            pe.wait_ge(dec_ready, 1)
            tl = Tiles("fox_qk", split=True)
            for g in range(9):
                if g < 8:
                    bank = bank_free(LIN["fox_qk"] + g)
                    for j in range(2):
                        for k in range(KD):
                            if g == 0 and j == 0:
                                pe.wait_ge(x_low, X_AT["mix_1"] + k + 1)
                            three(bank[:, j * T:(j + 1) * T], tl.next(), split_x(k), k == 0, k == KD - 1,
                                  lin_ready if k == KD - 1 and j == 1 else None)
                            tl.used()
                if g >= 1:
                    head_sums(HN["fox_qk"] + g - 1, ones64[:], P)
            tl.end()
            for half in range(2):
                for c in range(2):
                    bank = bank_free(LIN["fox_v"] + 2 * half + c)
                    for k in range(KD):
                        n, i = divmod(4 * (half * KD + k), CT)
                        if c == 0 and i == 0:
                            pe.wait_ge(low_in, SPLIT_AT["fox_v"] + n + 1)
                        three(bank[:, :], split_x(k, c * P, (c + 1) * P), split_tile(PLAN["fox_v"] + n, i, 4), k == 0,
                              k == KD - 1, lin_ready if k == KD - 1 else None)
                owed[0] += 1
            owed[0] += 1
            pe.wait_ge(lin_free, LIN["fox_v"] + 4)

            def fox_qk(i, q0, q1, k0, k1):
                lo = 64 * (i % 2)
                return qT[lo:lo + 64, i // 2, q0:q1], kT[lo:lo + 64, i // 2, k0:k1]

            attention(H, fox_qk, True)
            pe.wait_ge(o_ready, 16)
            project("fox_o", "fox_o", (0, 4), oT, KD)
            norm_sums("ffn2_1", KD)
            gated("ffn2_1")
            ple(1)

            norm_sums("mix2", KD)
            for c in range(2):
                for k in range(KD):
                    normed("mix2", k)
                    mm(B[3][:, c * 8:(c + 1) * 8], oT[:, k, c * P:(c + 1) * P],
                       params[:, COL["w_ba"] + k * 8:COL["w_ba"] + (k + 1) * 8], k == 0, k == KD - 1,
                       ba_ready if k == KD - 1 and c == 1 else None)
            tl = Tiles("mix_in", split=True)
            for g in range(14):
                bank = bank_free(LIN["mix_in"] + g)
                for j in range(2):
                    for k in range(KD):
                        if g == 0 and j == 0:
                            pe.wait_ge(x_low, X_AT["mix2"] + k + 1)
                        three(bank[:, j * T:(j + 1) * T], tl.next(), split_x(k), k == 0, k == KD - 1,
                              lin_ready if k == KD - 1 and j == 1 else None)
                        tl.used()
                    if g == 8 and j == 0:
                        pe.wait_ge(bg_ready, 1)
                        for i in range(2):
                            head_sums(HN["conv_a"] + i, ones64[:], P)
            tl.end()
            for g in range(4):
                head_sums(HN["dn_q"] + g, ones[:], P)
            pe.wait_ge(hn_rs, HN["dn_o"])
            beta, glog = small[:, 0:8], small[:, 8:16]
            for ch in range(8):
                mm(B[ch // 4][:, (ch % 4) * P:(ch % 4 + 1) * P], glog[:, ch:ch + 1].to_broadcast([P, P]), upper[:],
                   True, True)
            for ch in range(8):
                mm(B[2 + ch // 4][:, (ch % 4) * P:(ch % 4 + 1) * P], beta[:, ch:ch + 1].to_broadcast([P, P]),
                   ident[:], True, True)
            mm(B[4][:, 0:8], upper[:], glog, True, True)
            mm(B[4][:, 8:16], ones[:], glog, True, True, rows_ready)
            pe.wait_ge(dn_qk, 1)
            pe.wait_ge(gdiff, 1)
            for what in range(2):
                for ch in range(8):
                    c, hd = ch // 4, ch % 4
                    kc = qkv[:, 4 + hd, c * P:(c + 1) * P]
                    mm(B[4 + 2 * what + ch // 4][:, hd * P:(hd + 1) * P], kc,
                       kc if what == 0 else qkv[:, hd, c * P:(c + 1) * P], True, True,
                       dn_ready if ch == 7 else None)
            pe.wait_ge(gdecay, 1)
            pe.wait_ge(gdiff, 2)
            for ch in range(12):
                c, hd = (ch // 4, ch % 4) if ch < 8 else (0, ch % 4)
                src = qkv[:, (8 if ch < 8 else 4) + hd, c * P:(c + 1) * P]
                ins = nc.tensor.transpose(B[ch // 4][:, hd * P:(hd + 1) * P], src, ident[:])
            ins.then_inc(tok_ready, 1)
            pe.wait_ge(tok_scaled, 1)
            lw, x, xt, pm = DELTA["lw"], DELTA["x"], DELTA["xt"], DELTA["pm"]
            for i in range(7):
                for c in range(2):
                    pe.wait_ge(inv_done, 2 * i + c + 1)
                    for hd in range(4):
                        mm(B[c][:, hd * P:(hd + 1) * P], lw[:, 4 * c + hd, :], x[:, 4 * c + hd, :], True, True,
                           inv_p if hd == 3 else None)
                for c in range(2):
                    pe.wait_ge(inv_p_sb, 2 * i + c + 1)
                    for what in range(0 if i < 6 else 1, 2):
                        l, r = (xt, pm) if what == 0 else (pm, xt)
                        for hd in range(4):
                            mm(B[4 + 2 * what + c][:, hd * P:(hd + 1) * P], l[:, 4 * c + hd, :], r[:, 4 * c + hd, :],
                               True, True, inv_x if hd == 3 and what == 1 else None)
            pe.wait_ge(inv_done, 16)
            xt, vb, kd = DELTA["xt"], DELTA["vb"], DELTA["kd"]
            vn, state, intra, qd = DELTA["vn"], DELTA["state"], DELTA["intra"], DELTA["qd"]

            def four(bank, l, r, start=True, stop=True, inc=None):
                for hd in range(4):
                    mm(bank[:, hd * P:(hd + 1) * P], l(hd), r(hd), start and hd == 0, stop,
                       inc if hd == 3 else None)

            four(B[0], lambda d: xt[:, d, :], lambda d: vb[:, d, :], inc=dn_pe)
            pe.wait_ge(dn_sb, 1)
            four(B[2], lambda d: kd[:, d, :], lambda d: vn[:, d, :], inc=dn_pe)
            four(B[1], lambda d: vn[:, d, :], lambda d: intra[:, d, :], inc=dn_pe)
            pe.wait_ge(dn_sb, 2)
            four(B[3], lambda d: qkv[:, 4 + d, P:T], lambda d: state[:, d, :], inc=dn_pe)
            pe.wait_ge(dn_sb, 3)
            four(B[4], lambda d: xt[:, 4 + d, :], lambda d: vb[:, 4 + d, :], inc=dn_pe)
            pe.wait_ge(dn_sb, 4)
            four(B[5], lambda d: state[:, d, :], lambda d: qd[:, d, :], stop=False)
            four(B[5], lambda d: vn[:, 4 + d, :], lambda d: intra[:, 4 + d, :], start=False, inc=dn_pe)
            for g in range(2):
                head_sums(HN["dn_o"] + g, ones[:], P)
            pe.wait_ge(mix_ready, 1)
            project("mix_out", "mix_out", (0, 4), mixT, KD)

            norm_sums("ffn_2", KD)
            for c in range(2):
                for k in range(KD):
                    normed("ffn_2", k)
                    mm(B[3][:, c * 36:(c + 1) * 36], hn[:, k, c * P:(c + 1) * P],
                       params[:, COL["w_router"] + k * 36:COL["w_router"] + (k + 1) * 36], k == 0, k == KD - 1,
                       rt_ready if k == KD - 1 and c == 1 else None)
            for n in range(4):
                for i in range(4):
                    m = 4 * n + i
                    ins = nc.tensor.transpose(OUTB[n][:, i * P:(i + 1) * P],
                                              hn[:, m % KD, (m // KD) * P:(m // KD + 1) * P], ident[:])
            ins.then_inc(turn_h, 1)
            pe.wait_ge(rt_gate, 1)
            chosen = [route[:, c, 320:352] for c in range(2)]
            mm(B[3][:, 0:NE], upper[:], chosen[0], True, True)
            mm(B[3][:, NE:2 * NE], ones[:], chosen[0], True, False)
            mm(B[3][:, NE:2 * NE], upper[:], chosen[1], False, True)
            mm(B[3][:, 2 * NE:3 * NE], ones[:], chosen[0], True, False)
            mm(B[3][:, 2 * NE:3 * NE], ones[:], chosen[1], False, True, counted)

            def moe_gathered():
                pe.wait_ge(slots_in, 1)
                pe.wait_ge(h_tok_in, 2)
                def gather(r, half):
                    for k in range(4 * half, 4 * half + 4):
                        for c in range(2):
                            mm(B[6 + half][:, (k % 4) * P:(k % 4 + 1) * P], h_tok[:, c, k * P:(k + 1) * P],
                               slots[:, c, bass.ds(r * P, P)], c == 0, c == 1,
                               gather_sum if k == KD - 1 and c == 1 else None)

                def scatter(r, half, banks):
                    for m in range(4 * half, 4 * half + 4):
                        mm(banks[m % 4 // 2][:, (m % 2) * T:(m % 2 + 1) * T], y_slots[:, m * P:(m + 1) * P],
                           slots_T[:, bass.ds(r * T, T)], True, True, ex_scatter if m % 4 == 3 else None)

                gather(0, 0)
                gather(0, 1)
                for n in range(4):
                    for i in range(4):
                        qd, c = divmod(4 * n + i, 2)
                        ins = nc.tensor.transpose(B[2 + n][:, i * P:(i + 1) * P],
                                                  gated_slots[:, c, qd * P:(qd + 1) * P], ident[:])
                ins.then_inc(slots_turned, 1)
                base = PLAN["moe"]
                per = EXPERT_TILES // CT * QUAD

                def quad(r, first=False, last=False):

                    def arrived(i):
                        n = base + i
                        pe.wait_ge(slot_in[n % RING], r * (16 * per // RING) + 16 * (n // RING + 1))

                    def four_tiles(e, t):
                        n, i = base + (e * EXPERT_TILES + t) // CT, t % CT
                        return ring[:, n % RING, i * P:(i + 4) * P]

                    pe.wait_ge(gather_act, r + 1)
                    pe.wait_ge(gather_dve, r + 1)
                    for e in range(QUAD):
                        s0, n_e = CAP * e, r * QUAD + (e + 1)
                        for k in range(KD):
                            if 8 * k % CT == 0:
                                arrived(e * EC + 8 * k // CT)
                            g = CAP * (k % QUAD)
                            for part in range(2):
                                inc = None
                                if part == 1:
                                    inc = ex_gu if k == KD - 1 else ring_free if 8 * (k + 1) % CT == 0 else None
                                mm(B[part][g:g + CAP, :], gathered[:, k, s0:s0 + CAP], four_tiles(e, 8 * k + 4 * part),
                                   k < QUAD, k >= KD - QUAD, inc)
                        if first and e == 0:
                            pe.wait_ge(slots_T_in, 1)
                        for part in range(2):
                            pe.wait_ge(part_in[part], n_e)
                            for m in range(EC):
                                mm(B[2 + part][:, m * P:(m + 1) * P], partial[:, part, m * P:(m + 1) * P], stack[:],
                                   True, True, ex_turned if m == EC - 1 and part == 1 else None)
                        if not first and e == 0:
                            pe.wait_ge(y_act, r)
                            pe.wait_ge(y_dve, r)
                            scatter(r - 1, 0, B[6:8])
                        if not first and e == 1:
                            pe.wait_ge(ex_added, r * 2 - 1)
                            scatter(r - 1, 1, B[6:8])
                        if not last and e == 2:
                            if not first:
                                pe.wait_ge(ex_added, r * 2)
                            gather(r + 1, 0)
                        if not last and e == 3:
                            gather(r + 1, 1)
                        pe.wait_ge(ex_act, n_e)
                        for m in range(EC):
                            if m == 1:
                                arrived(e * EC + 3)
                            for half in range(2):
                                inc = None
                                if half == 1:
                                    inc = ring_free if m in (0, EC - 1) else None
                                mm(B[4 + half][s0:s0 + CAP, :], act[:, 0, m * CAP:(m + 1) * CAP],
                                   four_tiles(e, 64 + 8 * m + 4 * half), m == 0, m == EC - 1, inc)

                last = NE // QUAD - 1
                quad(0, first=True)
                with pe.Fori(1, last) as r:
                    quad(r)
                quad(last, last=True)
                pe.wait_ge(y_act, last + 1)
                pe.wait_ge(y_dve, last + 1)
                pe.wait_ge(ex_added, 2 * last)
                scatter(last, 0, B[6:8])
                scatter(last, 1, B[4:6])

            def moe_dense():
                pe.wait_ge(h_tok_in, 2)
                for e in range(NE):
                    if e >= 4:
                        pe.wait_ge(rt_free, e // 2 - 1)
                    for c in range(2):
                        mm(B[4 + (e // 2) % 2][:, (e % 2) * T + c * P:(e % 2) * T + (c + 1) * P],
                           route[:, c, 288 + e:289 + e].to_broadcast([P, P]), ident[:], True, True,
                           rt_rows if c == 1 and e % 2 == 1 else None)
                pe.wait_ge(rt_free, NE // 2)
                base = PLAN["moe"]

                def expert(r, first):
                    def place(t):
                        n = base + t // CT
                        return ring[:, n % RING, (t % CT) * P:(t % CT + 1) * P]

                    for i in range(EC):
                        n = base + i
                        pe.wait_ge(slot_in[n % RING], r * 16 + 16 * (n // RING + 1))
                    for m in range(EC + 1):
                        if m < EC:
                            for part in range(2):
                                for k in range(KD):
                                    mm(B[m % 2][:, part * T:(part + 1) * T], place(8 * k + 4 * part + m), hn[:, k, :],
                                       k == 0, k == KD - 1, gu_ready if part == 1 and k == KD - 1 else None)
                        if m >= 1:
                            pe.wait_ge(act_ready, r * EC + m)
                            for o in range(KD):
                                ins = mm(OUTB[o // 2][:, (o % 2) * T:(o % 2 + 1) * T], place(64 + 8 * (m - 1) + o),
                                         act[:, (m - 1) % 2, :], first and m == 1 and o % 2 == 0, True)
                            if m == EC:
                                ins.then_inc(ring_free, EC)

                expert(0, True)
                with pe.Fori(1, NE) as r:
                    expert(r, False)
                nc.tensor.transpose(B[0][:, 0:P], ident[:], ident[:]).then_inc(acc_ready, 1)

            assert owed[0] == 0
            pe.wait_ge(peak_in, 1)
            most = pe.value_load(peak[0:1, 0:1])
            with pe.If(most < CAP + 1):
                moe_gathered()
            with pe.Else():
                moe_dense()
            norm_sums("final", KD)
            assert owed[0] <= 1


        @block.scalar
        def _(act_e):
            st = Steps(act_e, act_step)

            def squares(name, src, nk, src_sem, counts):
                for i in range(nk // 2):
                    act_e.wait_ge(src_sem, counts(i))
                    nc.scalar.activation(sq[:, 2 * i:2 * i + 2, :], src[:, 2 * i:2 * i + 2, :],
                                         ACT.Square).then_inc(norm_sq, 1)
                nc.scalar.activation(small[:, 510:511], eps_col[:, 0:1], ACT.Ln)

            def root(name, dim):
                n = NORM[name]
                act_e.wait_ge(norm_sum, n + 1)
                st.link(nc.scalar.activation(lnv[:, n % 2, 0:T], B[2][:, 0:T], ACT.Ln, bias=eps_col[:, 0:1], scale=1.0 / dim))
                nc.scalar.activation(rstd[:, n % 2, :], lnv[:, n % 2, 0:T], ACT.Exp, scale=-0.5).then_inc(norm_rstd, 1)

            def norm(name, src, nk, dim, src_sem, counts):
                squares(name, src, nk, src_sem, counts)
                root(name, dim)

            def updates(name):
                product = {"ffn2_0": "mla_o", "ffn2_1": "fox_o", "ffn_2": "mix_out"}.get(name)
                if product:
                    return lin_free, lambda i: LIN[product] + i + 1
                return h_ready, lambda i: H_AT[name] + i + 1

            def residual_norm(name):
                norm(name, h[:], KD, D, *updates(name))

            def head_norms(first, n, ready, src, parts, dim, done, before, root_parts=None):
                root_parts = root_parts or parts

                def square(i):
                    act_e.wait_ge(*ready(i))
                    if i >= 2:
                        act_e.wait_ge(hn_sum, first + i - 1)
                    nc.scalar.activation(sqh[0:parts, (first + i) % 2, :, :].rearrange("p a t -> p (a t)"), src(i),
                                         ACT.Square).then_inc(hn_sq, 1)

                square(0)
                square(1)
                for i in range(0, n, 2):
                    if i + 2 < n:
                        square(i + 2)
                    for j in (i, i + 1):
                        g = first + j
                        act_e.wait_ge(hn_sum, g + 1)
                        st.done(nc.scalar.activation(lnv[0:root_parts, g % 2, :], B[2 + g % 2][0:root_parts, :], ACT.Ln,
                                                     bias=eps_col[0:root_parts, 0:1], scale=1.0 / dim))
                    st.settled()
                    for j in (i, i + 1):
                        g = first + j
                        if before + j - 1 > 0:
                            act_e.wait_ge(done, before + j - 1)
                        nc.scalar.activation(rsh[0:root_parts, g % 2, :], lnv[0:root_parts, g % 2, :], ACT.Exp,
                                             scale=-0.5).then_inc(hn_rs, 1)
                    if i + 3 < n:
                        square(i + 3)

            def sigmoid(out, x, done):
                st.link(nc.scalar.activation(out, x, ACT.Exp, scale=-1.0))
                st.link(nc.scalar.activation(out, out, ACT.Ln, bias=ones[:, 0:1]))
                nc.scalar.activation(out, out, ACT.Exp, scale=-1.0).then_inc(done, 1)

            def high_part(n, reg=0, wait=True):
                act_e.wait_ge(slot_in[n % RING], reg * 16 + 16 * (n // RING + 1))
                if wait:
                    act_e.wait_ge(ring_free, reg * RING + (n - 1))
                nc.scalar.activation(high[:, n % HIGH, :], ring[:, n % RING, :], ACT.Copy).then_inc(high_in, 1)

            def dense_ffn(name):
                base, f = PLAN[name], FFNS.index(name)
                if f:
                    act_e.wait_ge(acc_ready, f)
                    high_part(base, wait=False)
                    high_part(base + 1, wait=False)
                    squares(name, h, KD, *updates(name))
                else:
                    squares(name, h, KD, x_in, lambda i: 16)
                    act_e.wait_ge(rope_arg, 1)
                    st.done(nc.scalar.activation(sinr[:], sinr[:], ACT.Sin))
                    nc.scalar.activation(cosr[:], cosr[:], ACT.Sin).then_inc(rope_sin, 1)
                    high_part(base, wait=False)
                root(name, D)
                for k in range(KD):
                    act_e.wait_ge(x_full, KD * f + k + 1)
                    nc.scalar.activation(x_hi[:, k, :], sq[:, k, :], ACT.Copy).then_inc(x_high, 1)
                if not f:
                    high_part(base + 1, wait=False)

                def sigmoid_part(c, b, reg=0):
                    act_e.wait_ge(gu_ready, reg + (GU[name] + c + 1))
                    nc.scalar.activation(expg[:, b, :], B[b][:, 0:T], ACT.Exp, scale=-1.0).then_inc(sig_ready, 1)

                sigmoid_part(0, 0)
                with act_e.Fori(0, (FFC - 2) // RING) as r:
                    for j in range(RING):
                        high_part(base + 2 + j, reg=r)
                        sigmoid_part(1 + j, (1 + j) % 2, r * RING)
                for c in range(FFC - 1, FFC + 1):
                    if c + 1 <= FFC:
                        high_part(base + c + 1)
                    if c < FFC:
                        sigmoid_part(c, c % 2)

            def split_norm(name, base, after_split):
                high_part(base, wait=after_split)
                squares(name, h, KD, *updates(name))
                root(name, D)
                for k in range(KD):
                    act_e.wait_ge(norm_out, OUT_AT[name] + k + 1)
                    nc.scalar.activation(x_hi[:, k, :], oT[:, k, :], ACT.Copy).then_inc(x_high, 1)

            def highs(base, g, last, done=[1]):
                if g == 0:
                    done[0] = 1
                while done[0] <= min((16 * g + 15) // CT + 1, last):
                    high_part(base + done[0])
                    done[0] += 1

            def attention(first):
                for i in range(H + 1):
                    if i < H:
                        a = first + i
                        act_e.wait_ge(masked, a + 1)
                        if i >= 2:
                            act_e.wait_ge(turned, a - 1)
                        for b, (c0, c1) in enumerate(((0, P), (P, 3 * P))):
                            ins = nc.scalar.activation(probs[:, a % 2, c0:c1], logits[:, a % 2, c0:c1], ACT.Exp,
                                                       bias=nmax[:, a, b:b + 1], accum_out=psums[:, a, b:b + 1])
                        ins.then_inc(expd, 1)
                    if i >= 1:
                        a = first + i - 1
                        act_e.wait_ge(rcpd, a + 1)
                        for b, (c0, c1) in enumerate(((0, P), (P, 3 * P))):
                            ins = nc.scalar.activation(probs[:, a % 2, c0:c1], probs[:, a % 2, c0:c1], ACT.Copy,
                                                       scale=psums[:, a, b:b + 1])
                        ins.then_inc(prob_ready, 1)

            def ple(layer):
                name = f"ple_{layer}"
                residual_norm(name)
                for m in range(KD):
                    act_e.wait_ge(lin_ready, LIN[name] + m + 1)
                    if m >= 2:
                        act_e.wait_ge(lin_free, LIN[name] + m - 1)
                    nc.scalar.activation(expg[:, m % 2, :], OUTB[(LIN[name] + m) % 4][:, 0:T], ACT.Exp,
                                         scale=-1.0).then_inc(ple_e, 1)

            act_e.wait_ge(par_in, 16)
            act_e.wait_ge(consts, 1)

            dense_ffn("ffn1_0")
            act_e.wait_ge(consts, 2)
            residual_norm("mix_0")
            norm("q_lat", cq, 4, QR, lin_free, lambda i: LIN["mla_in"] + i + 1)
            norm("kv_lat", ckv, 2, KVR, lin_free, lambda i: LIN["mla_in"] + 3)
            head_norms(HN["mla_q"], 8, lambda g: (lin_ready, LIN["mla_q"] + g + 1),
                       lambda g: OUTB[(LIN["mla_q"] + g) % 4][0:QK, :], QK, QK, hn_done, 0)
            for b in range(2):
                for j in range(2):
                    nc.scalar.activation(sqh[NOPE:QK, b, j, :], kpe[NOPE:QK, :], ACT.Square)
            head_norms(HN["mla_k"], 8, lambda g: (lin_ready, LIN["mla_k"] + g + 1),
                       lambda g: OUTB[(LIN["mla_k"] + g) % 4][0:NOPE, :], NOPE, QK, hn_done, 8, root_parts=QK)
            attention(0)
            dense_ffn("ffn2_0")
            ple(0)

            dense_ffn("ffn1_1")
            fox = PLAN["fox_qk"]
            split_norm("mix_1", fox, True)
            act_e.wait_ge(f_abs, 1)
            st.link(nc.scalar.activation(small[:, 96:128], small[:, 64:96], ACT.Exp, scale=-1.0))
            nc.scalar.activation(small[:, 128:160], small[:, 96:128], ACT.Ln, bias=ones[:, 0:1]).then_inc(f_ln, 1)

            def fox_group(g):
                highs(fox, g, 6)
                return lin_ready, LIN["fox_qk"] + g + 1

            head_norms(HN["fox_qk"], 8, fox_group,
                       lambda g: OUTB[(LIN["fox_qk"] + g) % 4][:, :], P, 64, lin_free, LIN["fox_qk"])
            high_part(fox + 7)
            high_part(fox + 8)
            attention(H)
            dense_ffn("ffn2_1")
            ple(1)

            split_norm("mix2", PLAN["mix_in"], False)
            highs(PLAN["mix_in"], 0, 9)

            def conv_sigmoid(part):
                act_e.wait_ge(silu_in, part + 1)
                sigmoid(silu_tmp[part], qkv[:, 4 * part:4 * part + 4, :], silu_e)

            act_e.wait_ge(ba_abs, 1)
            st.done(nc.scalar.activation(small[:, 64:72], small[:, 32:40], ACT.Exp, scale=-1.0))
            st.done(nc.scalar.activation(small[:, 88:92], col("a_log", 0, 4), ACT.Exp))
            st.link(nc.scalar.activation(small[:, 72:80], small[:, 48:56], ACT.Exp, scale=-1.0))
            nc.scalar.activation(small[:, 80:88], small[:, 72:80], ACT.Ln, bias=ones[:, 0:1]).then_inc(ba_ln, 1)
            for g in range(14):
                if g == 8:
                    head_norms(HN["conv_a"], 2, lambda i: (hn_src, 1),
                               lambda i: y_a[:, 2 * i:2 * i + 2, :].rearrange("p a t -> p (a t)"), P, 64, hn_done, 16)
                if g:
                    highs(PLAN["mix_in"], g, 9)
                if g >= 10 and g % 2 == 0:
                    conv_sigmoid((g - 10) // 2)
                act_e.wait_ge(lin_ready, LIN["mix_in"] + g + 1)
                bank = OUTB[(LIN["mix_in"] + g) % 4][:, :].rearrange("p (a t) -> p a t", t=T)
                if g < 2:
                    dst = a_h[:, 2 * g:2 * g + 2, :]
                elif g < 4:
                    dst = convt[:, 2 * (g - 2):2 * (g - 2) + 2, :]
                elif g < 6:
                    dst = a_b[:, 2 * (g - 4):2 * (g - 4) + 2, :]
                elif g < 12:
                    dst = qkv_pad[:, 2 * (g - 6):2 * (g - 6) + 2, 3:PADQ]
                else:
                    dst = z_gate[:, 2 * (g - 12):2 * (g - 12) + 2, :]
                nc.scalar.activation(dst, bank, ACT.Copy).then_inc(lin_free, 1)
            head_norms(HN["dn_q"], 4, lambda g: (hn_src, 2 + g // 2),
                       lambda g: qkv[:, 2 * g:2 * g + 2, :].rearrange("p a t -> p (a t)"), P, 1, hn_done, 18)
            conv_sigmoid(2)
            act_e.wait_ge(gdiff, 1)
            st.done(nc.scalar.activation(DELTA["decay"], DELTA["decay"], ACT.Exp))
            st.done(nc.scalar.activation(DELTA["egrow"].rearrange("p c t -> p (c t)"), B[1][:, :], ACT.Exp))
            nc.scalar.activation(small[:, 144:160], small[:, 128:144], ACT.Exp).then_inc(gdecay, 1)
            sigmoid(pin[:], z_gate, z_exp)
            for i in range(14):
                act_e.wait_ge(inv_p, i + 1)
                c = i % 2
                nc.scalar.activation(DELTA["pm"].rearrange("p c t -> p (c t)")[:, c * 512:(c + 1) * 512], B[c][:, :],
                                     ACT.Copy).then_inc(inv_p_sb, 1)
            head_norms(HN["dn_o"], 2, lambda g: (hn_src, 4),
                       lambda g: convt[:, 2 * g:2 * g + 2, :].rearrange("p a t -> p (a t)"), P, 128, hn_done, 22)

            residual_norm("ffn_2")
            for i in range(2):
                act_e.wait_ge(rt_max, i + 1)
                c0, n, d0 = ((40, 4, 44), (200, 1, 201))[i]
                nc.scalar.activation(route[:, :, d0:d0 + n], route[:, :, c0:c0 + n], ACT.Exp).then_inc(rt_exp, 1)
            act_e.wait_ge(turn_h, 1)
            for c in range(2):
                ins = nc.scalar.activation(h_tok[:, c, 512:1024], OUTB[2 * c + 1][:, :], ACT.Copy)
            ins.then_inc(h_tok_in, 1)

            def moe_gathered():
                per = EXPERT_TILES // CT * QUAD

                def gathered_half(r):
                    act_e.wait_ge(gather_sum, r + 1)
                    nc.scalar.activation(gathered[:, 4:8, :].rearrange("p k s -> p (k s)"), B[7][:, :],
                                         ACT.Copy).then_inc(gather_act, 1)

                def quad(r, last=False):
                    for e in range(QUAD):
                        act_e.wait_ge(ex_gu, r * QUAD + (e + 1))
                        nc.scalar.activation(partial[:, 0, :], B[0][:, :], ACT.Copy).then_inc(part_in[0], 1)
                        act_e.wait_ge(ex_turned, r * QUAD + (e + 1))
                        nc.scalar.activation(expg[:, 0, 0:P].rearrange("p (m s) -> p m s", s=CAP), turned_part(0),
                                             ACT.Exp, scale=-1.0).then_inc(ex_exp, 1)
                    if not last:
                        gathered_half(r + 1)
                    act_e.wait_ge(ring_free, r * per + (PLAN["moe"] + per))
                    nc.scalar.activation(y_slots[:, 512:1024], B[5][:, :], ACT.Copy).then_inc(y_act, 1)

                gathered_half(0)
                with act_e.Fori(0, NE // QUAD - 1) as r:
                    quad(r)
                quad(NE // QUAD - 1, last=True)

            act_e.wait_ge(peak_in, 1)
            most = act_e.value_load(peak[0:1, 0:1])
            with act_e.If(most < CAP + 1):
                moe_gathered()
            with act_e.Else():
                with act_e.Fori(0, NE * EC // 2) as r:
                    for j in range(2):
                        act_e.wait_ge(gu_ready, r * 2 + (GU["moe"] + j + 1))
                        nc.scalar.activation(expg[:, j, :], B[j][:, 0:T], ACT.Exp, scale=-1.0).then_inc(sig_ready, 1)
            residual_norm("final")

        @block.vector
        def _(dve):
            st = Steps(dve, dve_step)
            V = nc.vector

            def norm_apply(name, src, nk, gain, dst):
                n = NORM[name]
                dve.wait_ge(norm_rstd, n + 1)
                for k in range(nk):
                    ins = V.scalar_tensor_tensor(out=dst[:, k, :], in0=src[:, k, :], scalar=col(gain, k),
                                                 in1=rstd[:, n % 2, :], op0=ALU.mult, op1=ALU.mult)
                    ins.then_inc(norm_out, 1)

            def split_norm(name):
                n = NORM[name]
                dve.wait_ge(norm_rstd, n + 1)
                for k in range(KD + 2):
                    if k < KD:
                        V.scalar_tensor_tensor(out=oT[:, k, :], in0=h[:, k, :], scalar=col("g_" + name, k),
                                               in1=rstd[:, n % 2, :], op0=ALU.mult, op1=ALU.mult).then_inc(norm_out, 1)
                    if k >= 2:
                        dve.wait_ge(x_high, X_AT[name] + k - 1)
                        V.tensor_tensor(x_lo[:, k - 2, :], oT[:, k - 2, :], x_hi[:, k - 2, :].bitcast(F32),
                                        ALU.subtract).then_inc(x_low, 1)

            def add_residual(bank, i, scale, inc):
                hh = h[:, 2 * i:2 * i + 2, :].rearrange("p a t -> p (a t)")
                ins = V.scalar_tensor_tensor(out=hh, in0=bank[:, :], scalar=scale, in1=hh, op0=ALU.mult, op1=ALU.add)
                if inc is not None:
                    ins.then_inc(inc, 1)
                return ins

            def low_part(name, c, reg=0):
                n = PLAN[name] + c
                dve.wait_ge(high_in, reg * RING + (SPLIT_AT[name] + c + 1))
                V.tensor_tensor(ring_lo[:, n % RING, :], ring[:, n % RING, :], high[:, n % HIGH, :].bitcast(F32),
                                ALU.subtract).then_inc(low_in, 1)

            def silu_times_up(b, wait_sig, at, reg, last):
                g, u = B[b][:, 0:T], B[b][:, T:2 * T]
                e, s = expg[:, b, :], gate_r[:, b, :]
                dve.wait_ge(sig_ready, wait_sig)
                V.tensor_scalar_add(e, e, 1.0).then_inc(glu_step, 1)
                dve.wait_ge(glu_step, reg + (at + 1))
                V.reciprocal(s, e).then_inc(glu_step, 1)
                dve.wait_ge(glu_step, reg + (at + 2))
                V.tensor_tensor(s, g, s, ALU.mult).then_inc(glu_step, 1)
                dve.wait_ge(glu_step, reg + (at + 3))
                V.tensor_tensor(act[:, b, :] if last is None else s, u, s, ALU.mult).then_inc(glu_step, 1)
                dve.wait_ge(glu_step, reg + (at + 4))
                if last is not None:
                    V.tensor_tensor(act[:, b, :], s, last, ALU.mult).then_inc(act_ready, 1)

            def dense_ffn(name):
                f, gu0 = FFNS.index(name), GU[name]
                n = NORM[name]
                low_part(name, 0)
                dve.wait_ge(norm_rstd, n + 1)
                for k in range(KD + 2):
                    if k < KD:
                        V.scalar_tensor_tensor(out=sq[:, k, :], in0=h[:, k, :], scalar=col("g_" + name, k),
                                               in1=rstd[:, n % 2, :], op0=ALU.mult, op1=ALU.mult).then_inc(x_full, 1)
                    if k >= 2:
                        dve.wait_ge(x_high, X_AT[name] + k - 1)
                        V.tensor_tensor(x_lo[:, k - 2, :], sq[:, k - 2, :], x_hi[:, k - 2, :].bitcast(F32),
                                        ALU.subtract).then_inc(x_low, 1)

                low_part(name, 1)

                def act_part(c, b, reg=0):
                    i = gu0 + c
                    silu_times_up(b, reg + (i + 1), 5 * i, reg * 5, None)
                    V.tensor_copy(act_hi[:, b, :], act[:, b, :]).then_inc(glu_step, 1)
                    dve.wait_ge(glu_step, reg * 5 + (5 * i + 5))
                    V.tensor_tensor(act_lo[:, b, :], act[:, b, :], act_hi[:, b, :].bitcast(F32),
                                    ALU.subtract).then_inc(act_parts, 1)

                act_part(0, 0)
                with dve.Fori(0, (FFC - 2) // RING) as r:
                    for j in range(RING):
                        low_part(name, 2 + j, r)
                        act_part(1 + j, (1 + j) % 2, r * RING)
                low_part(name, FFC)
                act_part(FFC - 1, (FFC - 1) % 2)
                dve.wait_ge(acc_ready, f + 1)
                for i in range(4):
                    add_residual(OUTB[i], i, 0.5, h_ready)

            def attention(first, fox):
                for i in range(H + 4):
                    if i < H:
                        a = first + i
                        dve.wait_ge(scores, a + 1)
                        s = B[a % 2]
                        lg = logits[:, a % 2, :]
                        if fox:
                            st.done(V.scalar_tensor_tensor(out=lg[:, 0:P], in0=s[:, 0:P], scalar=dtok[:, 0, i:i + 1],
                                                           in1=mask[:, 0:P], op0=ALU.add, op1=ALU.add))
                            st.link(V.scalar_tensor_tensor(out=lg[:, P:3 * P], in0=s[:, P:3 * P],
                                                           scalar=dtok[:, 1, i:i + 1], in1=mask[:, P:3 * P],
                                                           op0=ALU.add, op1=ALU.add))
                        else:
                            st.link(V.tensor_tensor(lg, s[:, 0:3 * P], mask[:], ALU.add))
                        st.done(V.tensor_reduce(nmax[:, a, 0:1], lg[:, 0:P], AXX, ALU.max))
                        st.link(V.tensor_reduce(nmax[:, a, 1:2], lg[:, P:3 * P], AXX, ALU.max))
                        V.tensor_scalar(nmax[:, a, :], nmax[:, a, :], -1.0, None, ALU.mult).then_inc(masked, 1)
                    if 1 <= i <= H:
                        a = first + i - 1
                        dve.wait_ge(expd, a + 1)
                        V.reciprocal(psums[:, a, :], psums[:, a, :]).then_inc(rcpd, 1)
                    if 2 <= i <= H + 1:
                        a = first + i - 2
                        dve.wait_ge(turned, a + 1)
                        V.tensor_copy(pT_sb[:, a % 2, :], B[2 + a % 2][:, 0:3 * P]).then_inc(pt_ready, 1)
                    if i >= 5 and i % 2 == 1:
                        pair = (first + i - 5) // 2
                        dve.wait_ge(pv_done, 2 * pair + 2)
                        V.tensor_copy(oT[:, (i - 5) // 2, :], B[4 + pair % 2][:, 0:T]).then_inc(o_ready, 1)

            def out_product(lin):
                for g in range(4):
                    dve.wait_ge(lin_ready, LIN[lin] + g + 1)
                    add_residual(OUTB[(LIN[lin] + g) % 4], g, 1.0, lin_free)

            def ple(layer):
                name = f"ple_{layer}"
                norm_apply(name, h, KD, f"g_ple_{layer}", hn)
                for m in range(KD):
                    bank = OUTB[(LIN[name] + m) % 4]
                    b = m % 2
                    dve.wait_ge(ple_e, KD * layer + m + 1)
                    st.link(V.tensor_scalar_add(expg[:, b, :], expg[:, b, :], 1.0))
                    st.link(V.reciprocal(gate_r[:, b, :], expg[:, b, :]))
                    V.tensor_tensor(act[:, b, :], bank[:, T:2 * T], gate_r[:, b, :], ALU.mult).then_inc(lin_free, 1)
                    dve.wait_ge(lin_free, LIN[name] + m + 1)
                    ins = V.tensor_tensor(h[:, m, :], h[:, m, :], act[:, b, :], ALU.add)
                    if m % 2:
                        ins.then_inc(h_ready, 1)

            def rotate(x, n):
                lo, hi = NOPE, QK
                xr = x.rearrange("p a t -> p (a t)")
                half = ROPE // 2
                turn = [(i + half) % ROPE for i in range(ROPE)]
                a = rope_t[lo:hi, 0, 0:n * T]
                b = rope_t[lo:hi, 1, 0:n * T]
                st.link(V.stream_shuffle(a, xr, turn))
                a3, b3 = (t.rearrange("p (a t) -> p a t", t=T) for t in (a, b))
                st.done(V.tensor_tensor(a3, a3, rep(sinr[lo:hi, :], n), ALU.mult))
                st.link(V.tensor_tensor(b3, x, rep(cosr[lo:hi, :], n), ALU.mult))
                st.link(V.tensor_tensor(x, a3, b3, ALU.add))

            dve.wait_ge(par_in, 16)
            dve.wait_ge(pos_in, 16)
            ang, turns = rope_t[:, 0, 0:T], rope_t[:, 1, 0:T]
            st.link(V.tensor_copy(ang, posi))
            st.link(V.tensor_scalar(ang, ang, col("inv_freq"), None, ALU.mult))
            st.link(V.tensor_scalar(turns, ang, 1.0 / TWO_PI, None, ALU.mult))
            st.link(V.tensor_scalar_add(turns, turns, ROUND))
            st.link(V.tensor_scalar_add(turns, turns, -ROUND))
            for part in (PI2_A, PI2_B, PI2_C):
                st.link(V.scalar_tensor_tensor(out=ang, in0=turns, scalar=-part, in1=ang, op0=ALU.mult, op1=ALU.add))
            st.link(V.tensor_scalar(ang, ang, 3.1415925, -3.1415925, ALU.min, ALU.max))
            st.done(V.tensor_copy(sinr[:], ang))
            V.tensor_scalar(cosr[:], ang, 0.5, None, ALU.mult).then_inc(rope_arg, 1)
            st.done(V.tensor_scalar(gq[:, 0:1], col("mla_qn"), float(QK) ** -0.5, None, ALU.mult))
            st.done(V.tensor_scalar(gq[:, 1:2], col("fox_qn"), 0.125, None, ALU.mult))
            dve.wait_ge(x_in, 16)
            dense_ffn("ffn1_0")
            norm_apply("mix_0", h, KD, "g_mix_0", hn)
            dve.wait_ge(rope_sin, 1)
            st.done(V.tensor_scalar(sinr[:], sinr[:], col("rope_sign"), None, ALU.mult))
            st.link(V.tensor_tensor(cosr[:], cosr[:], cosr[:], ALU.mult))
            st.link(V.tensor_scalar(cosr[:], cosr[:], -2.0, 1.0, ALU.mult, ALU.add))
            dve.wait_ge(consts, 2)
            L0 = LIN["mla_in"]
            for g in range(4):
                dve.wait_ge(lin_ready, L0 + g + 1)
                bank = OUTB[(L0 + g) % 4]
                if g < 3:
                    dst = (cq[:, 0:2, :], cq[:, 2:4, :], ckv)[g].rearrange("p a t -> p (a t)")
                    V.tensor_copy(dst, bank[:, :]).then_inc(lin_free, 1)
                else:
                    V.tensor_copy(kpe, bank[:, 0:T]).then_inc(lin_free, 1)
            norm_apply("q_lat", cq, 4, "g_q_lat", hn)
            norm_apply("kv_lat", ckv, 2, "g_kv_lat", hn[:, 4:6, :])
            dve.wait_ge(lin_free, L0 + 4)
            st.link(V.tensor_scalar(kr[NOPE:QK, :], kpe[NOPE:QK, :], col("mla_kn")[NOPE:QK], None, ALU.mult))
            rotate(kr[NOPE:QK, :].rearrange("p (a t) -> p a t", a=1), 1)
            for g in range(8):
                bank = OUTB[(LIN["mla_q"] + g) % 4]
                q2 = qT[0:QK, 2 * g:2 * g + 2, :].rearrange("p a t -> p (a t)")
                dve.wait_ge(hn_rs, HN["mla_q"] + g + 1)
                V.scalar_tensor_tensor(out=q2, in0=bank[0:QK, :], scalar=gq[0:QK, 0:1], in1=rsh[0:QK, g % 2, :],
                                       op0=ALU.mult, op1=ALU.mult).then_inc(lin_free, 1)
                dve.wait_ge(lin_free, LIN["mla_q"] + g + 1)
                rotate(qT[NOPE:QK, 2 * g:2 * g + 2, :], 2)
                dve.sem_inc(hn_done, 1)
            for g in range(8):
                bank = OUTB[(LIN["mla_k"] + g) % 4]
                gi = HN["mla_k"] + g
                dve.wait_ge(hn_rs, gi + 1)
                V.scalar_tensor_tensor(out=kT[0:NOPE, 2 * g:2 * g + 2, :].rearrange("p a t -> p (a t)"),
                                       in0=bank[0:NOPE, :], scalar=col("mla_kn")[0:NOPE], in1=rsh[0:NOPE, gi % 2, :],
                                       op0=ALU.mult, op1=ALU.mult).then_inc(lin_free, 1)
                V.tensor_tensor(kT[NOPE:QK, 2 * g:2 * g + 2, :], rep(kr[NOPE:QK, :], 2),
                                rsh[NOPE:QK, gi % 2, :].rearrange("p (a t) -> p a t", t=T), ALU.mult).then_inc(hn_done, 1)

            def copy_values(lin, halfway=None):
                for g in range(4):
                    if g == 2 and halfway:
                        halfway()
                    dve.wait_ge(lin_ready, LIN[lin] + g + 1)
                    half, c = g // 2, g % 2
                    V.tensor_copy(v_tok[:, c, half * 512:(half + 1) * 512],
                                  OUTB[(LIN[lin] + g) % 4][:, :]).then_inc(lin_free, 1)

            copy_values("mla_v")
            attention(0, False)
            out_product("mla_o")
            dense_ffn("ffn2_0")
            ple(0)

            dense_ffn("ffn1_1")
            low_part("fox_qk", 0)
            split_norm("mix_1")
            dve.wait_ge(f_ready, 1)
            zf = small[:, 32:64]
            st.link(V.tensor_tensor(zf.rearrange("p (c n) -> p c n", n=H),
                                    B[3][:, 0:2 * H].rearrange("p (c n) -> p c n", n=H),
                                    rep(col("b_f", 0, H), 2), ALU.add))
            V.scalar_tensor_tensor(out=small[:, 64:96], in0=zf, scalar=-1.0, in1=zf, op0=ALU.mult,
                                   op1=ALU.max).then_inc(f_abs, 1)
            dve.wait_ge(f_ln, 1)
            V.scalar_tensor_tensor(out=small[:, 0:32], in0=zf, scalar=0.0, in1=small[:, 128:160], op0=ALU.min,
                                   op1=ALU.subtract).then_inc(logf_ready, 1)
            dve.wait_ge(dec_sum, 1)
            V.tensor_copy(dtok[:, :, :].rearrange("p c n -> p (c n)"), B[3][:, 0:2 * H])
            V.tensor_scalar(ndec[:], B[3][0:H, P:3 * P], -1.0, None, ALU.mult).then_inc(dec_ready, 1)
            low_part("fox_qk", 1)
            for g in range(8):
                for c in {0: (2,), 2: (3, 4), 4: (5,)}.get(g, ()):
                    low_part("fox_qk", c)
                if g == 6:
                    low_part("fox_v", 0)
                bank = OUTB[(LIN["fox_qk"] + g) % 4]
                gi = HN["fox_qk"] + g
                dst = (qT if g < 4 else kT)[:, 2 * (g % 4):2 * (g % 4) + 2, :].rearrange("p a t -> p (a t)")
                dve.wait_ge(hn_rs, gi + 1)
                V.scalar_tensor_tensor(out=dst, in0=bank[:, :], scalar=gq[:, 1:2] if g < 4 else col("fox_kn"),
                                       in1=rsh[:, gi % 2, :], op0=ALU.mult, op1=ALU.mult).then_inc(lin_free, 1)
            low_part("fox_v", 1)
            copy_values("fox_v", lambda: low_part("fox_v", 2))
            attention(H, True)
            out_product("fox_o")
            dense_ffn("ffn2_1")
            ple(1)

            low_part("mix_in", 0)
            split_norm("mix2")
            low_part("mix_in", 1)
            st.done(V.memset(qkv_pad[:, :, 0:3], 0.0))
            st.done(V.memset(u_pad[:, :, 0:2], 0.0))
            dve.wait_ge(ba_ready, 1)
            ba = B[3][:, 0:16].rearrange("p (c n) -> p c n", n=8)

            def s3(lo):
                return small[:, lo:lo + 8].rearrange("p (c n) -> p c n", n=4)

            st.done(V.tensor_copy(s3(32), ba[:, :, 0:4]))
            st.link(V.tensor_tensor(s3(40), ba[:, :, 4:8], rep(col("dt_bias", 0, 4), 2), ALU.add))
            V.scalar_tensor_tensor(out=small[:, 48:56], in0=small[:, 40:48], scalar=-1.0, in1=small[:, 40:48], op0=ALU.mult,
                                   op1=ALU.max).then_inc(ba_abs, 1)
            dve.wait_ge(ba_ln, 1)
            st.done(V.tensor_scalar_add(small[:, 64:72], small[:, 64:72], 1.0))
            st.link(V.scalar_tensor_tensor(out=small[:, 56:64], in0=small[:, 40:48], scalar=0.0, in1=small[:, 80:88],
                                           op0=ALU.max, op1=ALU.add))
            st.done(V.reciprocal(small[:, 0:8], small[:, 64:72]))
            st.link(V.tensor_tensor(s3(8), s3(56), rep(small[:, 88:92], 2), ALU.mult))
            V.tensor_scalar(small[:, 8:16], small[:, 8:16], -1.0, None, ALU.mult).then_inc(bg_ready, 1)
            low_part("mix_in", 2)
            low_part("mix_in", 3)
            L = LIN["mix_in"]
            dve.wait_ge(lin_free, L + 4)
            st.link(V.tensor_tensor(u_pad[:, :, 2:PADU], convt, a_h, ALU.mult))
            for n in range(4):
                st.done(V.tensor_scalar(y_a[:, n, :], u_pad[:, n, 0:T], col("conv_a_w", n), None, ALU.mult))
            for tap in range(1, 3):
                st.settled()
                for n in range(4):
                    st.done(V.scalar_tensor_tensor(out=y_a[:, n, :], in0=u_pad[:, n, tap:tap + T],
                                                   scalar=col("conv_a_w", 4 * tap + n), in1=y_a[:, n, :],
                                                   op0=ALU.mult, op1=ALU.add))
            low_part("mix_in", 4)
            st.settled()
            dve.wait_ge(lin_free, L + 6)
            V.tensor_tensor(y_a, y_a, a_b, ALU.mult).then_inc(hn_src, 1)
            low_part("mix_in", 5)
            low_part("mix_in", 6)
            def silu(part):
                x = qkv[:, 4 * part:4 * part + 4, :]
                dve.wait_ge(silu_e, part + 1)
                if part < 2:
                    V.tensor_tensor(x, x, silu_tmp[part], ALU.mult).then_inc(hn_src, 1)
                else:
                    st.link(V.tensor_tensor(x, x, silu_tmp[part], ALU.mult))

            for part in range(3):
                dve.wait_ge(lin_free, L + 6 + 2 * (part + 1))
                tiles = range(4 * part, 4 * part + 4)
                for n in tiles:
                    st.done(V.tensor_scalar(qkv[:, n, :], qkv_pad[:, n, 0:T], col("dn_conv_w", n), None, ALU.mult))
                for tap in range(1, 4):
                    st.settled()
                    if tap == (3, 2, 1)[part]:
                        low_part("mix_in", 7 + part)
                    for n in tiles:
                        ins = V.scalar_tensor_tensor(out=qkv[:, n, :], in0=qkv_pad[:, n, tap:tap + T],
                                                     scalar=col("dn_conv_w", 12 * tap + n), in1=qkv[:, n, :],
                                                     op0=ALU.mult, op1=ALU.add)
                        if tap == 3 and n == tiles[-1]:
                            ins.then_inc(silu_in, 1)
                        else:
                            st.done(ins)
                if part:
                    silu(part - 1)

            def flat(x):
                return x.rearrange("p a t -> p (a t)")

            for g in range(2):
                dve.wait_ge(hn_rs, 24 + g + 1)
                for j in range(2):
                    n = 2 * g + j
                    ins = V.scalar_tensor_tensor(out=mixT[:, n, :], in0=y_a[:, n, :], scalar=col("conv_a_g", n),
                                                 in1=rsh[:, g % 2, j * T:(j + 1) * T], op0=ALU.mult, op1=ALU.mult)
                ins.then_inc(hn_done, 1)
            dve.wait_ge(hn_src, 3)
            for t in (DELTA["x"], DELTA["xt"]):
                st.done(V.tensor_copy(t, rep(ident[:], 8)))
            for g in range(4):
                dve.wait_ge(hn_rs, 26 + g + 1)
                x = flat(qkv[:, 2 * g:2 * g + 2, :])
                V.scalar_tensor_tensor(out=x, in0=x, scalar=128.0 ** -0.5 if g < 2 else 1.0, in1=rsh[:, g % 2, :],
                                       op0=ALU.mult, op1=ALU.mult).then_inc(hn_done, 1)
            dve.wait_ge(hn_done, 22)
            dve.sem_inc(dn_qk, 1)
            decay, brow, lt, intra = DELTA["decay"], DELTA["brow"], DELTA["lt"], DELTA["intra"]
            dve.wait_ge(rows_ready, 1)
            st.link(V.tensor_copy(small[:, 128:136], B[4][:, 0:8]))
            for ch in range(8):
                st.done(V.tensor_scalar(decay[:, ch, :], B[ch // 4][:, (ch % 4) * P:(ch % 4 + 1) * P],
                                        small[:, 128 + ch:129 + ch], 0.0, ALU.subtract, ALU.min))
            V.tensor_tensor(small[:, 136:144], B[4][:, 8:16], small[:, 128:136], ALU.subtract).then_inc(gdiff, 1)
            silu(2)
            bf = flat(brow)
            st.done(V.tensor_copy(bf[:, 0:512], B[2][:, :]))
            V.tensor_copy(bf[:, 512:1024], B[3][:, :]).then_inc(gdiff, 1)
            dve.wait_ge(gdecay, 1)
            st.link(V.tensor_tensor(decay, decay, rep(upper[:], 8), ALU.mult))
            st.done(V.tensor_tensor(DELTA["qd"], qkv[:, 0:4, P:T], DELTA["egrow"], ALU.mult))
            st.done(V.scalar_tensor_tensor(out=small[:, 160:168], in0=small[:, 0:8], scalar=-1.0,
                                           in1=small[:, 144:152], op0=ALU.mult, op1=ALU.mult))
            dve.wait_ge(dn_ready, 1)
            for b in range(2):
                st.done(V.tensor_tensor(flat(lt)[:, b * 512:(b + 1) * 512], B[4 + b][:, :],
                                        flat(decay)[:, b * 512:(b + 1) * 512], ALU.mult))
            dve.wait_ge(dn_ready, 2)
            for b in range(2):
                st.done(V.tensor_tensor(flat(intra)[:, b * 512:(b + 1) * 512], B[6 + b][:, :],
                                        flat(decay)[:, b * 512:(b + 1) * 512], ALU.mult))
            st.settled()
            st.link(V.tensor_tensor(lt, lt, brow, ALU.mult))
            dve.wait_ge(z_exp, 1)
            st.done(V.tensor_tensor(z_gate, z_gate, pin[:], ALU.mult))
            vb, kd = DELTA["vb"], DELTA["kd"]
            dve.wait_ge(tok_ready, 1)
            for ch in range(8):
                st.done(V.tensor_scalar(vb[:, ch, :], B[ch // 4][:, (ch % 4) * P:(ch % 4 + 1) * P],
                                        small[:, ch:ch + 1], None, ALU.mult))
            for hd in range(4):
                ins = V.tensor_scalar(kd[:, hd, :], B[2][:, hd * P:(hd + 1) * P], small[:, 152 + hd:153 + hd], None,
                                      ALU.mult)
            ins.then_inc(tok_scaled, 1)
            x, xt, lw = DELTA["x"], DELTA["xt"], DELTA["lw"]
            st.settled()
            for c in range(2):
                V.tensor_tensor(lw[:, 4 * c:4 * c + 4, :], lt[:, 4 * c:4 * c + 4, :], rep(level[:, 0, :], 4),
                                ALU.mult).then_inc(inv_done, 1)
            for i in range(7):
                for c in range(2):
                    if i < 6:
                        dve.wait_ge(inv_p, 2 * i + c + 1)
                        st.done(V.tensor_tensor(lw[:, 4 * c:4 * c + 4, :], lt[:, 4 * c:4 * c + 4, :],
                                                rep(level[:, i + 1, :], 4), ALU.mult))
                    dve.wait_ge(inv_x, 2 * i + c + 1)
                    if i < 6:
                        xb = flat(x)[:, c * 512:(c + 1) * 512]
                        st.done(V.tensor_tensor(xb, xb, B[4 + c][:, :], ALU.subtract))
                    xb = flat(xt)[:, c * 512:(c + 1) * 512]
                    V.tensor_tensor(xb, xb, B[6 + c][:, :], ALU.subtract).then_inc(inv_done, 1)
            vn, state = DELTA["vn"], DELTA["state"]
            dve.wait_ge(dn_pe, 1)
            V.tensor_copy(flat(vn)[:, 0:512], B[0][:, :]).then_inc(dn_sb, 1)
            dve.wait_ge(dn_pe, 2)
            V.tensor_copy(flat(state), B[2][:, :]).then_inc(dn_sb, 1)
            dve.wait_ge(dn_pe, 3)
            st.done(V.tensor_copy(convt[:, :, 0:P], B[1][:, :].rearrange("p (a t) -> p a t", t=P)))
            dve.wait_ge(dn_pe, 4)
            for hd in range(4):
                ins = V.scalar_tensor_tensor(out=vb[:, 4 + hd, :], in0=B[3][:, hd * P:(hd + 1) * P],
                                             scalar=small[:, 164 + hd:165 + hd], in1=vb[:, 4 + hd, :], op0=ALU.mult,
                                             op1=ALU.add)
            ins.then_inc(dn_sb, 1)
            dve.wait_ge(dn_pe, 5)
            V.tensor_copy(flat(vn)[:, 512:1024], B[4][:, :]).then_inc(dn_sb, 1)
            dve.wait_ge(dn_pe, 6)
            V.tensor_copy(convt[:, :, P:T], B[5][:, :].rearrange("p (a t) -> p a t", t=P)).then_inc(hn_src, 1)
            for g in range(2):
                dve.wait_ge(hn_rs, 30 + g + 1)
                y = flat(mixT[:, 4 + 2 * g:6 + 2 * g, :])
                V.scalar_tensor_tensor(out=y, in0=flat(convt[:, 2 * g:2 * g + 2, :]), scalar=col("dn_g"),
                                       in1=rsh[:, g % 2, :], op0=ALU.mult, op1=ALU.mult).then_inc(hn_done, 1)
                dve.wait_ge(hn_done, 22 + g + 1)
                ins = V.tensor_tensor(y, y, flat(z_gate[:, 2 * g:2 * g + 2, :]), ALU.mult)
            ins.then_inc(mix_ready, 1)
            out_product("mix_out")

            norm_apply("ffn_2", h, KD, "g_ffn_2", hn)
            dve.wait_ge(rt_ready, 1)

            def R(lo, n):
                return route[:, :, lo:lo + n]

            def wide(lo, n):
                return R(lo, 1).to_broadcast([P, 2, n])

            def both(x):
                return x.rearrange("p (a t) -> p a t", a=1).to_broadcast([P, 2, x.shape[1]])

            def first_best(x, n, best, tmp, hot):
                st.link(V.tensor_reduce(R(best, 1), R(x, n), AXX, ALU.max))
                st.link(V.tensor_tensor(R(tmp, n), R(x, n), wide(best, n), ALU.is_equal))
                st.link(V.tensor_tensor(R(tmp, n), R(tmp, n), both(col("first_wins", 0, n)), ALU.mult))
                st.link(V.tensor_reduce(R(best + 1, 1), R(tmp, n), AXX, ALU.max))
                st.link(V.tensor_tensor(R(hot, n), R(tmp, n), wide(best + 1, n), ALU.is_equal))

            dve.wait_ge(turn_h, 1)
            for c in range(2):
                ins = V.tensor_copy(h_tok[:, c, 0:512], OUTB[2 * c][:, :])
            ins.then_inc(h_tok_in, 1)
            st.link(V.tensor_copy(R(0, 36), B[3][:, 0:72].rearrange("p (c n) -> p c n", n=36)))
            first_best(0, 4, 36, 40, 48)
            V.tensor_tensor(R(40, 4), R(0, 4), wide(36, 4), ALU.subtract).then_inc(rt_max, 1)
            st.link(V.tensor_scalar(R(52, 4), R(48, 4), -1.0, -NEG, ALU.add, ALU.mult))
            for c in range(2):
                g3 = [route[:, c, lo:lo + 4].rearrange("p (g a) -> p g a", a=1).to_broadcast([P, NG, EPG])
                      for lo in (48, 52)]
                el = route[:, c, 4:36].rearrange("p (g e) -> p g e", e=EPG)
                ml = route[:, c, 64:96].rearrange("p (g e) -> p g e", e=EPG)
                st.link(V.tensor_tensor(ml, el, g3[0], ALU.mult))
                st.link(V.tensor_tensor(ml, ml, g3[1], ALU.add))
            first_best(64, 32, 192, 96, 128)
            st.link(V.scalar_tensor_tensor(out=R(224, 32), in0=R(128, 32), scalar=2.0 * NEG, in1=R(64, 32),
                                           op0=ALU.mult, op1=ALU.add))
            first_best(224, 32, 194, 96, 160)
            V.tensor_tensor(R(200, 1), R(194, 1), R(192, 1), ALU.subtract).then_inc(rt_max, 1)
            dve.wait_ge(rt_exp, 2)
            st.link(V.tensor_reduce(R(202, 1), R(44, 4), AXX, ALU.add))
            st.link(V.tensor_scalar_add(R(203, 1), R(201, 1), 1.0))
            st.link(V.tensor_tensor(R(202, 1), R(202, 1), R(203, 1), ALU.mult))
            st.link(V.reciprocal(R(204, 1), R(202, 1)))
            st.link(V.tensor_tensor(R(205, 1), R(204, 1), R(201, 1), ALU.mult))
            st.done(V.tensor_tensor(R(320, 32), R(128, 32), R(160, 32), ALU.add))
            st.done(V.tensor_tensor(R(64, 32), R(128, 32), wide(204, 32), ALU.mult))
            st.link(V.tensor_tensor(R(96, 32), R(160, 32), wide(205, 32), ALU.mult))
            V.tensor_tensor(R(288, 32), R(64, 32), R(96, 32), ALU.add).then_inc(rt_gate, 1)
            dve.wait_ge(counted, 1)
            st.link(V.tensor_reduce(small[:, 0:1], B[3][:, 2 * NE:3 * NE], AXX, ALU.max))
            V.tensor_copy(peak[:], small[:, 0:1]).then_inc(peak_in, 1)
            dve.wait_ge(rt_gate, 1)
            st.settled()
            st.link(V.tensor_tensor(R(0, 32), B[3][:, 0:2 * NE].rearrange("p (c e) -> p c e", e=NE), R(320, 32), ALU.mult))
            st.link(V.tensor_scalar(R(0, 32), R(0, 32), -1.0, CAP + 1.0, ALU.mult, ALU.add))

            def moe_gathered():
                def of_expert(lo, c):
                    return route[:, c, lo:lo + NE].rearrange("p (e a) -> p e a", a=1).to_broadcast([P, NE, CAP])

                for c in range(2):
                    s3_, g3_ = (x[:, c, :].rearrange("p (e s) -> p e s", s=CAP) for x in (slots, gated_slots))
                    st.link(V.tensor_tensor(s3_, rep(col("first_wins", 0, CAP), NE), of_expert(0, c), ALU.is_equal))
                    ins = V.tensor_tensor(g3_, s3_, of_expert(288, c), ALU.mult)
                ins.then_inc(slots_in, 1)
                per = EXPERT_TILES // CT * QUAD

                def gathered_half(r):
                    dve.wait_ge(gather_sum, r + 1)
                    V.tensor_copy(gathered[:, 0:4, :].rearrange("p k s -> p (k s)"), B[6][:, :]).then_inc(gather_dve, 1)

                def quad(r, first=False, last=False):
                    for e in range(QUAD):
                        dve.wait_ge(ex_gu, r * QUAD + (e + 1))
                        V.tensor_copy(partial[:, 1, :], B[1][:, :]).then_inc(part_in[1], 1)
                        x, sg, a = expg[:, 0, 0:P], gate_r[:, 0, 0:P], act[:, 0, 0:P]
                        sg3, a3 = (t.rearrange("p (m s) -> p m s", s=CAP) for t in (sg, a))
                        dve.wait_ge(ex_exp, r * QUAD + (e + 1))
                        V.tensor_scalar_add(x, x, 1.0).then_inc(ex_step, 1)
                        dve.wait_ge(ex_step, r * (3 * QUAD) + (3 * e + 1))
                        V.reciprocal(sg, x).then_inc(ex_step, 1)
                        dve.wait_ge(ex_step, r * (3 * QUAD) + (3 * e + 2))
                        V.tensor_tensor(sg3, turned_part(0), sg3, ALU.mult).then_inc(ex_step, 1)
                        dve.wait_ge(ex_step, r * (3 * QUAD) + (3 * e + 3))
                        V.tensor_tensor(a3, turned_part(1), sg3, ALU.mult).then_inc(ex_act, 1)
                        if not first and e < 2:
                            dve.wait_ge(ex_scatter, r * 2 + (e - 1))
                            for i in range(2):
                                add_residual(B[6 + i], 2 * e + i, 1.0, ex_added if i == 1 else None)
                    if not last:
                        gathered_half(r + 1)
                    dve.wait_ge(ring_free, r * per + (PLAN["moe"] + per))
                    V.tensor_copy(y_slots[:, 0:512], B[4][:, :]).then_inc(y_dve, 1)

                gathered_half(0)
                dve.wait_ge(slots_turned, 1)
                for n in range(4):
                    ins = V.tensor_copy(slots_T[:, n * 512:(n + 1) * 512], B[2 + n][:, :])
                ins.then_inc(slots_T_in, 1)
                last = NE // QUAD - 1
                quad(0, first=True)
                with dve.Fori(1, last) as r:
                    quad(r)
                quad(last, last=True)
                for half in range(2):
                    dve.wait_ge(ex_scatter, 2 * last + half + 1)
                    for i in range(2):
                        add_residual(B[(6, 4)[half] + i], 2 * half + i, 1.0, h_ready)

            def moe_dense():
                for i in range(NE // 2):
                    dve.wait_ge(rt_rows, i + 1)
                    V.tensor_copy(gate_rows[:, i * 512:(i + 1) * 512], B[4 + i % 2][:, :]).then_inc(rt_free, 1)
                dve.wait_ge(rt_free, NE // 2)
                with dve.Fori(0, NE) as r:
                    for j in range(EC):
                        i = GU["moe"] + j
                        silu_times_up(j % 2, r * EC + (i + 1), 5 * GU["moe"] + 4 * j, r * (4 * EC),
                                      gate_rows[:, bass.ds(r * T, T)])
                dve.wait_ge(acc_ready, len(FFNS) + 1)
                for i in range(4):
                    add_residual(OUTB[i], i, 1.0, h_ready)

            most = dve.value_load(peak[0:1, 0:1])
            with dve.If(most < CAP + 1):
                moe_gathered()
            with dve.Else():
                moe_dense()
            norm_apply("final", h, KD, "g_final", hn)


def _tiles(w):
    k, m = w.shape
    return w.reshape(k // P, P, m // P, P).transpose(2, 0, 1, 3).reshape(-1, P, P)


def _chunks(tiles):
    n = len(tiles)
    c = chunks_of(n)
    if c * CT > n:
        tiles = np.concatenate([tiles, np.zeros((c * CT - n, P, P), tiles.dtype)])
    return np.ascontiguousarray(tiles.reshape(c, CT, P, P).transpose(0, 2, 1, 3)).reshape(c, P, CT * P)


def _widen(w, width):
    k = w.shape[0]
    w = w.reshape(k, -1, width)
    return np.concatenate([w, np.zeros((k, w.shape[1], P - width), w.dtype)], axis=2).reshape(k, -1)


def _gated(w_gate, w_up, w_down, n):
    gate, up = _tiles(w_gate).reshape(n, KD, P, P), _tiles(w_up).reshape(n, KD, P, P)
    down = w_down.reshape(n, P, KD, P).transpose(0, 2, 1, 3)
    none = np.zeros((1, KD, P, P), gate.dtype)
    parts = [np.concatenate([gate, none]), np.concatenate([up, none]), np.concatenate([none, down])]
    return _chunks(np.concatenate(parts, axis=1).reshape(-1, P, P))


def _wide(w):
    k = w.shape[0]
    return w.reshape(k // P, P, 2, 4, P).transpose(2, 0, 3, 1, 4).reshape(-1, P, P)


def kernel(**inputs):
    import concourse.bacc as bacc
    from concourse.bass_utils import run_bass_kernel_spmd

    a = {k: np.asarray(v) for k, v in inputs.items()}

    def ffn(which, layer):
        w = a[f"{which}_w_in"][layer]
        return _gated(w[:, :FF], w[:, FF:], a[f"{which}_w_out"][layer], FFC)

    def ple(layer):
        gate = _tiles(a["ple_w_gate"][layer]).reshape(KD, KD, P, P)
        proj = _tiles(a["ple_w_proj"][layer]).reshape(KD, 2, P, P)
        return _chunks(np.concatenate([gate, proj], axis=1).reshape(-1, P, P))

    w = a["mla_w_in"][0]
    k_pe = np.concatenate([np.zeros((D, NOPE), w.dtype), w[:, QR + KVR:], np.zeros((D, P - QK), w.dtype)], axis=1)
    mla_in = _chunks(_tiles(np.concatenate([w[:, :QR + KVR], k_pe], axis=1)))
    mla_q = _chunks(_tiles(_widen(a["mla_w_uq"][0], QK)))
    ukv = a["mla_w_ukv"][0].reshape(KVR, H, NOPE + DV)
    mla_kv = _chunks(np.concatenate([_tiles(ukv[:, :, :NOPE].reshape(KVR, -1)), _wide(ukv[:, :, NOPE:].reshape(KVR, -1))]))
    fox = a["fox_w_in"][0]
    w2 = a["w_in_2"][0]
    order = [0, 2, 1, 3, 4, 5, 6]
    mix_in = np.concatenate([w2[:, 512 * i:512 * (i + 1)] for i in order], axis=1)
    def rows_of(w):
        e, k, m = w.shape
        return w.reshape(e, k // P, P, m // P, P).transpose(0, 1, 3, 2, 4)

    gate_up = np.concatenate([rows_of(a["w_gate_2"][0]), rows_of(a["w_up_2"][0])], axis=2).reshape(NE, -1, P, P)
    moe = _chunks(np.concatenate([gate_up, rows_of(a["w_down_2"][0]).reshape(NE, -1, P, P)], axis=1).reshape(-1, P, P))
    weights = np.concatenate([
        ffn("ffn1", 0), mla_in, mla_q, mla_kv, _chunks(_tiles(a["mla_w_o"][0])), ffn("ffn2", 0), ple(0),
        ffn("ffn1", 1), _chunks(_tiles(fox[:, :2048])), _chunks(_wide(fox[:, 2048:3072])),
        _chunks(_tiles(a["fox_w_o"][0])), ffn("ffn2", 1), ple(1),
        _chunks(_tiles(mix_in)), _chunks(_tiles(a["w_out_2"][0])), moe])
    assert weights.shape[0] == N_CHUNKS

    def cols(v):
        return v.reshape(-1, P).T

    def fill(v):
        return np.concatenate([v, np.zeros(P - len(v), v.dtype)])[:, None]

    def rows(v):
        return np.broadcast_to(v[None, :], (P, len(v)))

    def packed(v):
        return v.reshape(KD, P, -1).transpose(1, 0, 2).reshape(P, -1)

    f32 = np.float32
    half = ROPE // 2
    inv = (f32(10000.0) ** (-np.arange(0, ROPE, 2, dtype=f32) / f32(ROPE))).astype(f32)
    values = {
        "g_q_lat": cols(a["mla_g_q_lat"][0]), "g_kv_lat": cols(a["mla_g_kv_lat"][0]),
        "mla_qn": fill(a["mla_g_qn"][0]), "mla_kn": fill(a["mla_g_kn"][0]),
        "fox_qn": np.concatenate([a["fox_g_qn"][0]] * 2)[:, None],
        "fox_kn": np.concatenate([a["fox_g_kn"][0]] * 2)[:, None],
        "g_mix2": cols(a["mix_norm_g_2"][0]),
        "conv_a_w": np.concatenate([cols(a["conv_a_w_2"][0, j]) for j in range(3)], axis=1),
        "conv_a_g": cols(a["conv_a_norm_g_2"][0]),
        "dn_conv_w": np.concatenate([cols(a["dn_conv_w_2"][0, j]) for j in range(4)], axis=1),
        "dn_g": a["dn_norm_g_2"][0][:, None], "g_ffn_2": cols(a["ffn_norm_g_2"][0]),
        "g_final": cols(a["final_norm_g_2"]),
        "inv_freq": np.tile(inv, P // half)[:, None],
        "rope_sign": np.tile(np.repeat(np.array([-1.0, 1.0], f32), half), P // ROPE)[:, None],
        "b_f": rows(a["fox_b_f"][0]), "a_log": rows(a["dn_a_log_2"][0]), "dt_bias": rows(a["dn_dt_bias_2"][0]),
        "w_f": packed(fox[:, 3072:]), "w_ba": packed(w2[:, 3584:]),
        "w_router": packed(np.concatenate([a["router_group_w_2"][0], a["router_expert_w_2"][0]], axis=1)),
        "first_wins": np.broadcast_to(np.arange(32, 0, -1, dtype=f32)[None, :], (P, 32)),
    }
    for layer in range(DEPTH):
        for g in ("ffn1", "mix", "ffn2", "ple"):
            values[f"g_{g}_{layer}"] = cols(a[f"g_{g}"][layer])
    par = np.ascontiguousarray(np.concatenate([values[n] for n, _ in PARAMS], axis=1).astype(f32))

    def feature_major(x):
        return np.ascontiguousarray(x.T.reshape(-1, P, T).transpose(1, 0, 2))

    arrays = {
        "xT": feature_major(a["x"][0]),
        "pT": np.ascontiguousarray(np.concatenate([feature_major(a["p"][i, 0]) for i in range(DEPTH)], axis=1)),
        "pos": np.ascontiguousarray(np.broadcast_to(a["positions"], (P, T))),
        "par": par, "weights": weights,
    }
    nc = bacc.Bacc("TRN2", target_bir_lowering=False, num_devices=1)
    aps = [nc.dram_tensor(n, v.shape, mybir.dt.from_np(v.dtype), kind="ExternalInput").ap() for n, v in arrays.items()]
    out = nc.dram_tensor("outT", (P, KD, T), F32, kind="ExternalOutput").ap()
    two_block_kernel(nc, *aps, out)
    r = run_bass_kernel_spmd(nc, [arrays], core_ids=[0])
    y = np.asarray(r.results[0]["outT"])
    return np.ascontiguousarray(y.transpose(1, 0, 2).reshape(D, T).T)[None]
```
